# Optimizing a Trainium2 kernel written in Bass

```python
import jax, jax.numpy as jnp
from jax import lax
import numpy as np

D_MODEL = 1024
BATCH = 1
SEQ = 2048
DEPTH = 1

MIX_WIDTH = D_MODEL
GLA_HEADS = 4
GLA_DV = (MIX_WIDTH // 2) // GLA_HEADS
GLA_DK = GLA_DV // 2
GLA_GATE_RANK = 16
GLA_GATE_NORM = 16.0
GLA_CHUNK = 16
RET_HEADS = 4
RET_DK = (MIX_WIDTH // 2) // RET_HEADS
RET_DV = RET_DK
RET_CHUNK = 128
ROPE_BASE = 10000.0
N_EXPERTS = 32
TOP_K = 4
D_EXPERT = D_MODEL
SWIGLU_LIMIT = 7.0
SWIGLU_ALPHA = 1.702
EPS = 1e-6

GLA_QK = GLA_HEADS * GLA_DK
GLA_VW = GLA_HEADS * GLA_DV
RET_QK = RET_HEADS * RET_DK
RET_VW = RET_HEADS * RET_DV
MIX_IN = 2 * GLA_QK + 2 * GLA_VW + GLA_GATE_RANK + 2 * RET_QK + 2 * RET_VW

kernel_name = 'hymba_gla_retnet_moe_adaln'

def rmsnorm(x, w):
    xf = x.astype(jnp.float32)
    y = xf * lax.rsqrt(jnp.mean(xf * xf, axis=-1, keepdims=True) + EPS)
    return (y * w.astype(jnp.float32)).astype(x.dtype)

def layernorm_nobias(x, w):
    xf = x.astype(jnp.float32)
    mu = jnp.mean(xf, axis=-1, keepdims=True)
    var = jnp.mean(jnp.square(xf - mu), axis=-1, keepdims=True)
    return ((xf - mu) * lax.rsqrt(var + EPS) * w.astype(jnp.float32))

def rotary(x, positions):
    half = x.shape[-1] // 2
    inv = ROPE_BASE ** (-jnp.arange(half, dtype=jnp.float32) / half)
    ang = positions.astype(jnp.float32)[..., None] * inv
    cos = jnp.cos(ang)[:, :, None, :]
    sin = jnp.sin(ang)[:, :, None, :]
    x1, x2 = x[..., :half].astype(jnp.float32), x[..., half:].astype(jnp.float32)
    return jnp.concatenate([x1 * cos - x2 * sin, x1 * sin + x2 * cos], axis=-1).astype(x.dtype)

def chunk_state_scan(decay, U):
    def step(S, inp):
        d, u = inp
        return d * S + u, S
    _, prev = lax.scan(step, jnp.zeros_like(U[0]), (decay, U))
    return prev

def gla_chunked(q, k, v, log_a):
    B, S, H, dk = q.shape
    dv = v.shape[-1]
    C = GLA_CHUNK
    N = S // C
    q = q.reshape(B, N, C, H, dk)
    k = k.reshape(B, N, C, H, dk)
    v = v.reshape(B, N, C, H, dv)
    b = jnp.cumsum(log_a.astype(jnp.float32).reshape(B, N, C, H, dk), axis=2)
    causal = jnp.tril(jnp.ones((C, C), dtype=bool))[:, :, None, None]
    diff = b[:, :, :, None] - b[:, :, None, :]
    decay = jnp.exp(jnp.where(causal, diff, -jnp.inf))
    A = jnp.einsum('bntshd,bnshd->bnhts', decay * q[:, :, :, None], k)
    o_intra = jnp.einsum('bnhts,bnshv->bnthv', A, v)
    b_last = b[:, :, -1]
    k_up = k * jnp.exp(b_last[:, :, None] - b)
    U = jnp.einsum('bnshd,bnshv->nbhdv', k_up, v).astype(jnp.float32)
    chunk_decay = jnp.exp(b_last).transpose(1, 0, 2, 3)[..., None]
    S_prev = chunk_state_scan(chunk_decay, U)
    o_inter = jnp.einsum('bnthd,nbhdv->bnthv', q * jnp.exp(b), S_prev)
    return (o_intra + o_inter).reshape(B, S, H, dv)

def retention_chunked(q, k, v, log_gamma):
    B, S, H, dk = q.shape
    dv = v.shape[-1]
    C = RET_CHUNK
    N = S // C
    q = q.reshape(B, N, C, H, dk)
    k = k.reshape(B, N, C, H, dk)
    v = v.reshape(B, N, C, H, dv)
    idx = jnp.arange(C, dtype=jnp.float32)
    rel = idx[:, None] - idx[None, :]
    Dmask = jnp.where((rel >= 0)[None], jnp.exp(rel[None] * log_gamma[:, None, None]), 0.0)
    scores = jnp.einsum('bnthd,bnshd->bnhts', q, k) * Dmask
    o_intra = jnp.einsum('bnhts,bnshv->bnthv', scores, v)
    xi = jnp.exp((idx + 1.0)[:, None] * log_gamma[None, :])
    zeta = jnp.exp((C - 1.0 - idx)[:, None] * log_gamma[None, :])
    U = jnp.einsum('bnshd,bnshv->nbhdv', k * zeta[None, None, :, :, None], v).astype(jnp.float32)
    chunk_decay = jnp.broadcast_to(jnp.exp(C * log_gamma)[None, None, :, None, None], (N, 1, H, 1, 1))
    R_prev = chunk_state_scan(chunk_decay, U)
    o_inter = jnp.einsum('bnthd,nbhdv->bnthv', q * xi[None, None, :, :, None], R_prev)
    return (o_intra + o_inter).reshape(B, S, H, dv)

def hybrid_mixer(h, positions, w_in, w_gk2, b_gk, gla_onorm, ret_onorm, w_out):
    B, S, _ = h.shape
    sizes = [GLA_QK, GLA_QK, GLA_VW, GLA_VW, GLA_GATE_RANK, RET_QK, RET_QK, RET_VW, RET_VW]
    cuts = np.cumsum(sizes)[:-1].tolist()
    proj = h @ w_in
    gq, gk, gv, gg, glr, rq, rk, rv, rg = jnp.split(proj, cuts, axis=-1)
    gq = gq.reshape(B, S, GLA_HEADS, GLA_DK) * (GLA_DK ** -0.5)
    gk = gk.reshape(B, S, GLA_HEADS, GLA_DK)
    gv = gv.reshape(B, S, GLA_HEADS, GLA_DV)
    log_a = jax.nn.log_sigmoid((glr @ w_gk2 + b_gk).astype(jnp.float32)) / GLA_GATE_NORM
    log_a = log_a.reshape(B, S, GLA_HEADS, GLA_DK)
    o_gla = gla_chunked(gq, gk, gv, log_a)
    o_gla = rmsnorm(o_gla.astype(jnp.float32), gla_onorm) * jax.nn.silu(gg.reshape(B, S, GLA_HEADS, GLA_DV).astype(jnp.float32))
    log_gamma = jnp.log(1.0 - jnp.exp2(-5.0 - jnp.arange(RET_HEADS, dtype=jnp.float32)))
    rq = rotary(rq.reshape(B, S, RET_HEADS, RET_DK), positions)
    rk = rotary(rk.reshape(B, S, RET_HEADS, RET_DK), positions) * (RET_DK ** -0.5)
    rv = rv.reshape(B, S, RET_HEADS, RET_DV)
    o_ret = retention_chunked(rq, rk, rv, log_gamma)
    o_ret = layernorm_nobias(o_ret, ret_onorm) * jax.nn.silu(rg.reshape(B, S, RET_HEADS, RET_DV).astype(jnp.float32))
    o = jnp.concatenate([o_gla.reshape(B, S, GLA_VW), o_ret.reshape(B, S, RET_VW)], axis=-1).astype(h.dtype)
    return o @ w_out

def moe_ffn(h, w_router, b_router, w_gu, b_gu, w_down, b_down):
    B, S, D = h.shape
    T = B * S
    hf = h.reshape(T, D)
    logits = (hf @ w_router + b_router).astype(jnp.float32)
    top_val, top_idx = lax.top_k(logits, TOP_K)
    weights = jax.nn.softmax(top_val, axis=-1).astype(h.dtype)
    flat_e = top_idx.reshape(-1)
    order = jnp.argsort(flat_e)
    sorted_e = flat_e[order]
    tok = order // TOP_K
    group_sizes = jnp.bincount(flat_e, length=N_EXPERTS).astype(jnp.int32)
    xs = hf[tok]
    gu = lax.ragged_dot(xs, w_gu, group_sizes) + b_gu[sorted_e]
    gate, up = jnp.split(gu, 2, axis=-1)
    gate = jnp.minimum(gate, SWIGLU_LIMIT)
    up = jnp.clip(up, -SWIGLU_LIMIT, SWIGLU_LIMIT)
    act = (up + 1.0) * (gate * jax.nn.sigmoid(SWIGLU_ALPHA * gate))
    out = lax.ragged_dot(act.astype(h.dtype), w_down, group_sizes) + b_down[sorted_e]
    out = out * weights.reshape(-1)[order][:, None]
    y = jnp.zeros((T, D), dtype=out.dtype).at[tok].add(out)
    return y.reshape(B, S, D).astype(h.dtype)

def setup_inputs(seed: int = 0) -> dict:
    key = jax.random.key(seed)
    ks = jax.random.split(key, 24)
    f32 = jnp.float32
    L, D, E, F = DEPTH, D_MODEL, N_EXPERTS, D_EXPERT
    nrm = lambda k, shape, fan: jax.random.normal(k, shape, f32) * (fan ** -0.5)
    x = jax.random.normal(ks[0], (BATCH, SEQ, D), f32)
    c = jax.random.normal(ks[1], (BATCH, D), f32)
    positions = (jnp.arange(SEQ, dtype=jnp.int32)[None, :]
                 + jax.random.randint(ks[2], (BATCH, 1), 0, 1024, dtype=jnp.int32))
    return {
        'x': x,
        'c': c,
        'positions': positions,
        'w_ada': nrm(ks[3], (L, D, 6 * D), D),
        'b_ada': 0.02 * jax.random.normal(ks[4], (L, 6 * D), f32),
        'norm1': 1.0 + 0.05 * jax.random.normal(ks[5], (L, D), f32),
        'w_in': nrm(ks[6], (L, D, MIX_IN), D),
        'w_gk2': nrm(ks[7], (L, GLA_GATE_RANK, GLA_QK), GLA_GATE_RANK),
        'b_gk': 0.1 * jax.random.normal(ks[8], (L, GLA_QK), f32),
        'gla_onorm': 1.0 + 0.05 * jax.random.normal(ks[9], (L, GLA_DV), f32),
        'ret_onorm': 1.0 + 0.05 * jax.random.normal(ks[10], (L, RET_DV), f32),
        'w_out': nrm(ks[11], (L, MIX_WIDTH, D), MIX_WIDTH),
        'norm2': 1.0 + 0.05 * jax.random.normal(ks[12], (L, D), f32),
        'w_router': nrm(ks[13], (L, D, E), D),
        'b_router': 0.01 * jax.random.normal(ks[14], (L, E), f32),
        'w_gu': nrm(ks[15], (L, E, D, 2 * F), D),
        'b_gu': 0.02 * jax.random.normal(ks[16], (L, E, 2 * F), f32),
        'w_down': nrm(ks[17], (L, E, F, D), F),
        'b_down': 0.02 * jax.random.normal(ks[18], (L, E, D), f32),
        'norm_f': 1.0 + 0.05 * jax.random.normal(ks[19], (D,), f32),
    }

def reference(x, c, positions, w_ada, b_ada, norm1, w_in, w_gk2, b_gk, gla_onorm, ret_onorm,
              w_out, norm2, w_router, b_router, w_gu, b_gu, w_down, b_down, norm_f):
    for l in range(DEPTH):
        mod = jax.nn.silu(c) @ w_ada[l] + b_ada[l]
        sh1, sc1, g1, sh2, sc2, g2 = jnp.split(mod[:, None, :], 6, axis=-1)
        h = rmsnorm(x, norm1[l]) * (1.0 + sc1) + sh1
        x = x + g1 * hybrid_mixer(h, positions, w_in[l], w_gk2[l], b_gk[l],
                                  gla_onorm[l], ret_onorm[l], w_out[l])
        h = rmsnorm(x, norm2[l]) * (1.0 + sc2) + sh2
        x = x + g2 * moe_ffn(h, w_router[l], b_router[l], w_gu[l], b_gu[l], w_down[l], b_down[l])
    return rmsnorm(x, norm_f)


_drawn_inputs = setup_inputs


def setup_inputs(seed=0):
    import zlib

    import numpy as np

    out = dict(_drawn_inputs(seed))
    spreads = {}
    factors = {'b_router': 2.673, 'b_gu': 6.905, 'b_down': 8.0}
    for name, (base, spread) in spreads.items():
        noise = np.random.default_rng([zlib.crc32(name.encode()), seed]).standard_normal(out[name].shape)
        drawn = base * np.exp(spread * noise) if base else spread * noise
        out[name] = __import__('jax').numpy.asarray(drawn.astype(out[name].dtype))
    for name, factor in factors.items():
        out[name] = (out[name] * factor).astype(out[name].dtype)
    return out
```

```python
from contextlib import ExitStack

import numpy as np
import concourse.bass as bass
from concourse import mybir

P = 128
F32 = mybir.dt.float32
F32R = mybir.dt.float32r
I32 = mybir.dt.int32
ALU = mybir.AluOpType
ACT = mybir.ActivationFunctionType
AX_X = mybir.AxisListType.X

D = 1024
S = 2048
NT = S // P
KD = D // P
N = 512
EPS = 1e-6

GH, GDK, GDV, RANK = 4, 64, 128, 16
RH, RDK = 4, 128
GATE_NORM = 16.0
SUB = 32
ROPE_BASE = 10000.0
PROJ = 3584
NC_IN = PROJ // N
GLR = 1536
C_GQ, C_GK, C_GV, C_GG = 0, 256, 512, 1024
C_RQ, C_RK, C_RV, C_RG = 1536, 2048, 2560, 3072

E = 32
TOPK = 4
GT = 4
ROWS = S + P
PLACES = E * NT
NG = (S * TOPK - E) // (GT * P) + E
LIMIT = 7.0
SIG = 1.702



def w_in_column(chunk):
    return chunk * N + (RANK if chunk * N >= GLR else 0)


class Kit:

    def __init__(self, nc, ctx, phase):
        self.nc, self.ctx, self.phase, self.signals = nc, ctx, phase, []

    def sb(self, name, shape, dt=F32):
        return self.ctx.enter_context(self.nc.sbuf_tensor(f"{self.phase}_{name}", shape, dt))

    def ps(self, name, shape):
        return self.ctx.enter_context(self.nc.psum_tensor(f"{self.phase}_bank_{name}", shape, F32))

    def sem(self, name):
        self.signals.append(self.nc.alloc_semaphore(f"{self.phase}_{name}"))
        return self.signals[-1]

    def sems(self, names):
        return [self.sem(n) for n in names.split()]

    def clear_sems(self):
        self.nc.clear_and_free_semaphores(self.signals)
        self.nc.all_engine_barrier()


class Steps:

    def __init__(self, eng, sem, per_turn=0):
        self.eng, self.sem, self.per_turn, self.base, self.n = eng, sem, per_turn, 0, 0

    def turn(self, i):
        self.base, self.n = i * self.per_turn, 0

    def __call__(self, ins):
        ins.then_inc(self.sem, 1)
        self.n += 1
        self.eng.wait_ge(self.sem, self.base + self.n)

    def check(self):
        assert self.n == self.per_turn, (self.n, self.per_turn)


def split_product(nc, out, act_hi, act_lo, w_hi, w_lo, first, last):
    nc.tensor.matmul(out, act_hi, w_hi, start=first, stop=False)
    nc.tensor.matmul(out, act_hi, w_lo, start=False, stop=False)
    return nc.tensor.matmul(out, act_lo, w_hi, start=False, stop=last)


def row(ap, n=P):
    return ap.rearrange("o n -> (o n)").partition_broadcast(n)


def constants():
    p = np.arange(P, dtype=np.float64)
    s, t = p[:, None], p[None, :]
    parts = {}
    parts["ident"] = (s == t).astype(np.float64)
    parts["ones"] = np.ones((P, P))
    parts["before"] = (s < t).astype(np.float64)
    parts["causal"] = (s <= t).astype(np.float64)
    parts["sum_to"] = (s <= t) / GATE_NORM
    parts["sum_after"] = (s > t) / GATE_NORM
    log_gamma = np.log(1.0 - 2.0 ** (-5.0 - np.arange(RH)))
    rel = (t - s)[:, None, :] * log_gamma[None, :, None]
    parts["decay"] = (np.where((t >= s)[:, None, :], np.exp(np.minimum(rel, 0.0)), 0.0) * RDK ** -0.5).reshape(P, -1)
    parts["xi"] = np.broadcast_to(np.exp((p + 1)[None, None, :] * log_gamma[None, :, None]), (P, RH, P)).reshape(P, -1)
    parts["zeta"] = np.exp((P - 1 - p)[:, None] * log_gamma[None, :]) * RDK ** -0.5
    half = RDK // 2
    inv = (np.float32(ROPE_BASE) ** (-np.arange(half, dtype=np.float32) / np.float32(half))).astype(np.float32)
    parts["inv_freq"] = np.broadcast_to(inv, (P, half))
    parts["expert"] = np.broadcast_to(np.arange(E), (P, E))
    parts["expert_row"] = np.broadcast_to(np.arange(E) * NT, (P, E))
    parts["tile_from"] = np.broadcast_to(np.arange(NT) * P, (P, NT))
    parts["number"] = p[:, None]
    parts["eps"] = np.full((P, 1), EPS)
    parts["token"] = p[:, None] + P * np.arange(NT)[None, :]
    at, n = {}, 0
    for name, a in parts.items():
        at[name] = (n, a.shape[1])
        n += a.shape[1]
    return np.concatenate([np.asarray(a, np.float32) for a in parts.values()], axis=1), at


CONST_AT = constants()[1]
GAMMA_TILE = [float(np.exp(P * np.log(1.0 - 2.0 ** (-5.0 - h)))) for h in range(RH)]


def phase_modulation(nc, k, A, keep):
    W_SLOTS = 3
    n_chunk = 6 * D // N
    c_col, neg, den, silu = (k.sb(n, [P, KD]) for n in ("c_col", "exp_neg_c", "den", "silu"))
    silu_rep = k.sb("silu_rep", [P, KD, P])
    w = k.sb("w_ada", [P, W_SLOTS, KD, N])
    b = k.sb("b_ada", [P, 6 * D])
    mod = k.sb("mod", [P, 6 * D])
    norms = k.sb("norms", [P, 2, D])
    zero = k.sb("zero", [P, D])
    acc = k.ps("acc", [P, 2, N])
    c_in, b_in, mod_out, const_in, exp_done, dve_step = k.sems("c_in b_in mod_out const_in exp_done dve_step")
    silu_ready, acc_full, acc_read, mod_ready = k.sems("silu_ready acc_full acc_read mod_ready")
    zero_set, zero_out = k.sems("zero_set zero_out")
    w_in = [k.sem(f"w_in{s}") for s in range(W_SLOTS)]
    w_dram = A["w_ada"].rearrange("o (s p) n -> p (o s) n", p=P)
    ones = keep["const"]("ones")
    with nc.Block() as block:

        @block.sync
        def _(sp):
            sp.dma_start(c_col[:], A["c"].rearrange("o (s p) -> p (o s)", p=P),
                         allow_slow_non_contiguous=True).then_inc(c_in, 16)
            sp.dma_start(keep["const_all"][:], A["const"]).then_inc(const_in, 16)
            for n in range(n_chunk):
                if n >= W_SLOTS:
                    sp.wait_ge(acc_full, n - W_SLOTS + 1)
                sp.dma_start(w[:, n % W_SLOTS], w_dram[:, :, n * N:(n + 1) * N]).then_inc(w_in[n % W_SLOTS], 16)
            sp.wait_ge(mod_ready, 1)
            for j, name in ((2, "g1"), (3, "sh2"), (4, "A2"), (5, "g2")):
                sp.dma_start(keep[name], mod[:, j * D:(j + 1) * D]).then_inc(mod_out, 16)
            sp.wait_ge(mod_out, 64)

        @block.scalar
        def _(act):
            act.dma_start(b[:], row(A["b_ada"])).then_inc(b_in, 16)
            act.dma_start(norms[:, 0], row(A["norm1"])).then_inc(b_in, 16)
            act.dma_start(norms[:, 1], row(A["norm2"])).then_inc(b_in, 16)
            act.wait_ge(c_in, 16)
            nc.scalar.activation(neg[:], c_col[:], ACT.Exp, scale=-1.0).then_inc(exp_done, 1)

        @block.gpsimd
        def _(pool):
            nc.gpsimd.memset(keep["glr_t"][:], 1.0).then_inc(zero_set, 1)
            nc.gpsimd.memset(zero[:], 0.0).then_inc(zero_set, 1)
            pool.wait_ge(zero_set, 2)
            pool.dma_start(keep["h2"][S:ROWS, :], zero[:]).then_inc(zero_out, 16)
            for half in range(2):
                pool.dma_start(keep["y"][half][S:ROWS, :], zero[:, 0:N]).then_inc(zero_out, 16)
            pool.wait_ge(zero_out, 48)

        @block.vector
        def _(dve):
            step = Steps(dve, dve_step)
            dve.wait_ge(exp_done, 1)
            step(nc.vector.tensor_scalar(den[:], neg[:], 1.0, None, ALU.add))
            step(nc.vector.reciprocal(neg[:], den[:]))
            step(nc.vector.tensor_tensor(silu[:], c_col[:], neg[:], ALU.mult))
            dve.wait_ge(const_in, 16)
            for s in range(KD):
                nc.vector.tensor_scalar(silu_rep[:, s], ones, silu[:, s:s + 1], None, ALU.mult).then_inc(silu_ready, 1)
            dve.wait_ge(b_in, 48)
            for n in range(n_chunk):
                dve.wait_ge(acc_full, n + 1)
                nc.vector.tensor_tensor(mod[:, n * N:(n + 1) * N], acc[:, n % 2], b[:, n * N:(n + 1) * N],
                                        ALU.add).then_inc(acc_read, 1)
            dve.wait_ge(acc_read, n_chunk)
            step(nc.vector.tensor_copy(keep["sh1"][:], mod[:, 0:D]))
            step(nc.vector.scalar_tensor_tensor(out=keep["A1"][:], in0=mod[:, D:2 * D], scalar=1.0, in1=norms[:, 0],
                                                op0=ALU.add, op1=ALU.mult))
            nc.vector.scalar_tensor_tensor(out=mod[:, 4 * D:5 * D], in0=mod[:, 4 * D:5 * D], scalar=1.0,
                                           in1=norms[:, 1], op0=ALU.add, op1=ALU.mult).then_inc(mod_ready, 1)

        @block.tensor
        def _(pe):
            pe.wait_ge(silu_ready, KD)
            for n in range(n_chunk):
                pe.wait_ge(w_in[n % W_SLOTS], 16 * (n // W_SLOTS + 1))
                if n >= 2:
                    pe.wait_ge(acc_read, n - 1)
                for s in range(KD):
                    mm = nc.tensor.matmul(acc[:, n % 2], silu_rep[:, s], w[:, n % W_SLOTS, s],
                                          start=(s == 0), stop=(s == KD - 1))
                mm.then_inc(acc_full, 1)


def phase_projection(nc, k, A, keep):
    HT = NT // 2
    raw = k.sb("w_raw", [P, 2, KD, N])
    whi, wlo = (k.sb(n, [P, 2, KD, N], F32R) for n in ("w_hi", "w_lo"))
    rraw = k.sb("rank_raw", [P, KD, RANK])
    rhi, rlo = (k.sb(n, [P, KD, P], F32R) for n in ("rank_hi", "rank_lo"))
    hhi, hlo = (k.sb(n, [P, KD, HT, P], F32R) for n in ("h_hi", "h_lo"))
    x = k.sb("x", [P, 2, D])
    squares = k.sb("squares", [P, D], mybir.dt.bfloat16)
    ssq, rs, rinv = (k.sb(n, [P, 2]) for n in ("ssq", "rms", "rinv"))
    sum_done, wait_carrier = k.sems("sum_done wait_carrier")
    stage = k.sb("stage", [P, 2, N])
    tp = k.ps("tp", [P, 2, KD, P])
    acc = k.ps("acc", [P, 2, N])
    racc = k.ps("racc", [P, N])
    sq_done, dve_step, h_ready, t_done, hi_done, lo_done = k.sems(
        "sq_done dve_step h_ready t_done hi_done lo_done")
    whi_done, wlo_done, mm_done, acc_read, r_done, r_read, rank_in, rank_set, rhi_done, rlo_done = k.sems(
        "whi_done wlo_done mm_done acc_read r_done r_read rank_in rank_set rhi_done rlo_done")
    x_in = [k.sem(f"x_in{s}") for s in range(2)]
    raw_in = [k.sem(f"raw_in{s}") for s in range(2)]
    out_done = [k.sem(f"out_done{s}") for s in range(2)]
    USES = [(NC_IN + 1) // 2, NC_IN // 2]
    x_t = A["x"].rearrange("o (t p) d -> p (o t) d", p=P)
    w_t = A["w_in"].rearrange("o (s p) n -> p (o s) n", p=P)
    proj_t = keep["proj"].rearrange("(t p) n -> p t n", p=P)

    with nc.Block() as block:

        @block.gpsimd
        def _(pool):
            nc.gpsimd.memset(rhi[:].bitcast(F32), 0.0).then_inc(rank_set, 1)
            nc.gpsimd.memset(rlo[:].bitcast(F32), 0.0).then_inc(rank_set, 1)
            pool.dma_start(rraw[:], w_t[:, :, GLR:GLR + RANK]).then_inc(rank_in, 16)
            pool.sem_inc(wlo_done, 1)
            pool.sem_inc(t_done, 2)
            with pool.Fori(0, 2) as half:

                def load_w(c):
                    pool.wait_ge(wlo_done, half * NC_IN + max(c, 1))
                    pool.sem_inc(wait_carrier, 1)
                    col = w_in_column(c)
                    pool.dma_start(raw[:, c % 2], w_t[:, :, col:col + N]).then_inc(raw_in[c % 2], 16)

                def load_x(i):
                    pool.wait_ge(t_done, half * HT + i + 1)
                    pool.sem_inc(wait_carrier, 1)
                    pool.dma_start(x[:, i % 2], x_t[:, bass.ds(half * HT + i, 1)]).then_inc(x_in[i % 2], 16)

                load_x(0)
                load_w(0)
                load_x(1)
                load_w(1)
                for i in range(2, HT):
                    load_x(i)
                for c in range(2, NC_IN):
                    load_w(c)

        @block.scalar
        def _(act):
            act.wait_ge(rank_in, 16)
            act.wait_ge(rank_set, 2)
            nc.scalar.copy(rhi[:, :, 0:RANK], rraw[:]).then_inc(rhi_done, 1)
            act.sem_inc(out_done[0], 16)
            act.sem_inc(out_done[1], 16)
            with act.Fori(0, 2) as half:

                def split_hi(c):
                    act.wait_ge(raw_in[c % 2], (half * USES[c % 2] + c // 2 + 1) * 16)
                    act.wait_ge(mm_done, half * NC_IN * HT + max(c - 1, 0) * HT + 1)
                    nc.scalar.copy(whi[:, c % 2], raw[:, c % 2]).then_inc(whi_done, 1)

                def square(i):
                    act.wait_ge(x_in[i % 2], (half * (HT // 2) + i // 2 + 1) * 16)
                    nc.scalar.activation(squares[:], x[:, i % 2], ACT.Square,
                                         accum_out=ssq[:, i % 2:i % 2 + 1]).then_inc(sum_done, 1)
                    act.wait_ge(sum_done, half * HT + i + 1)
                    nc.scalar.activation(rs[:, i % 2:i % 2 + 1], ssq[:, i % 2:i % 2 + 1], ACT.Sqrt, scale=1.0 / D,
                                         bias=keep["const"]("eps")).then_inc(sq_done, 1)

                def h_hi(i):
                    act.wait_ge(t_done, half * HT + i + 3)
                    for b in range(2):
                        nc.scalar.copy(hhi[:, 4 * b:4 * b + 4, i], tp[:, i % 2, 4 * b:4 * b + 4]).then_inc(hi_done, 1)

                def evacuate(c, i):
                    act.wait_ge(mm_done, (half * NC_IN + c) * HT + i + 2)
                    act.wait_ge(out_done[i % 2], ((half * NC_IN + c) * (HT // 2) + i // 2 + 1) * 16)
                    nc.scalar.copy(stage[:, i % 2], acc[:, i % 2]).then_inc(acc_read, 1)

                split_hi(0)
                square(0)
                square(1)
                h_hi(0)
                for c in range(NC_IN):
                    if 1 <= c < NC_IN - 1:
                        split_hi(c + 1)
                    for i in range(HT):
                        if c == 0 and i + 2 < HT:
                            square(i + 2)
                        if c == 0 and i + 1 < HT:
                            h_hi(i + 1)
                        evacuate(c, i)
                        if c == 0 and i == 2:
                            split_hi(1)
                    for b in range(2 if c == 0 else 0):
                        act.wait_ge(r_done, half * 2 + b + 1)
                        nc.scalar.copy(keep["glr_t"][0:RANK, bass.ds((half * 2 + b) * N, N)],
                                       racc[0:RANK, :]).then_inc(r_read, 1)

        @block.sync
        def _(sp):
            with sp.Fori(0, 2) as half:
                for c in range(NC_IN):
                    for i in range(HT):
                        sp.wait_ge(acc_read, (half * NC_IN + c) * HT + i + 3)
                        sp.dma_start(proj_t[:, bass.ds(half * HT + i, 1), c * N:(c + 1) * N],
                                       stage[:, i % 2]).then_inc(out_done[i % 2], 16)
            for s in range(2):
                sp.wait_ge(out_done[s], (NC_IN * HT + 1) * 16)

        @block.vector
        def _(dve):
            step = Steps(dve, dve_step, 2 * HT)
            dve.wait_ge(rhi_done, 1)
            nc.vector.tensor_tensor(rlo[:, :, 0:RANK], rraw[:], rhi[:, :, 0:RANK], ALU.subtract).then_inc(rlo_done, 1)
            with dve.Fori(0, 2) as half:
                step.turn(half)

                def split_lo(c):
                    dve.wait_ge(whi_done, half * NC_IN + c + 1)
                    dve.wait_ge(mm_done, half * NC_IN * HT + max(c - 1, 0) * HT + 1)
                    nc.vector.tensor_tensor(wlo[:, c % 2], raw[:, c % 2], whi[:, c % 2], ALU.subtract).then_inc(wlo_done, 1)

                def make_h(i):
                    s = i % 2
                    dve.wait_ge(sq_done, half * HT + i + 1)
                    step(nc.vector.reciprocal(rinv[:, s:s + 1], rs[:, s:s + 1]))
                    last = nc.vector.scalar_tensor_tensor(out=x[:, s], in0=x[:, s], scalar=rinv[:, s:s + 1],
                                                          in1=keep["A1"][:], op0=ALU.mult, op1=ALU.mult)
                    step(last)
                    nc.vector.tensor_tensor(x[:, s], x[:, s], keep["sh1"][:], ALU.add).then_inc(h_ready, 1)

                def h_lo(i):
                    for b in range(2):
                        dve.wait_ge(hi_done, (half * HT + i) * 2 + b + 1)
                        nc.vector.tensor_tensor(hlo[:, 4 * b:4 * b + 4, i], tp[:, i % 2, 4 * b:4 * b + 4],
                                                hhi[:, 4 * b:4 * b + 4, i], ALU.subtract).then_inc(lo_done, 1)

                make_h(0)
                split_lo(0)
                make_h(1)
                h_lo(0)
                for i in range(HT):
                    if i + 2 < HT:
                        make_h(i + 2)
                    if i + 1 < HT:
                        h_lo(i + 1)
                    if i == 2:
                        split_lo(1)
                step.check()
                for c in range(2, NC_IN):
                    split_lo(c)

        @block.tensor
        def _(pe):
            pe.sem_inc(mm_done, 1)
            pe.sem_inc(lo_done, 4)
            pe.sem_inc(acc_read, 2)
            pe.sem_inc(r_read, 1)
            with pe.Fori(0, 2) as half:

                def transposes(i):
                    pe.wait_ge(h_ready, half * HT + i + 1)
                    pe.wait_ge(lo_done, (half * HT + i) * 2 + 2)
                    for s in range(KD):
                        mm = nc.tensor.transpose(tp[:, i % 2, s], x[:, i % 2, s * P:(s + 1) * P], keep["const"]("ident"))
                    mm.then_inc(t_done, 1)

                transposes(0)
                for c in range(NC_IN):
                    pe.wait_ge(whi_done, half * NC_IN + c + 1)
                    pe.wait_ge(wlo_done, half * NC_IN + c + 2)
                    for i in range(HT):
                        if c == 0 and i + 1 < HT:
                            transposes(i + 1)
                        if c == 0:
                            pe.wait_ge(lo_done, (half * HT + i) * 2 + 6)
                        pe.wait_ge(acc_read, (half * NC_IN + c) * HT + i + 1)
                        for s in range(KD):
                            mm = split_product(nc, acc[:, i % 2], hhi[:, s, i], hlo[:, s, i], whi[:, c % 2, s],
                                               wlo[:, c % 2, s], s == 0, s == KD - 1)
                        mm.then_inc(mm_done, 1)
                    for b in range(2 if c == 0 else 0):
                        pe.wait_ge(rlo_done, 1)
                        pe.wait_ge(r_read, half * 2 + b + 1)
                        t0 = b * (HT // 2)
                        for s in range(KD):
                            mm = split_product(nc, racc[:], rhi[:, s], rlo[:, s], hhi[:, s, t0:t0 + HT // 2],
                                               hlo[:, s, t0:t0 + HT // 2], s == 0, s == KD - 1)
                        mm.then_inc(r_done, 1)


def phase_mixer(nc, k, A, keep):
    const = keep["const"]
    PAIR = GH // 2
    NSUB = P // SUB
    kcols = [SUB * (i + 1) for i in range(NSUB)]
    kfrom = [sum(kcols[:i]) for i in range(NSUB)]
    KW = sum(kcols)
    CLAMP = 80.0
    proj = k.sb("proj", [P, 2, PROJ])
    o_out = k.sb("o_out", [P, 2, D])
    wgk = k.sb("wgk", [RANK + 1, 2 * P])
    normw = k.sb("normw", [P, 2, GDV])
    pos_i, pos_f = k.sb("pos_i", [P, NT], I32), k.sb("pos_f", [P, NT])
    ang, turns, red, wrap = (k.sb(n, [P, NT, RDK // 2]) for n in ("ang", "turns", "red", "wrap"))
    sin, cos = k.sb("sin", [P, NT, RDK // 2]), k.sb("cos", [P, NT, RDK // 2])
    glr = k.sb("glr", [RANK + 1, P])
    az, la, bs = k.sb("neg_abs", [P, 2 * P]), k.sb("log_decay", [P, 2 * P]), k.sb("run", [P, 4 * P])
    az_e, az_l = k.sb("az_exp", [P, 2 * P]), k.sb("az_ln", [P, 2 * P])
    dq, dk = k.sb("dq", [P, 2 * NSUB, SUB]), k.sb("dk", [P, PAIR, KW])
    eq, ek, eb = k.sb("eq", [P, 2 * NSUB, SUB]), k.sb("ek", [P, PAIR, KW]), k.sb("eb", [P, 4 * P])
    qt, qe, kt = k.sb("qt", [P, PAIR, NSUB, 2, SUB]), k.sb("qe", [P, PAIR, P]), k.sb("kt", [P, PAIR, KW])
    kup = k.sb("kup", [P, GH * GDK])
    sg = k.sb("sg", [P, GH, P])
    St = k.sb("gla_state", [P, PAIR, 2 * GDV])
    rm = k.sb("rope_m", [P, 2, 2 * RH, RDK // 2])
    rc = k.sb("rope_c", [P, 2, 2 * RH, RDK // 2])
    rr = k.sb("rope", [P, 2 * RH, RDK])
    rqT, rkT, rqx = (k.sb(n, [P, RH, P]) for n in ("rqT", "rkT", "rqx"))
    kz, sr = k.sb("kz", [P, RH, RDK]), k.sb("sr", [P, RH, P])
    R = k.sb("ret_state", [P, RH, RDK])
    mu = k.sb("mu", [P, RH])
    oc, sq = k.sb("oc", [P, 8, GDV]), k.sb("sq", [P, 8, GDV])
    var, lnv, r8 = (k.sb(n, [P, 8]) for n in ("var", "lnv", "r8"))
    ge, gl, gw, ginv = k.sb("ge", [P, 2, N]), k.sb("gl", [P, 2, N]), k.sb("gw", [P, 2, N]), k.sb("ginv", [P, 2, N])
    b_z, b_run, b_gT, b_gs, b_go, b_gu, b_q, b_k = (k.ps(n, [P, N]) for n in "z run gT gs go gu q k".split())
    names = ("glr z az az_e ln la run bs exps d qk kup gs sg go gu gS rm rr rt rqT kz rqx rs sr ro ru rR og oc sq var lnv r8 ge "
             "gl ginv gw o out").split()
    ev = {n: k.sem("ev_" + n) for n in names}
    setup_dma, pos_step, pool_set, dve_step, pool_step, sin_done = k.sems(
        "setup_dma pos_step pool_set dve_step pool_step sin_done")
    p_in = [k.sem(f"p_in{s}") for s in range(2)]
    o_done = [k.sem(f"o_done{s}") for s in range(2)]
    proj_t = keep["proj"].rearrange("(t p) n -> p t n", p=P)
    o_t = keep["o"].rearrange("(t p) n -> p t n", p=P)
    TWO_PI = 2 * np.pi
    c1 = float(np.float32(np.floor(TWO_PI * 2 ** 5) / 2 ** 5))
    c2 = float(np.float32(np.floor((TWO_PI - c1) * 2 ** 14) / 2 ** 14))
    c3 = float(np.float32(TWO_PI - c1 - c2))
    MAGIC = 12582912.0
    HALF = RDK // 2

    def heads(ap, n):
        return ap.rearrange("p (h d) -> p h d", h=n)

    def bc(ap, shape):
        return ap.to_broadcast(shape)

    with nc.Block() as block:

        @block.sync
        def _(sp):
            sp.dma_start(wgk[0:RANK, :], A["w_gk2"].rearrange("o r n -> (o r) n")).then_inc(setup_dma, 16)
            sp.dma_start(wgk[RANK:RANK + 1, :], A["b_gk"]).then_inc(setup_dma, 16)
            sp.dma_start(normw[:, 0], row(A["gla_onorm"])).then_inc(setup_dma, 16)
            sp.dma_start(normw[:, 1], row(A["ret_onorm"])).then_inc(setup_dma, 16)
            sp.dma_start(pos_i[:], A["positions"].rearrange("o (t p) -> p (o t)", p=P),
                         allow_slow_non_contiguous=True).then_inc(setup_dma, 16)
            for u in range(2):
                sp.sem_inc(o_done[u], 16)
            with sp.Fori(0, NT // 2) as j:
                for u in range(2):
                    i = j * 2 + u
                    for n in ("go", "kup", "gw", "ge", "rr"):
                        sp.wait_ge(ev[n], i + 1)
                    sp.dma_start(proj[:, u], proj_t[:, bass.ds(i, 1)]).then_inc(p_in[u], 16)
                    if u == 0:
                        with sp.If(j > 0):
                            sp.wait_ge(ev["o"], i + 2)
                            sp.dma_start(o_t[:, bass.ds(i, 1)], o_out[:, 1]).then_inc(o_done[1], 16)
                    else:
                        sp.wait_ge(ev["o"], i + 2)
                        sp.dma_start(o_t[:, bass.ds(i, 1)], o_out[:, 0]).then_inc(o_done[0], 16)
            sp.wait_ge(ev["o"], NT + 2)
            sp.dma_start(o_t[:, NT:NT + 1], o_out[:, 1]).then_inc(o_done[1], 16)
            for u in range(2):
                sp.wait_ge(o_done[u], 16 * (NT // 2 + 1))

        @block.gpsimd
        def _(pool):
            own = Steps(pool, pool_step, 2 * 2)
            nc.gpsimd.memset(St[:], 0.0).then_inc(pool_set, 1)
            nc.gpsimd.memset(R[:], 0.0).then_inc(pool_set, 1)
            nc.gpsimd.memset(sg[:], 0.0).then_inc(pool_set, 1)
            nc.gpsimd.memset(qt[:], 0.0).then_inc(pool_set, 1)
            for n in names:
                pool.sem_inc(ev[n], 2)
            pool.wait_ge(setup_dma, 80)
            pool.wait_ge(sin_done, 2)
            with pool.Fori(0, NT // 2) as j:
                own.turn(j)
                for u in range(2):
                    i = j * 2 + u
                    pj = proj[:, u]
                    now, last = i + 3, i + 2
                    sin_i = sin[:, bass.ds(i, 1)]
                    pool.wait_ge(ev["z"], last)
                    nc.gpsimd.tensor_copy(glr[:], keep["glr_t"][:, bass.ds(i * P, P)]).then_inc(ev["glr"], 1)
                    pool.wait_ge(p_in[u], (j + 1) * 16)
                    pool.wait_ge(ev["rr"], last)
                    x = heads(pj[:, C_RQ:C_RQ + 2 * N], 2 * RH)
                    nc.gpsimd.tensor_tensor(rm[:, 0], x[:, :, HALF:], sin_i.to_broadcast([P, 2 * RH, HALF]), ALU.mult)
                    nc.gpsimd.tensor_tensor(rm[:, 1], x[:, :, 0:HALF], sin_i.to_broadcast([P, 2 * RH, HALF]),
                                            ALU.mult).then_inc(ev["rm"], 1)
                    pool.wait_ge(ev["o"], last)
                    nc.gpsimd.tensor_tensor(heads(gw[:, 0], GH), heads(pj[:, C_GG:C_GG + N], GH),
                                            normw[:, 0:1].to_broadcast([P, GH, GDV]), ALU.mult)
                    nc.gpsimd.tensor_tensor(heads(gw[:, 1], RH), heads(pj[:, C_RG:C_RG + N], RH),
                                            normw[:, 1:2].to_broadcast([P, RH, RDK]), ALU.mult).then_inc(ev["gw"], 1)
                    pool.wait_ge(ev["exps"], now)
                    pool.wait_ge(ev["gu"], last)
                    nc.gpsimd.tensor_tensor(kup[:], pj[:, C_GK:C_GK + GH * GDK], eb[:, 2 * P:4 * P],
                                            ALU.mult).then_inc(ev["kup"], 1)
                    pool.wait_ge(ev["rr"], now)
                    pool.wait_ge(ev["ru"], last)
                    nc.gpsimd.tensor_tensor(kz[:], rr[:, RH:2 * RH],
                                            const("zeta").unsqueeze(2).to_broadcast([P, RH, RDK]),
                                            ALU.mult).then_inc(ev["kz"], 1)
                    pool.wait_ge(ev["ginv"], now)
                    pool.wait_ge(ev["gw"], now)
                    own(nc.gpsimd.tensor_tensor(gw[:], gw[:], ginv[:], ALU.mult))
                    pool.wait_ge(ev["out"], now)
                    own(nc.gpsimd.tensor_tensor(o_out[:, u], o_out[:, u], gw[:].rearrange("p a n -> p (a n)"), ALU.mult))
                    pool.sem_inc(ev["o"], 1)
                own.check()

        @block.scalar
        def _(act):
            act.wait_ge(pos_step, 1)
            nc.scalar.activation(sin[:], red[:], ACT.Sin).then_inc(sin_done, 1)
            nc.scalar.activation(cos[:], wrap[:], ACT.Sin).then_inc(sin_done, 1)
            with act.Fori(0, NT // 2) as j:
                for u in range(2):
                    i = j * 2 + u
                    pj = proj[:, u]
                    now, last = i + 3, i + 2
                    act.wait_ge(p_in[u], (j + 1) * 16)
                    nc.scalar.activation(ge[:, 0], pj[:, C_GG:C_GG + N], ACT.Exp, scale=-1.0)
                    nc.scalar.activation(ge[:, 1], pj[:, C_RG:C_RG + N], ACT.Exp, scale=-1.0).then_inc(ev["ge"], 1)
                    act.wait_ge(ev["z"], now)
                    nc.scalar.activation(az[:], b_z[:, 0:2 * P], ACT.Abs).then_inc(ev["az"], 1)
                    act.wait_ge(ev["az"], now)
                    nc.scalar.activation(az_e[:], az[:], ACT.Exp, scale=-1.0).then_inc(ev["az_e"], 1)
                    act.wait_ge(ev["az_e"], now)
                    act.wait_ge(ev["la"], last)
                    nc.scalar.activation(az_l[:], az_e[:], ACT.Ln, bias=const("ones")[:, 0:1]).then_inc(ev["ln"], 1)
                    act.wait_ge(ev["bs"], now)
                    act.wait_ge(ev["d"], now)
                    act.wait_ge(ev["qk"], last)
                    act.wait_ge(ev["gS"], last)
                    act.wait_ge(ev["kup"], last)
                    nc.scalar.activation(eb[:], bs[:], ACT.Exp)
                    nc.scalar.activation(eq[:], dq[:], ACT.Exp)
                    nc.scalar.activation(ek[:], dk[:], ACT.Exp, scale=-1.0).then_inc(ev["exps"], 1)
                    act.wait_ge(ev["ge"], now)
                    nc.scalar.activation(gl[:], ge[:], ACT.Ln, bias=const("ones")[:, 0:1]).then_inc(ev["gl"], 1)
                    act.wait_ge(ev["gl"], now)
                    act.wait_ge(ev["o"], last)
                    nc.scalar.activation(ginv[:], gl[:], ACT.Exp, scale=-1.0).then_inc(ev["ginv"], 1)
                    act.wait_ge(ev["rt"], now)
                    act.wait_ge(ev["rs"], last)
                    act.wait_ge(ev["rqx"], last)
                    nc.scalar.copy(rqT[:], heads(b_q[:], RH))
                    nc.scalar.copy(rkT[:], heads(b_k[:], RH)).then_inc(ev["rqT"], 1)
                    act.wait_ge(ev["go"], now)
                    act.wait_ge(ev["out"], last)
                    nc.scalar.copy(oc[:, 0:GH], heads(b_go[:], GH)).then_inc(ev["og"], 1)
                    act.wait_ge(ev["og"], now)
                    act.wait_ge(ev["oc"], now)
                    act.wait_ge(ev["var"], last)
                    nc.scalar.activation(sq[:], oc[:], ACT.Square).then_inc(ev["sq"], 1)
                    act.wait_ge(ev["var"], now)
                    nc.scalar.activation(lnv[:], var[:], ACT.Ln, scale=1.0 / GDV, bias=const("eps")).then_inc(ev["lnv"], 1)
                    act.wait_ge(ev["lnv"], now)
                    act.wait_ge(ev["out"], last)
                    nc.scalar.activation(r8[:], lnv[:], ACT.Exp, scale=-0.5).then_inc(ev["r8"], 1)

        @block.vector
        def _(dve):
            own = Steps(dve, dve_step, 0)
            dve.wait_ge(setup_dma, 80)
            own(nc.vector.tensor_copy(pos_f[:], pos_i[:]))
            own(nc.vector.tensor_tensor(ang[:], pos_f[:].unsqueeze(2).to_broadcast([P, NT, HALF]),
                                        const("inv_freq").unsqueeze(1).to_broadcast([P, NT, HALF]), ALU.mult))

            def reduce_turns(out, a):
                own(nc.vector.tensor_scalar(turns[:], a, 1.0 / TWO_PI, MAGIC, ALU.mult, ALU.add))
                own(nc.vector.tensor_scalar(turns[:], turns[:], MAGIC, None, ALU.subtract))
                own(nc.vector.scalar_tensor_tensor(out=out, in0=turns[:], scalar=-c1, in1=a, op0=ALU.mult, op1=ALU.add))
                own(nc.vector.scalar_tensor_tensor(out=out, in0=turns[:], scalar=-c2, in1=out, op0=ALU.mult, op1=ALU.add))
                own(nc.vector.scalar_tensor_tensor(out=out, in0=turns[:], scalar=-c3, in1=out, op0=ALU.mult, op1=ALU.add))

            def clamp(ap):
                own(nc.vector.tensor_scalar(ap, ap, float(np.float32(3.1415925)), -float(np.float32(3.1415925)), ALU.min, ALU.max))

            reduce_turns(red[:], ang[:])
            own(nc.vector.tensor_scalar(wrap[:], red[:], float(np.pi / 2), None, ALU.add))
            own(nc.vector.tensor_scalar(turns[:], wrap[:], float(np.pi), -TWO_PI, ALU.is_gt, ALU.mult))
            own(nc.vector.tensor_tensor(wrap[:], wrap[:], turns[:], ALU.add))
            clamp(red[:])
            clamp(wrap[:])
            dve.sem_inc(pos_step, 1)
            dve.wait_ge(pool_set, 4)
            dve.wait_ge(sin_done, 2)
            SETUP = own.n
            own.per_turn = PER = 2 * 11
            with dve.Fori(0, NT // 2) as j:
                own.base, own.n = j * PER + SETUP, 0
                for u in range(2):
                    i = j * 2 + u
                    pj = proj[:, u]
                    now, last = i + 3, i + 2
                    cos_i = cos[:, bass.ds(i, 1)]
                    dve.wait_ge(p_in[u], (j + 1) * 16)
                    x = heads(pj[:, C_RQ:C_RQ + 2 * N], 2 * RH)
                    own(nc.vector.tensor_tensor(rc[:, 0], x[:, :, 0:HALF], cos_i.to_broadcast([P, 2 * RH, HALF]), ALU.mult))
                    own(nc.vector.tensor_tensor(rc[:, 1], x[:, :, HALF:], cos_i.to_broadcast([P, 2 * RH, HALF]), ALU.mult))
                    dve.wait_ge(ev["rm"], now)
                    dve.wait_ge(ev["rt"], last)
                    dve.wait_ge(ev["kz"], last)
                    own(nc.vector.tensor_tensor(rr[:, :, 0:HALF], rc[:, 0], rm[:, 0], ALU.subtract))
                    nc.vector.tensor_tensor(rr[:, :, HALF:], rc[:, 1], rm[:, 1], ALU.add).then_inc(ev["rr"], 1)
                    dve.wait_ge(ev["ln"], now)
                    dve.wait_ge(ev["run"], last)
                    nc.vector.scalar_tensor_tensor(out=la[:], in0=b_z[:, 0:2 * P], scalar=0.0, in1=az_l[:],
                                                   op0=ALU.min, op1=ALU.subtract).then_inc(ev["la"], 1)
                    dve.wait_ge(ev["run"], now)
                    dve.wait_ge(ev["exps"], last)
                    nc.vector.tensor_copy(bs[:], b_run[:]).then_inc(ev["bs"], 1)
                    dve.wait_ge(ev["bs"], now)
                    b2 = bs[:, 0:2 * P]
                    sub = b2.rearrange("p (c t) -> p c t", t=SUB)
                    own(nc.vector.tensor_tensor(dq[:], sub, sub[:, :, SUB // 2 - 1:SUB // 2].to_broadcast([P, 2 * NSUB, SUB]),
                                                ALU.subtract))
                    bp = b2.rearrange("p (a t) -> p a t", a=PAIR)
                    for c in range(NSUB):
                        ref = c * SUB + SUB // 2 - 1
                        own(nc.vector.tensor_tensor(dk[:, :, kfrom[c]:kfrom[c] + kcols[c]], bp[:, :, 0:kcols[c]],
                                                    bp[:, :, ref:ref + 1].to_broadcast([P, PAIR, kcols[c]]), ALU.subtract))
                    own(nc.vector.tensor_scalar(dq[:], dq[:], CLAMP, None, ALU.min))
                    nc.vector.tensor_scalar(dk[:], dk[:], -CLAMP, None, ALU.max).then_inc(ev["d"], 1)
                    dve.wait_ge(ev["rqT"], now)
                    dve.wait_ge(ev["ro"], last)
                    nc.vector.tensor_tensor(rqx[:], rqT[:], heads(const("xi"), RH), ALU.mult).then_inc(ev["rqx"], 1)
                    dve.wait_ge(ev["rs"], now)
                    nc.vector.tensor_tensor(sr[:], heads(b_q[:], RH), heads(const("decay"), RH), ALU.mult).then_inc(ev["sr"], 1)
                    dve.wait_ge(ev["exps"], now)
                    dve.wait_ge(ev["gs"], last)
                    dve.wait_ge(ev["go"], last)
                    q_t = b_gT[:, 0:2 * P].rearrange("p (a t) -> p a t", a=PAIR)
                    k_t = b_gT[:, 2 * P:4 * P].rearrange("p (a t) -> p a t", a=PAIR)
                    scale = GDK ** -0.5
                    for h in range(2):
                        rows = slice(h * GDK, (h + 1) * GDK)
                        nc.vector.scalar_tensor_tensor(out=qt[rows, :, :, h].rearrange("p a c t -> p (a c) t"),
                                                       in0=b_gT[rows, 0:2 * P].rearrange("p (c t) -> p c t", t=SUB),
                                                       scalar=scale, in1=eq[rows], op0=ALU.mult, op1=ALU.mult)
                    nc.vector.scalar_tensor_tensor(out=qe[:], in0=q_t, scalar=scale,
                                                   in1=eb[:, 0:2 * P].rearrange("p (a t) -> p a t", a=PAIR),
                                                   op0=ALU.mult, op1=ALU.mult)
                    for c in range(NSUB):
                        ins = nc.vector.tensor_tensor(kt[:, :, kfrom[c]:kfrom[c] + kcols[c]], k_t[:, :, 0:kcols[c]],
                                                      ek[:, :, kfrom[c]:kfrom[c] + kcols[c]], ALU.mult)
                    ins.then_inc(ev["qk"], 1)
                    dve.wait_ge(ev["gs"], now)
                    for c in range(NSUB):
                        cols = slice(c * SUB, (c + 1) * SUB)
                        ins = nc.vector.tensor_tensor(
                            sg[0:kcols[c], :, cols], heads(b_gs[:], GH)[0:kcols[c], :, cols],
                            const("causal")[0:kcols[c], cols].unsqueeze(1).to_broadcast([kcols[c], GH, SUB]), ALU.mult)
                    ins.then_inc(ev["sg"], 1)
                    dve.wait_ge(ev["ro"], now)
                    own(nc.vector.tensor_reduce(mu[:], heads(b_k[:], RH), AX_X, ALU.add))
                    own(nc.vector.tensor_scalar(mu[:], mu[:], -1.0 / RDK, None, ALU.mult))
                    dve.wait_ge(ev["out"], last)
                    nc.vector.tensor_tensor(oc[:, GH:8], heads(b_k[:], RH), mu[:].unsqueeze(2).to_broadcast([P, RH, RDK]),
                                            ALU.add).then_inc(ev["oc"], 1)
                    dve.wait_ge(ev["ru"], now)
                    for h in range(RH):
                        ins = nc.vector.scalar_tensor_tensor(out=R[:, h], in0=R[:, h], scalar=GAMMA_TILE[h],
                                                             in1=b_z[:, h * RDK:(h + 1) * RDK], op0=ALU.mult, op1=ALU.add)
                    ins.then_inc(ev["rR"], 1)
                    dve.wait_ge(ev["gu"], now)
                    dve.wait_ge(ev["go"], now)
                    for h in range(GH):
                        pr, rows = h // 2, slice((h % 2) * GDK, (h % 2 + 1) * GDK)
                        cols = slice((h % 2) * GDV, (h % 2 + 1) * GDV)
                        ins = nc.vector.scalar_tensor_tensor(
                            out=St[rows, pr, cols], in0=St[rows, pr, cols], scalar=eb[rows, (pr + 1) * P - 1:(pr + 1) * P],
                            in1=b_gu[rows, pr * 2 * GDV + cols.start:pr * 2 * GDV + cols.stop], op0=ALU.mult, op1=ALU.add)
                    ins.then_inc(ev["gS"], 1)
                    dve.wait_ge(ev["sq"], now)
                    nc.vector.tensor_reduce(var[:], sq[:], AX_X, ALU.add).then_inc(ev["var"], 1)
                    dve.wait_ge(ev["r8"], now)
                    dve.wait_ge(o_done[u], (j + 1) * 16)
                    nc.vector.tensor_tensor(heads(o_out[:, u], 8), oc[:], r8[:].unsqueeze(2).to_broadcast([P, 8, GDV]),
                                            ALU.mult).then_inc(ev["out"], 1)
                own.check()

        @block.tensor
        def _(pe):
            pe.wait_ge(setup_dma, 80)
            pe.wait_ge(pool_set, 4)
            ident = const("ident")
            with pe.Fori(0, NT // 2) as j:
                for u in range(2):
                    i = j * 2 + u
                    pj = proj[:, u]
                    now, last = i + 3, i + 2
                    pe.wait_ge(ev["glr"], now)
                    pe.wait_ge(ev["rR"], last)
                    nc.tensor.matmul(b_z[:, 0:2 * P], glr[:], wgk[:], start=True, stop=True).then_inc(ev["z"], 1)
                    pe.wait_ge(p_in[u], (j + 1) * 16)
                    pe.wait_ge(ev["qk"], last)
                    for c in range(4):
                        nc.tensor.transpose(b_gT[:, c * P:(c + 1) * P], pj[:, C_GQ + c * P:C_GQ + (c + 1) * P], ident)
                    pe.wait_ge(ev["rr"], now)
                    pe.wait_ge(ev["sr"], last)
                    pe.wait_ge(ev["oc"], last)
                    for h in range(RH):
                        nc.tensor.transpose(b_q[:, h * P:(h + 1) * P], rr[:, h], ident)
                    for h in range(RH):
                        mm = nc.tensor.transpose(b_k[:, h * P:(h + 1) * P], rr[:, RH + h], ident)
                    mm.then_inc(ev["rt"], 1)
                    pe.wait_ge(ev["la"], now)
                    pe.wait_ge(ev["bs"], last)
                    for c in range(2):
                        nc.tensor.matmul(b_run[:, c * P:(c + 1) * P], la[:, c * P:(c + 1) * P], const("sum_to"),
                                         start=True, stop=True)
                    nc.tensor.matmul(b_run[:, 2 * P:4 * P], const("sum_after"), la[:], start=True,
                                     stop=True).then_inc(ev["run"], 1)
                    pe.wait_ge(ev["rqT"], now)
                    for h in range(RH):
                        mm = nc.tensor.matmul(b_q[:, h * P:(h + 1) * P], rkT[:, h], rqT[:, h], start=True, stop=True)
                    mm.then_inc(ev["rs"], 1)
                    pe.wait_ge(ev["kz"], now)
                    for h in range(RH):
                        mm = nc.tensor.matmul(b_z[:, h * RDK:(h + 1) * RDK], kz[:, h],
                                              pj[:, C_RV + h * RDK:C_RV + (h + 1) * RDK], start=True, stop=True)
                    mm.then_inc(ev["ru"], 1)
                    pe.wait_ge(ev["qk"], now)
                    pe.wait_ge(ev["sg"], last)
                    for a in range(PAIR):
                        for c in range(NSUB):
                            mm = nc.tensor.matmul(heads(b_gs[:], GH)[0:kcols[c], 2 * a:2 * a + 2, c * SUB:(c + 1) * SUB],
                                                  kt[:, a, kfrom[c]:kfrom[c] + kcols[c]], qt[:, a, c],
                                                  start=True, stop=True)
                    mm.then_inc(ev["gs"], 1)
                    pe.wait_ge(ev["kup"], now)
                    pe.wait_ge(ev["gS"], last)
                    for c in range(PAIR):
                        mm = nc.tensor.matmul(b_gu[:, c * 2 * GDV:(c + 1) * 2 * GDV], kup[:, c * P:(c + 1) * P],
                                              pj[:, C_GV + c * 2 * GDV:C_GV + (c + 1) * 2 * GDV], start=True, stop=True)
                    mm.then_inc(ev["gu"], 1)
                    pe.wait_ge(ev["sr"], now)
                    pe.wait_ge(ev["rqx"], now)
                    pe.wait_ge(ev["rR"], last)
                    for h in range(RH):
                        nc.tensor.matmul(b_k[:, h * P:(h + 1) * P], sr[:, h], pj[:, C_RV + h * RDK:C_RV + (h + 1) * RDK],
                                         start=True, stop=False)
                        mm = nc.tensor.matmul(b_k[:, h * P:(h + 1) * P], rqx[:, h], R[:, h], start=False, stop=True)
                    mm.then_inc(ev["ro"], 1)
                    pe.wait_ge(ev["sg"], now)
                    pe.wait_ge(ev["og"], last)
                    for c in range(PAIR):
                        cols = slice(c * 2 * GDV, (c + 1) * 2 * GDV)
                        nc.tensor.matmul(b_go[:, cols], qe[:, c], St[:, c], start=True, stop=False, skip_group_check=True)
                        for h in (2 * c, 2 * c + 1):
                            mm = nc.tensor.matmul(b_go[:, h * GDV:(h + 1) * GDV], sg[:, h],
                                                  pj[:, C_GV + h * GDV:C_GV + (h + 1) * GDV], start=False,
                                                  stop=(h % 2 == 1), skip_group_check=True)
                    mm.then_inc(ev["go"], 1)




def phase_routing(nc, k, A, keep):
    const = keep["const"]
    raw = k.sb("w_raw", [P, KD, N])
    whi, wlo = (k.sb(n, [P, 2, KD, N], F32R) for n in ("w_hi", "w_lo"))
    wr = k.sb("w_router", [P, KD, E])
    br = k.sb("b_router", [P, E])
    bd = k.sb("b_down", [E, D])
    g1, A2, sh2, g2 = (k.sb(n, [P, D]) for n in ("g1", "A2", "sh2", "g2"))
    empty = k.sb("empty", [P, PLACES, 2], I32)
    o, x = k.sb("o", [P, 2, D]), k.sb("x", [P, 2, D])
    ohi, olo = (k.sb(n, [P, KD, P], F32R) for n in ("o_hi", "o_lo"))
    x2, h2, yi = (k.sb(n, [P, D]) for n in ("x2", "h2", "yi"))
    squares = k.sb("squares", [P, D], mybir.dt.bfloat16)
    h2T = k.sb("h2T", [P, KD, P])
    ssq, lnv, rs = (k.sb(n, [P, 1]) for n in ("ssq", "lnv", "rs"))
    lg, lr, mask, ex, W, key, pick, kf, rkf = (k.sb(n, [P, E]) for n in
                                               "lg lr mask ex W key pick kf rkf".split())
    best, top = k.sb("best", [P, 8]), k.sb("top", [P, 8])
    neg, den = k.sb("neg", [P, 1]), k.sb("den", [P, 1])
    run = k.sb("run", [P, E])
    ri, ra, rb = (k.sb(n, [P, E], I32) for n in ("ri", "ra", "rb"))
    wj, idx, rec = k.sb("wj", [P, TOPK]), k.sb("idx", [P, TOPK], I32), k.sb("rec", [P, TOPK, 2], I32)
    wT = k.sb("wT", [E, P])
    over = k.sb("over", [P, E, NT])
    tiles, groups, cumg, cumt, sel = (k.sb(n, [P, E]) for n in "tiles groups cumg cumt sel".split())
    gT, tT = k.sb("gT", [E, P]), k.sb("tT", [E, P])
    col = k.sb("col", [P, 8])
    table, table_i = k.sb("table", [P, 4]), k.sb("table_i", [P, 4], I32)
    acc, tp, tq = k.ps("acc", [P, 2, N]), k.ps("tp", [P, KD, P]), k.ps("tq", [P, KD, P])
    sm, wt = k.ps("sm", [P, N]), k.ps("wt", [P, N])
    names = ("t1 ohi olo mm xg x2 sq lnv rs h2 t2 h2t lg lgs ex W mask rk wt wtc bd yi rec stored").split()
    ev = {n: k.sem("ev_" + n) for n in names}
    setup_dma, w_in, whi_done, wlo_done, pool_set, dve_step, h2_out, y_out, place_out, empty_set, empty_out = k.sems(
        "setup_dma w_in whi_done wlo_done pool_set dve_step h2_out y_out place_out empty_set empty_out")
    table_step, table_out, wait_carrier, table_ready, table_t = k.sems(
        "table_step table_out wait_carrier table_ready table_t")
    o_in = [k.sem(f"o_in{s}") for s in range(2)]
    x_in = [k.sem(f"x_in{s}") for s in range(2)]
    o_t = keep["o"].rearrange("(t p) n -> p t n", p=P)
    x_t = A["x"].rearrange("o (t p) d -> p (o t) d", p=P)
    h2_t = keep["h2"].rearrange("(t p) n -> p t n", p=P)
    y_t = [y.rearrange("(t p) n -> p t n", p=P) for y in keep["y"]]
    w_t = A["w_out"].rearrange("o (s p) n -> p (o s) n", p=P)
    NOWHERE = 3.0e38
    with nc.Block() as block:

        @block.sync
        def _(sp):
            sp.dma_start(raw[:], w_t[:, :, 0:N]).then_inc(w_in, 16)
            sp.dma_start(wr[:], A["w_router"].rearrange("o (s p) e -> p (o s) e", p=P)).then_inc(setup_dma, 16)
            sp.dma_start(br[:], row(A["b_router"])).then_inc(setup_dma, 16)
            sp.dma_start(bd[:], A["b_down"].rearrange("o e d -> (o e) d")).then_inc(setup_dma, 16)
            for t, n in ((g1, "g1"), (A2, "A2"), (sh2, "sh2"), (g2, "g2")):
                sp.dma_start(t[:], keep[n]).then_inc(setup_dma, 16)
            sp.wait_ge(wlo_done, 1)
            sp.dma_start(raw[:], w_t[:, :, N:2 * N]).then_inc(w_in, 16)
            with sp.Fori(0, NT // 2) as j:
                for u in range(2):
                    i = j * 2 + u
                    sp.wait_ge(ev["t1"], i + 1)
                    sp.dma_start(o[:, u], o_t[:, bass.ds(i + 1, 1)]).then_inc(o_in[u], 16)
                    sp.wait_ge(ev["x2"], i + 1)
                    sp.dma_start(x[:, u], x_t[:, bass.ds(i, 1)]).then_inc(x_in[u], 16)
            sp.wait_ge(table_step, 1)
            sp.dma_start(keep["groups"], table_i[:]).then_inc(table_out, 16)
            sp.wait_ge(table_out, 16)

        @block.gpsimd
        def _(pool):
            nc.gpsimd.memset(run[:], 0.0).then_inc(pool_set, 1)
            for n in names:
                pool.sem_inc(ev[n], 2)
            pool.wait_ge(empty_set, 1)
            pool.dma_start(keep["places"].rearrange("(p q) c -> p (q c)", p=P), empty[:].rearrange("p q c -> p (q c)")
                           ).then_inc(empty_out, 16)
            pool.wait_ge(empty_out, 16)
            with pool.Fori(0, NT) as i:
                pool.wait_ge(ev["yi"], i + 3)
                pool.sem_inc(wait_carrier, 1)
                for half in range(2):
                    pool.dma_start(y_t[half][:, bass.ds(i, 1)], yi[:, half * N:(half + 1) * N]).then_inc(y_out, 16)
                pool.wait_ge(ev["rec"], i + 3)
                pool.sem_inc(wait_carrier, 1)
                for c in range(TOPK):
                    pool.indirect_dma_start(out=keep["places"], out_offset=bass.IndirectOffsetOnAxis(ap=idx[:, c:c + 1], axis=0),
                                            in_=rec[:, c], in_offset=None).then_inc(place_out, 16)
                pool.wait_ge(y_out, (i + 1) * 32)
                pool.wait_ge(place_out, (i + 1) * 16 * TOPK)
                pool.sem_inc(ev["stored"], 1)

        @block.scalar
        def _(act):
            act.sem_inc(h2_out, 16)
            for c in range(2):
                act.wait_ge(w_in, 16 * (c + 1))
                nc.scalar.copy(whi[:, c], raw[:]).then_inc(whi_done, 1)
            with act.Fori(0, NT) as i:
                now, last = i + 3, i + 2
                act.wait_ge(ev["t1"], now)
                act.wait_ge(ev["mm"], last)
                for b in range(2):
                    nc.scalar.copy(ohi[:, 4 * b:4 * b + 4], tp[:, 4 * b:4 * b + 4]).then_inc(ev["ohi"], 1)
                act.wait_ge(ev["x2"], now)
                nc.scalar.activation(squares[:], x2[:], ACT.Square, accum_out=ssq[:]).then_inc(ev["sq"], 1)
                act.wait_ge(ev["sq"], now)
                nc.scalar.activation(lnv[:], ssq[:], ACT.Ln, scale=1.0 / D, bias=const("eps")).then_inc(ev["lnv"], 1)
                act.wait_ge(ev["lnv"], now)
                act.wait_ge(ev["h2"], last)
                nc.scalar.activation(rs[:], lnv[:], ACT.Exp, scale=-0.5).then_inc(ev["rs"], 1)
                act.wait_ge(ev["h2"], now)
                act.dma_start(h2_t[:, bass.ds(i, 1)], h2[:]).then_inc(h2_out, 16)
                act.wait_ge(ev["t2"], now)
                act.wait_ge(ev["lg"], last)
                for b in range(2):
                    ins = nc.scalar.copy(h2T[:, 4 * b:4 * b + 4], tq[:, 4 * b:4 * b + 4])
                ins.then_inc(ev["h2t"], 1)
                act.wait_ge(ev["lgs"], now)
                act.wait_ge(ev["W"], last)
                nc.scalar.activation(ex[:], lg[:], ACT.Exp, bias=neg[:]).then_inc(ev["ex"], 1)
                act.wait_ge(ev["wt"], now)
                act.wait_ge(ev["bd"], last)
                nc.scalar.copy(wT[:], wt[0:E, 0:P]).then_inc(ev["wtc"], 1)
            act.wait_ge(h2_out, 16 * (NT + 1))

        @block.vector
        def _(dve):
            own = Steps(dve, dve_step)
            own(nc.vector.memset(empty[:], 0))
            own(nc.vector.tensor_scalar(col[:, 0:1], const("number"), float(S), None, ALU.add))
            nc.vector.tensor_copy(empty[:, :, 0], col[:, 0:1].to_broadcast([P, PLACES])).then_inc(empty_set, 1)
            for c in range(2):
                dve.wait_ge(whi_done, c + 1)
                nc.vector.tensor_tensor(wlo[:, c], raw[:], whi[:, c], ALU.subtract).then_inc(wlo_done, 1)
            dve.wait_ge(setup_dma, 7 * 16)
            dve.wait_ge(pool_set, 1)
            SETUP = own.n
            own.per_turn = PER = 2 * 25
            with dve.Fori(0, NT // 2) as j:
                own.base, own.n = j * PER + SETUP, 0
                for u in range(2):
                    i = j * 2 + u
                    now, last = i + 3, i + 2
                    for b in range(2):
                        dve.wait_ge(ev["ohi"], i * 2 + b + 3)
                        nc.vector.tensor_tensor(olo[:, 4 * b:4 * b + 4], tp[:, 4 * b:4 * b + 4], ohi[:, 4 * b:4 * b + 4],
                                                ALU.subtract).then_inc(ev["olo"], 1)
                    dve.wait_ge(ev["mm"], now)
                    own(nc.vector.tensor_tensor(x2[:], acc[:].rearrange("p a n -> p (a n)"), g1[:], ALU.mult))
                    dve.wait_ge(x_in[u], (j + 1) * 16)
                    nc.vector.tensor_tensor(x2[:], x2[:], x[:, u], ALU.add).then_inc(ev["x2"], 1)
                    dve.wait_ge(ev["rs"], now)
                    dve.wait_ge(ev["t2"], last)
                    dve.wait_ge(h2_out, (i + 1) * 16)
                    own(nc.vector.scalar_tensor_tensor(out=h2[:], in0=x2[:], scalar=rs[:], in1=A2[:], op0=ALU.mult,
                                                       op1=ALU.mult))
                    nc.vector.tensor_tensor(h2[:], h2[:], sh2[:], ALU.add).then_inc(ev["h2"], 1)
                    dve.wait_ge(ev["lg"], now)
                    own(nc.vector.tensor_tensor(lg[:], sm[:, 0:E], br[:], ALU.add))
                    dve.sem_inc(wait_carrier, 1)
                    own(nc.vector.max(best[:], lg[:]))
                    nc.vector.tensor_scalar(neg[:], best[:, 0:1], -1.0, None, ALU.mult).then_inc(ev["lgs"], 1)
                    own(nc.vector.memset(best[:, TOPK:8], NOWHERE))
                    dve.sem_inc(wait_carrier, 1)
                    own(nc.vector.match_replace(lr[:], best[:], lg[:], -NOWHERE))
                    dve.wait_ge(ev["rk"], last)
                    nc.vector.tensor_tensor(mask[:], lr[:], lg[:], ALU.not_equal).then_inc(ev["mask"], 1)
                    dve.wait_ge(ev["mask"], now)
                    dve.wait_ge(ev["ex"], now)
                    own(nc.vector.tensor_tensor(W[:], ex[:], mask[:], ALU.mult))
                    own(nc.vector.tensor_reduce(den[:], W[:], AX_X, ALU.add))
                    own(nc.vector.reciprocal(den[:], den[:]))
                    nc.vector.tensor_scalar(W[:], W[:], den[:], None, ALU.mult).then_inc(ev["W"], 1)
                    dve.wait_ge(ev["rk"], now)
                    own(nc.vector.tensor_tensor(rkf[:], sm[:, E:2 * E], run[:], ALU.add))
                    own(nc.vector.tensor_tensor(run[:], sm[:, 2 * E:3 * E], run[:], ALU.add))
                    own(nc.vector.tensor_copy(ri[:], rkf[:]))
                    own(nc.vector.tensor_scalar(ra[:], ri[:], P - 1, 9, ALU.bitwise_and, ALU.logical_shift_left))
                    own(nc.vector.tensor_scalar(rb[:], ri[:], 7, None, ALU.logical_shift_right))
                    own(nc.vector.tensor_tensor(kf[:], ra[:], rb[:], ALU.add))
                    own(nc.vector.scalar_tensor_tensor(out=kf[:], in0=kf[:], scalar=1.0, in1=const("expert_row"),
                                                       op0=ALU.add, op1=ALU.add))
                    own(nc.vector.tensor_tensor(key[:], kf[:], mask[:], ALU.mult))
                    dve.sem_inc(wait_carrier, 1)
                    own(nc.vector.max(top[:], key[:]))
                    dve.wait_ge(ev["stored"], last)
                    own(nc.vector.tensor_scalar(idx[:], top[:, 0:TOPK], 1.0, None, ALU.subtract))
                    dve.wait_ge(ev["W"], now)
                    for c in range(TOPK):
                        own(nc.vector.scalar_tensor_tensor(out=pick[:], in0=key[:], scalar=top[:, c:c + 1], in1=W[:],
                                                           op0=ALU.is_equal, op1=ALU.mult, accum_out=wj[:, c:c + 1]))
                    own(nc.vector.tensor_copy(rec[:, :, 0], const("token")[:, bass.ds(i, 1)].to_broadcast([P, TOPK])))
                    nc.vector.tensor_copy(rec[:].bitcast(F32)[:, :, 1], wj[:]).then_inc(ev["rec"], 1)
                    dve.wait_ge(ev["bd"], now)
                    own(nc.vector.tensor_tensor(yi[:], acc[:].rearrange("p a n -> p (a n)"), g2[:], ALU.mult))
                    nc.vector.tensor_tensor(yi[:], yi[:], x2[:], ALU.add).then_inc(ev["yi"], 1)
                own.check()

            fin = Steps(dve, k.sem("fin"))
            fin(nc.vector.tensor_tensor(over[:], run[:].unsqueeze(2).to_broadcast([P, E, NT]),
                                        const("tile_from").unsqueeze(1).to_broadcast([P, E, NT]), ALU.is_gt))
            fin(nc.vector.tensor_reduce(tiles[:], over[:], AX_X, ALU.add))
            fin(nc.vector.tensor_reduce(groups[:], over[:].rearrange("p e (g t) -> p e g t", t=GT)[:, :, :, 0], AX_X, ALU.add))
            dve.sem_inc(table_ready, 1)
            dve.wait_ge(table_t, 1)
            fin(nc.vector.tensor_copy(gT[:], wt[0:E, 0:P]))
            fin(nc.vector.tensor_copy(tT[:], wt[0:E, P:2 * P]))
            dve.sem_inc(table_ready, 1)
            dve.wait_ge(table_t, 2)
            fin(nc.vector.tensor_copy(cumg[:], sm[:, 0:E]))
            fin(nc.vector.tensor_copy(cumt[:], sm[:, E:2 * E]))
            number, expert = const("number"), col[:, 1:2]
            fin(nc.vector.tensor_scalar(sel[:], cumg[:], number, None, ALU.is_le))
            fin(nc.vector.tensor_reduce(expert, sel[:], AX_X, ALU.add))
            fin(nc.vector.tensor_scalar(sel[:], const("expert"), expert, None, ALU.is_equal))
            fin(nc.vector.tensor_tensor(cumg[:], cumg[:], groups[:], ALU.subtract))
            for c, src in ((2, cumg), (3, tiles), (4, cumt)):
                fin(nc.vector.tensor_tensor(pick[:], sel[:], src[:], ALU.mult))
                fin(nc.vector.tensor_reduce(col[:, c:c + 1], pick[:], AX_X, ALU.add))
            fin(nc.vector.tensor_tensor(col[:, 5:6], number, col[:, 2:3], ALU.subtract))
            fin(nc.vector.tensor_scalar(col[:, 5:6], col[:, 5:6], float(GT), None, ALU.mult))
            fin(nc.vector.tensor_tensor(col[:, 6:7], col[:, 3:4], col[:, 5:6], ALU.subtract))
            fin(nc.vector.tensor_scalar(table[:, 1:2], col[:, 6:7], float(GT), 0.0, ALU.min, ALU.max))
            fin(nc.vector.tensor_scalar(col[:, 7:8], table[:, 1:2], 0.0, None, ALU.is_gt))
            fin(nc.vector.tensor_tensor(table[:, 0:1], expert, col[:, 7:8], ALU.mult))
            fin(nc.vector.tensor_tensor(col[:, 4:5], col[:, 4:5], col[:, 5:6], ALU.add))
            fin(nc.vector.tensor_tensor(table[:, 2:3], col[:, 4:5], col[:, 7:8], ALU.mult))
            fin(nc.vector.scalar_tensor_tensor(out=col[:, 6:7], in0=expert, scalar=float(NT), in1=col[:, 5:6],
                                               op0=ALU.mult, op1=ALU.add))
            fin(nc.vector.tensor_tensor(table[:, 3:4], col[:, 6:7], col[:, 7:8], ALU.mult))
            nc.vector.tensor_copy(table_i[:], table[:]).then_inc(table_step, 1)

        @block.tensor
        def _(pe):
            ident = const("ident")
            pe.wait_ge(wlo_done, 2)
            pe.wait_ge(setup_dma, 7 * 16)
            with pe.Fori(0, NT // 2) as j:
                for u in range(2):
                    i = j * 2 + u
                    now, last = i + 3, i + 2
                    pe.wait_ge(o_in[u], (j + 1) * 16)
                    pe.wait_ge(ev["olo"], i * 2 + 2)
                    for s in range(KD):
                        mm = nc.tensor.transpose(tp[:, s], o[:, u, s * P:(s + 1) * P], ident)
                    mm.then_inc(ev["t1"], 1)
                    pe.wait_ge(ev["olo"], i * 2 + 4)
                    pe.wait_ge(ev["yi"], last)
                    for c in range(2):
                        for s in range(KD):
                            mm = split_product(nc, acc[:, c], ohi[:, s], olo[:, s], whi[:, c, s], wlo[:, c, s],
                                               s == 0, s == KD - 1)
                    mm.then_inc(ev["mm"], 1)
                    pe.wait_ge(ev["h2"], now)
                    pe.wait_ge(ev["h2t"], last)
                    for s in range(KD):
                        mm = nc.tensor.transpose(tq[:, s], h2[:, s * P:(s + 1) * P], ident)
                    mm.then_inc(ev["t2"], 1)
                    pe.wait_ge(ev["h2t"], now)
                    pe.wait_ge(ev["rec"], last)
                    for s in range(KD):
                        mm = nc.tensor.matmul(sm[:, 0:E], h2T[:, s], wr[:, s], start=(s == 0), stop=(s == KD - 1))
                    mm.then_inc(ev["lg"], 1)
                    pe.wait_ge(ev["mask"], now)
                    nc.tensor.matmul(sm[:, E:2 * E], const("before"), mask[:], start=True, stop=True)
                    nc.tensor.matmul(sm[:, 2 * E:3 * E], const("ones"), mask[:], start=True, stop=True).then_inc(ev["rk"], 1)
                    pe.wait_ge(ev["W"], now)
                    pe.wait_ge(ev["wtc"], last)
                    nc.tensor.transpose(wt[0:E, 0:P], W[:], ident).then_inc(ev["wt"], 1)
                    pe.wait_ge(ev["wtc"], now)
                    pe.wait_ge(ev["x2"], now)
                    for c in range(2):
                        mm = nc.tensor.matmul(acc[:, c], wT[:], bd[:, c * N:(c + 1) * N], start=True, stop=True)
                    mm.then_inc(ev["bd"], 1)
            pe.wait_ge(table_ready, 1)
            nc.tensor.transpose(wt[0:E, 0:P], groups[:], ident)
            nc.tensor.transpose(wt[0:E, P:2 * P], tiles[:], ident).then_inc(table_t, 1)
            pe.wait_ge(table_ready, 2)
            nc.tensor.matmul(sm[:, 0:E], gT[:], const("causal")[0:E, 0:E], start=True, stop=True)
            nc.tensor.matmul(sm[:, E:2 * E], tT[:], const("before")[0:E, 0:E], start=True, stop=True).then_inc(table_t, 1)


def phase_experts(nc, k, A, keep):
    const = keep["const"]
    NCH, NGU, H = 6, 4, N // 2
    RAW = 3
    raw = k.sb("w_raw", [P, RAW, KD, H])
    whi, wlo = (k.sb(n, [P, 2, KD, N], F32R) for n in ("w_hi", "w_lo"))
    bias = k.sb("bias", [P, 2, D])
    g2 = k.sb("g2", [P, D])
    xs = k.sb("rows", [P, GT, D])
    xhi, xlo = (k.sb(n, [P, GT, KD, P], F32R) for n in ("x_hi", "x_lo"))
    ahi, alo = (k.sb(n, [P, GT, KD, P], F32R) for n in ("a_hi", "a_lo"))
    gu = k.sb("gate_up", [P, 2, N])
    sg = k.sb("sigmoid", [P, 2, H])
    act_row = k.sb("act_row", [P, GT, H])
    weighted = k.sb("weighted", [P, GT, N])
    rec_next, rec_now = k.sb("rec_next", [P, GT, 2], I32), k.sb("rec_now", [P, GT, 2], I32)
    table = k.sb("table", [1, 4 * P], I32)
    acc = k.ps("acc", [P, 5, N])
    tx = k.ps("tx", [P, 2, 4, P])
    ta = k.ps("ta", [P, 2, P])
    (table_in, g2_in, bias_in, hi_done, lo_done, mm_done, read_done, sg_in, sg_done, act_done, ta_done, ahi_done,
     alo_done, tx_done, xhi_done, xlo_done, weighted_done, rec_next_in, rec_now_in, rec_used, rows_in, y_out, y_added,
     dve_step, wait_carrier) = k.sems(
         "table_in g2_in bias_in hi_done lo_done mm_done read_done sg_in sg_done act_done ta_done ahi_done "
         "alo_done tx_done xhi_done xlo_done weighted_done rec_next_in rec_now_in rec_used rows_in y_out y_added "
         "dve_step wait_carrier")
    raw_in = [k.sem(f"raw_in{s}") for s in range(RAW)]
    gu_w = A["w_gu"].rearrange("o e (s p) n -> p (o e) s n", p=P)
    dn_w = A["w_down"].rearrange("o e (s p) n -> p (o e) s n", p=P)
    gu_b = A["b_gu"].rearrange("o e n -> (o e) n")
    places = keep["places"].rearrange("(p q) c -> p q c", p=P)

    def bank(c, t):
        return c % 2 if t == 0 else t + 1

    def field(eng, g, f, most):
        return eng.value_load(table[0:1, bass.ds(g * 4 + f, 1)], min_val=0, max_val=most)

    EXPERT, TILES, BEFORE, PLACE = range(4)

    class Group:

        def __init__(self, eng, g):
            self.T = field(eng, g, TILES, GT)
            self.before = field(eng, g, BEFORE, NG * GT)
            self.g = g

        def chunk_tile(self, c, t):
            return self.before * NCH + self.T * c + (t + 2)

        def chunks_before(self, c):
            return self.before * NCH + self.T * c + 1

        def gu_tile(self, c, t):
            return self.before * NGU + self.T * c + (t + 2)

        def down_tile(self, c, t):
            return self.before * 2 + self.T * (c - NGU) + (t + 2)

        def halves(self, n):
            return self.g * (2 * NCH) + (n + RAW)

    with nc.Block() as block:

        @block.sync
        def _(sp):
            sp.dma_start(table[:], keep["groups"].rearrange("g f -> (g f)").unsqueeze(0)).then_inc(table_in, 16)
            sp.dma_start(g2[:], keep["g2"]).then_inc(g2_in, 16)
            sp.sem_inc(lo_done, RAW)
            sp.sem_inc(read_done, 1)
            sp.sem_inc(mm_done, 1)
            sp.wait_ge(table_in, 16)
            with sp.Fori(0, NG) as g:
                G = Group(sp, g)
                expert = field(sp, g, EXPERT, E - 1)
                with sp.If(G.T > 0):
                    for n in range(2 * NCH):
                        c, half = n // 2, n % 2
                        if n == 0:
                            sp.wait_ge(act_done, G.before * NGU + 1)
                            sp.dma_start(bias[:].rearrange("p a n -> p (a n)"),
                                         gu_b[bass.ds(expert, 1), :].rearrange("o n -> (o n)").partition_broadcast(P)
                                         ).then_inc(bias_in, 16)
                        sp.wait_ge(lo_done, G.halves(n - RAW + 1))
                        w, col = (gu_w, half * D + c * H) if c < NGU else (dn_w, (c - NGU) * N + half * H)
                        sp.dma_start(raw[:, n % RAW], w[:, bass.ds(expert, 1), :, col:col + H]
                                     ).then_inc(raw_in[n % RAW], 16)
                    sp.nop()

        @block.gpsimd
        def _(pool):
            pool.wait_ge(table_in, 16)
            for s in (ta_done, alo_done, weighted_done, y_added, act_done, rec_used):
                pool.sem_inc(s, 1)
            pool.sem_inc(tx_done, 1)

            def fetch_rows(g, T, place, before):
                pool.dma_start(rec_next[:], places[:, bass.ds(place, GT), :]).then_inc(rec_next_in, 16)
                pool.wait_ge(rec_next_in, (g + 1) * 16)
                pool.sem_inc(wait_carrier, 1)
                for t in range(GT):
                    with pool.If(T > t):
                        pool.indirect_dma_start(out=xs[:, t], out_offset=None, in_=keep["h2"],
                                                in_offset=bass.IndirectOffsetOnAxis(ap=rec_next[:, t, 0:1], axis=0)
                                                ).then_inc(rows_in, 16)
                pool.wait_ge(rows_in, (before + T) * 16)
                pool.sem_inc(wait_carrier, 1)

            T0 = field(pool, 0, TILES, GT)
            fetch_rows(0, T0, 0, 0)
            with pool.Fori(0, NG) as g:
                G = Group(pool, g)
                place = field(pool, g, PLACE, PLACES - GT)
                nT, nbefore, nplace = field(pool, g + 1, TILES, GT), field(pool, g + 1, BEFORE, NG * GT), field(pool, g + 1, PLACE, PLACES - GT)
                with pool.If(G.T > 0):
                    pool.wait_ge(rec_used, g + 1)
                    pool.sem_inc(wait_carrier, 1)
                    pool.dma_start(rec_now[:], places[:, bass.ds(place, GT), :]).then_inc(rec_now_in, 16)
                    pool.wait_ge(rec_now_in, (g + 1) * 16)
                    pool.sem_inc(wait_carrier, 1)
                    with pool.If(nT > 0):
                        pool.wait_ge(tx_done, G.before + G.T + 1)
                        pool.sem_inc(wait_carrier, 1)
                        fetch_rows(g + 1, nT, nplace, nbefore)
                    for c in (NGU, NGU + 1):
                        for t in range(GT):
                            with pool.If(G.T > t):
                                pool.wait_ge(weighted_done, G.down_tile(c, t))
                                pool.sem_inc(wait_carrier, 1)
                                pool.indirect_dma_start(
                                    out=keep["y"][c - NGU],
                                    out_offset=bass.IndirectOffsetOnAxis(ap=rec_now[:, t, 0:1], axis=0),
                                    in_=weighted[:, t], in_offset=None, compute_op=ALU.add).then_inc(y_out, 16)
                                pool.wait_ge(y_out, (G.down_tile(c, t) - 1) * 16)
                                pool.sem_inc(y_added, 1)
                    pool.sem_inc(wait_carrier, 1)

        @block.scalar
        def _(act):
            act.wait_ge(table_in, 16)

            def weights_hi(g, n, freed):
                act.wait_ge(raw_in[n % RAW], (g * (2 * NCH // RAW) + n // RAW + 1) * 16)
                act.wait_ge(mm_done, freed)
                c, half = n // 2, n % 2
                nc.scalar.copy(whi[:, c % 2, :, half * H:(half + 1) * H], raw[:, n % RAW]).then_inc(hi_done, 1)

            def rows_hi(base, t):
                act.wait_ge(tx_done, base + (t + 2))
                for b in range(2):
                    nc.scalar.copy(xhi[:, t, 4 * b:4 * b + 4], tx[:, b]).then_inc(xhi_done, 1)

            for half in range(2):
                weights_hi(0, half, 1)
            T0 = field(act, 0, TILES, GT)
            for t in range(GT):
                with act.If(T0 > t):
                    rows_hi(0, t)
            with act.Fori(0, NG) as g:
                G = Group(act, g)
                nT = field(act, g + 1, TILES, GT)
                with act.If(G.T > 0):
                    for c in range(NCH):
                        if c < NCH - 1:
                            for half in range(2):
                                weights_hi(g, 2 * (c + 1) + half, G.chunks_before(c))
                        else:
                            with act.If(nT > 0):
                                for half in range(2):
                                    weights_hi(g + 1, half, G.chunks_before(c))
                        for t in range(GT):
                            with act.If(G.T > t):
                                if 1 <= c <= NGU:
                                    act.wait_ge(ta_done, G.gu_tile(c - 1, t))
                                    nc.scalar.copy(ahi[:, t, 2 * c - 2:2 * c], ta[:]).then_inc(ahi_done, 1)
                                if c < NGU:
                                    act.wait_ge(sg_in, G.gu_tile(c, t) - 1)
                                    nc.scalar.activation(sg[:, t % 2], gu[:, t % 2, 0:H], ACT.Sigmoid,
                                                         scale=SIG).then_inc(sg_done, 1)
                        if c >= NGU:
                            for t in (0, 1) if c == NGU else (2, 3):
                                with act.If(nT > t):
                                    rows_hi(G.before + G.T, t)
                    act.nop()

        @block.vector
        def _(dve):
            dve.wait_ge(table_in, 16)
            dve.wait_ge(g2_in, 16)

            def weights_lo(g, n, freed):
                dve.wait_ge(hi_done, g * (2 * NCH) + n + 1)
                dve.wait_ge(mm_done, freed)
                c, half = n // 2, n % 2
                cols = slice(half * H, (half + 1) * H)
                nc.vector.tensor_tensor(wlo[:, c % 2, :, cols], raw[:, n % RAW], whi[:, c % 2, :, cols],
                                        ALU.subtract).then_inc(lo_done, 1)

            def rows_lo(base, t):
                for b in range(2):
                    dve.wait_ge(xhi_done, base * 2 + (2 * t + b + 1))
                    nc.vector.tensor_tensor(xlo[:, t, 4 * b:4 * b + 4], tx[:, b], xhi[:, t, 4 * b:4 * b + 4],
                                            ALU.subtract).then_inc(xlo_done, 1)

            def swiglu(G, g, c, t):
                if t == 0 and c == 0:
                    dve.wait_ge(bias_in, (g + 1) * 16)
                u = t % 2
                dve.wait_ge(act_done, G.gu_tile(c, t) - 1)
                dve.wait_ge(mm_done, G.chunk_tile(c, t))
                nc.vector.tensor_tensor(gu[:, u].rearrange("p (a n) -> p a n", a=2),
                                        acc[:, bank(c, t)].rearrange("p (a n) -> p a n", a=2),
                                        bias[:, :, c * H:(c + 1) * H], ALU.add).then_inc(read_done, 1)
                dve.wait_ge(read_done, G.chunk_tile(c, t))
                nc.vector.tensor_scalar(gu[:, u, 0:H], gu[:, u, 0:H], LIMIT, None, ALU.min).then_inc(sg_in, 1)
                nc.vector.tensor_scalar(gu[:, u, H:N], gu[:, u, H:N], LIMIT, -LIMIT, ALU.min, ALU.max).then_inc(dve_step, 1)
                dve.wait_ge(sg_done, G.gu_tile(c, t) - 1)
                nc.vector.tensor_tensor(gu[:, u, 0:H], gu[:, u, 0:H], sg[:, u], ALU.mult).then_inc(dve_step, 1)
                dve.wait_ge(dve_step, (G.gu_tile(c, t) - 1) * 2)
                nc.vector.scalar_tensor_tensor(out=act_row[:, t], in0=gu[:, u, H:N], scalar=1.0, in1=gu[:, u, 0:H],
                                               op0=ALU.add, op1=ALU.mult).then_inc(act_done, 1)

            for half in range(2):
                weights_lo(0, half, 1)
            T0 = field(dve, 0, TILES, GT)
            for t in range(GT):
                with dve.If(T0 > t):
                    rows_lo(0, t)
            with dve.Fori(0, NG) as g:
                G = Group(dve, g)
                nT = field(dve, g + 1, TILES, GT)
                with dve.If(G.T > 0):
                    for c in range(NCH):
                        if c < NCH - 1:
                            for half in range(2):
                                weights_lo(g, 2 * (c + 1) + half, G.chunks_before(c))
                        else:
                            with dve.If(nT > 0):
                                for half in range(2):
                                    weights_lo(g + 1, half, G.chunks_before(c))
                        if c == NGU:
                            dve.wait_ge(rec_now_in, (g + 1) * 16)
                            dve.sem_inc(wait_carrier, 1)
                        for t in range(GT):
                            with dve.If(G.T > t):
                                if 1 <= c <= NGU:
                                    dve.wait_ge(ahi_done, G.gu_tile(c - 1, t) - 1)
                                    nc.vector.tensor_tensor(alo[:, t, 2 * c - 2:2 * c], ta[:], ahi[:, t, 2 * c - 2:2 * c],
                                                            ALU.subtract).then_inc(alo_done, 1)
                                if c < NGU:
                                    swiglu(G, g, c, t)
                                else:
                                    dve.wait_ge(mm_done, G.chunk_tile(c, t))
                                    dve.wait_ge(y_added, G.before * 2 + (t + 2 if c > NGU else 1))
                                    cols = slice((c - NGU) * N, (c - NGU + 1) * N)
                                    nc.vector.scalar_tensor_tensor(
                                        out=weighted[:, t], in0=acc[:, bank(c, t)], scalar=rec_now[:].bitcast(F32)[:, t, 1:2],
                                        in1=g2[:, cols], op0=ALU.mult, op1=ALU.mult).then_inc(weighted_done, 1)
                                    dve.wait_ge(weighted_done, G.down_tile(c, t))
                                    dve.sem_inc(read_done, 1)
                        if c >= NGU:
                            for t in (0, 1) if c == NGU else (2, 3):
                                with dve.If(nT > t):
                                    rows_lo(G.before + G.T, t)
                    dve.sem_inc(rec_used, 1)

        @block.tensor
        def _(pe):
            ident = const("ident")
            pe.wait_ge(table_in, 16)

            def rows(t):
                for s in range(KD):
                    mm = nc.tensor.transpose(tx[:, s // 4, s % 4], xs[:, t, s * P:(s + 1) * P], ident)
                mm.then_inc(tx_done, 1)

            def activations(G, c, t):
                pe.wait_ge(act_done, G.gu_tile(c, t))
                pe.wait_ge(alo_done, G.gu_tile(c, t) - 1)
                for s in range(2):
                    mm = nc.tensor.transpose(ta[:, s], act_row[:, t, s * P:(s + 1) * P], ident)
                mm.then_inc(ta_done, 1)

            T0 = field(pe, 0, TILES, GT)
            pe.sem_inc(xlo_done, 2)
            for t in range(GT):
                with pe.If(T0 > t):
                    if t == 0:
                        pe.wait_ge(rows_in, T0 * 16)
                    pe.wait_ge(xlo_done, 2 * t + 2)
                    rows(t)
            with pe.Fori(0, NG) as g:
                G = Group(pe, g)
                nT = field(pe, g + 1, TILES, GT)
                with pe.If(G.T > 0):
                    for c in range(NCH):
                        pe.wait_ge(lo_done, G.halves(2 * c + 2))
                        if c == 0:
                            pe.wait_ge(xlo_done, (G.before + G.T) * 2 + 2)
                        for t in range(GT):
                            with pe.If(G.T > t):
                                if c == 0:
                                    pe.wait_ge(read_done, G.chunks_before(0))
                                elif t == 0:
                                    if c >= 2:
                                        pe.wait_ge(read_done, G.chunk_tile(c - 2, 0))
                                else:
                                    pe.wait_ge(read_done, G.chunk_tile(c - 1, t))
                                a_hi, a_lo = (xhi, xlo) if c < NGU else (ahi, alo)
                                for s in range(KD):
                                    if c == NGU and s == 3:
                                        activations(G, NGU - 1, t)
                                    if c == NGU and s == 2 * (NGU - 1):
                                        pe.wait_ge(alo_done, G.gu_tile(NGU - 1, t))
                                    mm = split_product(nc, acc[:, bank(c, t)], a_hi[:, t, s], a_lo[:, t, s],
                                                       whi[:, c % 2, s], wlo[:, c % 2, s], s == 0, s == KD - 1)
                                mm.then_inc(mm_done, 1)
                                if 1 <= c < NGU:
                                    activations(G, c - 1, t)
                        if c >= NGU:
                            for t in (0, 1) if c == NGU else (2, 3):
                                with pe.If(nT > t):
                                    if t == 0:
                                        pe.wait_ge(rows_in, (G.before + G.T + nT) * 16)
                                    pe.wait_ge(xlo_done, (G.before + G.T) * 2 + (2 * t + 2))
                                    rows(t)
                    pe.nop()


def phase_finish(nc, k, A, keep):
    const = keep["const"]
    SLOTS = 4
    y, z = k.sb("y", [P, SLOTS, D]), k.sb("z", [P, SLOTS, D])
    squares = k.sb("squares", [P, D], mybir.dt.bfloat16)
    nf = k.sb("norm_f", [P, D])
    ssq, rms, rinv = (k.sb(n, [P, NT]) for n in ("ssq", "rms", "rinv"))
    nf_in, sq_done, rms_done, inv_done, done = k.sems("nf_in sq_done rms_done inv_done done")
    y_in = [k.sem(f"y_in{s}") for s in range(SLOTS)]
    out_done = [k.sem(f"out_done{s}") for s in range(SLOTS)]
    y_t = [a.rearrange("(t p) n -> p t n", p=P) for a in keep["y"]]
    out_t = keep["out"].rearrange("o (t p) d -> p (o t) d", p=P)
    with nc.Block() as block:

        @block.sync
        def _(sp):
            sp.dma_start(nf[:], A["norm_f"].partition_broadcast(P)).then_inc(nf_in, 16)
            for i in range(NT):
                if i >= SLOTS:
                    sp.wait_ge(done, i - SLOTS + 1)
                for half in range(2):
                    sp.dma_start(y[:, i % SLOTS, half * N:(half + 1) * N], y_t[half][:, i]).then_inc(y_in[i % SLOTS], 16)

        @block.scalar
        def _(act):
            for i in range(NT):
                act.wait_ge(y_in[i % SLOTS], 32 * (i // SLOTS + 1))
                nc.scalar.activation(squares[:], y[:, i % SLOTS], ACT.Square, accum_out=ssq[:, i:i + 1]).then_inc(sq_done, 1)
                act.wait_ge(sq_done, i + 1)
                nc.scalar.activation(rms[:, i:i + 1], ssq[:, i:i + 1], ACT.Sqrt, scale=1.0 / D,
                                     bias=const("eps")).then_inc(rms_done, 1)

        @block.vector
        def _(dve):
            dve.wait_ge(nf_in, 16)
            for i in range(NT):
                s = i % SLOTS
                dve.wait_ge(rms_done, i + 1)
                nc.vector.reciprocal(rinv[:, i:i + 1], rms[:, i:i + 1]).then_inc(inv_done, 1)
                dve.wait_ge(inv_done, i + 1)
                if i >= SLOTS:
                    dve.wait_ge(out_done[s], 16 * (i // SLOTS))
                nc.vector.scalar_tensor_tensor(out=z[:, s], in0=y[:, s], scalar=rinv[:, i:i + 1], in1=nf[:],
                                               op0=ALU.mult, op1=ALU.mult).then_inc(done, 1)

        @block.gpsimd
        def _(pool):
            for i in range(NT):
                pool.wait_ge(done, i + 1)
                pool.dma_start(out_t[:, i], z[:, i % SLOTS]).then_inc(out_done[i % SLOTS], 16)
            for s in range(SLOTS):
                pool.wait_ge(out_done[s], 16 * (NT // SLOTS))


def program(nc, A, out):
    def dram(name, shape, dt=F32):
        return nc.dram_tensor(name, shape, dt, kind="Internal").ap()

    with ExitStack() as ctx:
        k = Kit(nc, ctx, "keep")
        keep = {n: dram(n + "_rep", (P, D)) for n in ("g1", "sh2", "A2", "g2")}
        keep["proj"] = dram("proj", (S, PROJ))
        keep["o"] = dram("mixed", (S + P, D))
        keep["h2"] = dram("h2_rows", (ROWS, D))
        keep["y"] = [dram(f"y_rows{half}", (ROWS, N)) for half in range(2)]
        keep["places"] = dram("places", (P * PLACES, 2), I32)
        keep["groups"] = dram("groups", (P, 4), I32)
        keep["const_all"] = k.sb("const", [P, sum(w for _, w in CONST_AT.values())])
        keep["const"] = lambda name: keep["const_all"][:, CONST_AT[name][0]:sum(CONST_AT[name])]
        keep["out"] = out

        def run(phase):
            with ExitStack() as c:
                k = Kit(nc, c, phase.__name__[6:9])
                phase(nc, k, A, keep)
                k.clear_sems()

        with ExitStack() as mixing:
            keep["glr_t"] = Kit(nc, mixing, "mixing").sb("glr_t", [RANK + 1, S])
            with ExitStack() as early:
                ke = Kit(nc, early, "early")
                keep["A1"], keep["sh1"] = ke.sb("A1", [P, D]), ke.sb("sh1", [P, D])
                run(phase_modulation)
                run(phase_projection)
            run(phase_mixer)
        run(phase_routing)
        run(phase_experts)
        run(phase_finish)


_INS = ['x', 'c', 'positions', 'w_ada', 'b_ada', 'norm1', 'w_in', 'w_gk2', 'b_gk', 'gla_onorm', 'ret_onorm', 'w_out',
        'norm2', 'w_router', 'b_router', 'w_gu', 'b_gu', 'w_down', 'b_down', 'norm_f']


def kernel(**inputs):
    import concourse.bacc as bacc
    from concourse.bass_utils import run_bass_kernel_spmd

    nc = bacc.Bacc("TRN2", target_bir_lowering=False, num_devices=1)
    arrays = {n: np.ascontiguousarray(inputs[n]) for n in _INS}
    arrays["const"] = constants()[0]
    A = {n: nc.dram_tensor("in_" + n, a.shape, mybir.dt.from_np(a.dtype), kind="ExternalInput").ap()
         for n, a in arrays.items()}
    out = nc.dram_tensor("out", (1, S, D), F32, kind="ExternalOutput").ap()
    program(nc, A, out)
    r = run_bass_kernel_spmd(nc, [{"in_" + n: a for n, a in arrays.items()}], core_ids=[0])
    return r.results[0]["out"]
```

```python
from contextlib import ExitStack

import numpy as np
import concourse.bass as bass
from concourse import mybir

P = 128
F32 = mybir.dt.float32
F32R = mybir.dt.float32r
I32 = mybir.dt.int32
ALU = mybir.AluOpType
ACT = mybir.ActivationFunctionType
AX_X = mybir.AxisListType.X

D = 1024
S = 2048
NT = S // P
KD = D // P
N = 512
EPS = 1e-6

GH, GDK, GDV, RANK = 4, 64, 128, 16
RH, RDK = 4, 128
GATE_NORM = 16.0
SUB = 32
ROPE_BASE = 10000.0
PROJ = 3584
NC_IN = PROJ // N
GLR = 1536
C_GQ, C_GK, C_GV, C_GG = 0, 256, 512, 1024
C_RQ, C_RK, C_RV, C_RG = 1536, 2048, 2560, 3072

E = 32
TOPK = 4
GT = 4
ROWS = S + P
PLACES = E * NT
NG = (S * TOPK - E) // (GT * P) + E
LIMIT = 7.0
SIG = 1.702



def w_in_column(chunk):
    return chunk * N + (RANK if chunk * N >= GLR else 0)


class Kit:

    def __init__(self, nc, ctx, phase):
        self.nc, self.ctx, self.phase, self.signals = nc, ctx, phase, []

    def sb(self, name, shape, dt=F32):
        return self.ctx.enter_context(self.nc.sbuf_tensor(f"{self.phase}_{name}", shape, dt))

    def ps(self, name, shape):
        return self.ctx.enter_context(self.nc.psum_tensor(f"{self.phase}_bank_{name}", shape, F32))

    def sem(self, name):
        self.signals.append(self.nc.alloc_semaphore(f"{self.phase}_{name}"))
        return self.signals[-1]

    def sems(self, names):
        return [self.sem(n) for n in names.split()]

    def clear_sems(self):
        self.nc.clear_and_free_semaphores(self.signals)
        self.nc.all_engine_barrier()


class Steps:

    def __init__(self, eng, sem, per_turn=0):
        self.eng, self.sem, self.per_turn, self.base, self.n = eng, sem, per_turn, 0, 0

    def turn(self, i):
        self.base, self.n = i * self.per_turn, 0

    def __call__(self, ins):
        ins.then_inc(self.sem, 1)
        self.n += 1
        self.eng.wait_ge(self.sem, self.base + self.n)

    def check(self):
        assert self.n == self.per_turn, (self.n, self.per_turn)


def split_product(nc, out, act_hi, act_lo, w_hi, w_lo, first, last):
    nc.tensor.matmul(out, act_hi, w_hi, start=first, stop=False)
    nc.tensor.matmul(out, act_hi, w_lo, start=False, stop=False)
    return nc.tensor.matmul(out, act_lo, w_hi, start=False, stop=last)


def load_ln_exp(nc):
    nc.scalar.add_instruction(mybir.InstLoadActFuncSet(act_func_set_id=6, name=nc.get_next_instruction_name(),
                                                       engine=mybir.EngineType.Activation))


def row(ap, n=P):
    return ap.rearrange("o n -> (o n)").partition_broadcast(n)


def constants():
    p = np.arange(P, dtype=np.float64)
    s, t = p[:, None], p[None, :]
    parts = {}
    parts["ident"] = (s == t).astype(np.float64)
    parts["ones"] = np.ones((P, P))
    parts["before"] = (s < t).astype(np.float64)
    parts["causal"] = (s <= t).astype(np.float64)
    parts["sum_to"] = (s <= t) / GATE_NORM
    parts["sum_after"] = (s > t) / GATE_NORM
    log_gamma = np.log(1.0 - 2.0 ** (-5.0 - np.arange(RH)))
    rel = (t - s)[:, None, :] * log_gamma[None, :, None]
    parts["decay"] = (np.where((t >= s)[:, None, :], np.exp(np.minimum(rel, 0.0)), 0.0) * RDK ** -0.5).reshape(P, -1)
    parts["xi"] = np.broadcast_to(np.exp((p + 1)[None, None, :] * log_gamma[None, :, None]), (P, RH, P)).reshape(P, -1)
    parts["zeta"] = np.exp((P - 1 - p)[:, None] * log_gamma[None, :]) * RDK ** -0.5
    half = RDK // 2
    inv = (np.float32(ROPE_BASE) ** (-np.arange(half, dtype=np.float32) / np.float32(half))).astype(np.float32)
    parts["inv_freq"] = np.broadcast_to(inv, (P, half))
    parts["expert"] = np.broadcast_to(np.arange(E), (P, E))
    parts["expert_row"] = np.broadcast_to(np.arange(E) * NT, (P, E))
    parts["tile_from"] = np.broadcast_to(np.arange(NT) * P, (P, NT))
    parts["number"] = p[:, None]
    parts["eps"] = np.full((P, 1), EPS)
    parts["token"] = p[:, None] + P * np.arange(NT)[None, :]
    at, n = {}, 0
    for name, a in parts.items():
        at[name] = (n, a.shape[1])
        n += a.shape[1]
    return np.concatenate([np.asarray(a, np.float32) for a in parts.values()], axis=1), at


CONST_AT = constants()[1]
GAMMA_TILE = [float(np.exp(P * np.log(1.0 - 2.0 ** (-5.0 - h)))) for h in range(RH)]


def phase_modulation(nc, k, A, keep):
    W_SLOTS = 3
    n_chunk = 6 * D // N
    c_col, neg, den, silu = (k.sb(n, [P, KD]) for n in ("c_col", "exp_neg_c", "den", "silu"))
    silu_rep = k.sb("silu_rep", [P, KD, P])
    w = k.sb("w_ada", [P, W_SLOTS, KD, N])
    b = k.sb("b_ada", [P, 6 * D])
    mod = k.sb("mod", [P, 6 * D])
    norms = k.sb("norms", [P, 2, D])
    zero = k.sb("zero", [P, D])
    acc = k.ps("acc", [P, 2, N])
    c_in, b_in, mod_out, const_in, exp_done, dve_step = k.sems("c_in b_in mod_out const_in exp_done dve_step")
    silu_ready, acc_full, acc_read, mod_ready = k.sems("silu_ready acc_full acc_read mod_ready")
    zero_set, zero_out = k.sems("zero_set zero_out")
    w_in = [k.sem(f"w_in{s}") for s in range(W_SLOTS)]
    w_dram = A["w_ada"].rearrange("o (s p) n -> p (o s) n", p=P)
    ones = keep["const"]("ones")
    with nc.Block() as block:

        @block.sync
        def _(sp):
            sp.dma_start(c_col[:], A["c"].rearrange("o (s p) -> p (o s)", p=P),
                         allow_slow_non_contiguous=True).then_inc(c_in, 16)
            sp.dma_start(keep["const_all"][:], A["const"]).then_inc(const_in, 16)
            for n in range(n_chunk):
                if n >= W_SLOTS:
                    sp.wait_ge(acc_full, n - W_SLOTS + 1)
                sp.dma_start(w[:, n % W_SLOTS], w_dram[:, :, n * N:(n + 1) * N]).then_inc(w_in[n % W_SLOTS], 16)
            sp.wait_ge(mod_ready, 1)
            for j, name in ((2, "g1"), (3, "sh2"), (4, "A2"), (5, "g2")):
                sp.dma_start(keep[name], mod[:, j * D:(j + 1) * D]).then_inc(mod_out, 16)
            sp.wait_ge(mod_out, 64)

        @block.scalar
        def _(act):
            act.dma_start(b[:], row(A["b_ada"])).then_inc(b_in, 16)
            act.dma_start(norms[:, 0], row(A["norm1"])).then_inc(b_in, 16)
            act.dma_start(norms[:, 1], row(A["norm2"])).then_inc(b_in, 16)
            act.wait_ge(c_in, 16)
            nc.scalar.activation(neg[:], c_col[:], ACT.Exp, scale=-1.0).then_inc(exp_done, 1)

        @block.gpsimd
        def _(pool):
            nc.gpsimd.memset(keep["glr_t"][:], 1.0).then_inc(zero_set, 1)
            nc.gpsimd.memset(zero[:], 0.0).then_inc(zero_set, 1)
            pool.wait_ge(zero_set, 2)
            pool.dma_start(keep["h2"][S:ROWS, :], zero[:]).then_inc(zero_out, 16)
            for half in range(2):
                pool.dma_start(keep["y"][half][S:ROWS, :], zero[:, 0:N]).then_inc(zero_out, 16)
            pool.wait_ge(zero_out, 48)

        @block.vector
        def _(dve):
            step = Steps(dve, dve_step)
            dve.wait_ge(exp_done, 1)
            step(nc.vector.tensor_scalar(den[:], neg[:], 1.0, None, ALU.add))
            step(nc.vector.reciprocal(neg[:], den[:]))
            step(nc.vector.tensor_tensor(silu[:], c_col[:], neg[:], ALU.mult))
            dve.wait_ge(const_in, 16)
            for s in range(KD):
                nc.vector.tensor_scalar(silu_rep[:, s], ones, silu[:, s:s + 1], None, ALU.mult).then_inc(silu_ready, 1)
            dve.wait_ge(b_in, 48)
            for n in range(n_chunk):
                dve.wait_ge(acc_full, n + 1)
                nc.vector.tensor_tensor(mod[:, n * N:(n + 1) * N], acc[:, n % 2], b[:, n * N:(n + 1) * N],
                                        ALU.add).then_inc(acc_read, 1)
            dve.wait_ge(acc_read, n_chunk)
            step(nc.vector.tensor_copy(keep["sh1"][:], mod[:, 0:D]))
            step(nc.vector.scalar_tensor_tensor(out=keep["A1"][:], in0=mod[:, D:2 * D], scalar=1.0, in1=norms[:, 0],
                                                op0=ALU.add, op1=ALU.mult))
            nc.vector.scalar_tensor_tensor(out=mod[:, 4 * D:5 * D], in0=mod[:, 4 * D:5 * D], scalar=1.0,
                                           in1=norms[:, 1], op0=ALU.add, op1=ALU.mult).then_inc(mod_ready, 1)

        @block.tensor
        def _(pe):
            pe.wait_ge(silu_ready, KD)
            for n in range(n_chunk):
                pe.wait_ge(w_in[n % W_SLOTS], 16 * (n // W_SLOTS + 1))
                if n >= 2:
                    pe.wait_ge(acc_read, n - 1)
                for s in range(KD):
                    mm = nc.tensor.matmul(acc[:, n % 2], silu_rep[:, s], w[:, n % W_SLOTS, s],
                                          start=(s == 0), stop=(s == KD - 1))
                mm.then_inc(acc_full, 1)


def phase_projection(nc, k, A, keep):
    HT = NT // 2
    raw = k.sb("w_raw", [P, 2, KD, N])
    whi, wlo = (k.sb(n, [P, 2, KD, N], F32R) for n in ("w_hi", "w_lo"))
    rraw = k.sb("rank_raw", [P, KD, RANK])
    rhi, rlo = (k.sb(n, [P, KD, P], F32R) for n in ("rank_hi", "rank_lo"))
    hhi, hlo = (k.sb(n, [P, KD, HT, P], F32R) for n in ("h_hi", "h_lo"))
    x = k.sb("x", [P, 2, D])
    squares = k.sb("squares", [P, D], mybir.dt.bfloat16)
    ssq, rs, rinv = (k.sb(n, [P, 2]) for n in ("ssq", "rms", "rinv"))
    sum_done, wait_carrier = k.sems("sum_done wait_carrier")
    stage = k.sb("stage", [P, 2, N])
    tp = k.ps("tp", [P, 2, KD, P])
    acc = k.ps("acc", [P, 2, N])
    racc = k.ps("racc", [P, N])
    sq_done, dve_step, h_ready, t_done, hi_done, lo_done = k.sems(
        "sq_done dve_step h_ready t_done hi_done lo_done")
    whi_done, wlo_done, mm_done, acc_read, r_done, r_read, rank_in, rank_set, rhi_done, rlo_done = k.sems(
        "whi_done wlo_done mm_done acc_read r_done r_read rank_in rank_set rhi_done rlo_done")
    x_in = [k.sem(f"x_in{s}") for s in range(2)]
    raw_in = [k.sem(f"raw_in{s}") for s in range(2)]
    out_done = [k.sem(f"out_done{s}") for s in range(2)]
    USES = [(NC_IN + 1) // 2, NC_IN // 2]
    x_t = A["x"].rearrange("o (t p) d -> p (o t) d", p=P)
    w_t = A["w_in"].rearrange("o (s p) n -> p (o s) n", p=P)
    proj_t = keep["proj"].rearrange("(t p) n -> p t n", p=P)

    with nc.Block() as block:

        @block.gpsimd
        def _(pool):
            nc.gpsimd.memset(rhi[:].bitcast(F32), 0.0).then_inc(rank_set, 1)
            nc.gpsimd.memset(rlo[:].bitcast(F32), 0.0).then_inc(rank_set, 1)
            pool.dma_start(rraw[:], w_t[:, :, GLR:GLR + RANK]).then_inc(rank_in, 16)
            pool.sem_inc(wlo_done, 1)
            pool.sem_inc(t_done, 2)
            with pool.Fori(0, 2) as half:

                def load_w(c):
                    pool.wait_ge(wlo_done, half * NC_IN + max(c, 1))
                    pool.sem_inc(wait_carrier, 1)
                    col = w_in_column(c)
                    pool.dma_start(raw[:, c % 2], w_t[:, :, col:col + N]).then_inc(raw_in[c % 2], 16)

                def load_x(i):
                    pool.wait_ge(t_done, half * HT + i + 1)
                    pool.sem_inc(wait_carrier, 1)
                    pool.dma_start(x[:, i % 2], x_t[:, bass.ds(half * HT + i, 1)]).then_inc(x_in[i % 2], 16)

                load_x(0)
                load_w(0)
                load_x(1)
                load_w(1)
                for i in range(2, HT):
                    load_x(i)
                for c in range(2, NC_IN):
                    load_w(c)

        @block.scalar
        def _(act):
            act.wait_ge(rank_in, 16)
            act.wait_ge(rank_set, 2)
            nc.scalar.copy(rhi[:, :, 0:RANK], rraw[:]).then_inc(rhi_done, 1)
            act.sem_inc(out_done[0], 16)
            act.sem_inc(out_done[1], 16)
            with act.Fori(0, 2) as half:

                def split_hi(c):
                    act.wait_ge(raw_in[c % 2], (half * USES[c % 2] + c // 2 + 1) * 16)
                    act.wait_ge(mm_done, half * NC_IN * HT + max(c - 1, 0) * HT + 1)
                    nc.scalar.copy(whi[:, c % 2], raw[:, c % 2]).then_inc(whi_done, 1)

                def square(i):
                    act.wait_ge(x_in[i % 2], (half * (HT // 2) + i // 2 + 1) * 16)
                    nc.scalar.activation(squares[:], x[:, i % 2], ACT.Square,
                                         accum_out=ssq[:, i % 2:i % 2 + 1]).then_inc(sum_done, 1)
                    act.wait_ge(sum_done, half * HT + i + 1)
                    nc.scalar.activation(rs[:, i % 2:i % 2 + 1], ssq[:, i % 2:i % 2 + 1], ACT.Sqrt, scale=1.0 / D,
                                         bias=keep["const"]("eps")).then_inc(sq_done, 1)

                def h_hi(i):
                    act.wait_ge(t_done, half * HT + i + 3)
                    for b in range(2):
                        nc.scalar.copy(hhi[:, 4 * b:4 * b + 4, i], tp[:, i % 2, 4 * b:4 * b + 4]).then_inc(hi_done, 1)

                def evacuate(c, i):
                    act.wait_ge(mm_done, (half * NC_IN + c) * HT + i + 2)
                    act.wait_ge(out_done[i % 2], ((half * NC_IN + c) * (HT // 2) + i // 2 + 1) * 16)
                    nc.scalar.copy(stage[:, i % 2], acc[:, i % 2]).then_inc(acc_read, 1)

                split_hi(0)
                square(0)
                square(1)
                h_hi(0)
                for c in range(NC_IN):
                    if 1 <= c < NC_IN - 1:
                        split_hi(c + 1)
                    for i in range(HT):
                        if c == 0 and i + 2 < HT:
                            square(i + 2)
                        if c == 0 and i + 1 < HT:
                            h_hi(i + 1)
                        evacuate(c, i)
                        if c == 0 and i == 2:
                            split_hi(1)
                    for b in range(2 if c == 0 else 0):
                        act.wait_ge(r_done, half * 2 + b + 1)
                        nc.scalar.copy(keep["glr_t"][0:RANK, bass.ds((half * 2 + b) * N, N)],
                                       racc[0:RANK, :]).then_inc(r_read, 1)

        @block.sync
        def _(sp):
            with sp.Fori(0, 2) as half:
                for c in range(NC_IN):
                    for i in range(HT):
                        sp.wait_ge(acc_read, (half * NC_IN + c) * HT + i + 3)
                        sp.dma_start(proj_t[:, bass.ds(half * HT + i, 1), c * N:(c + 1) * N],
                                       stage[:, i % 2]).then_inc(out_done[i % 2], 16)
            for s in range(2):
                sp.wait_ge(out_done[s], (NC_IN * HT + 1) * 16)

        @block.vector
        def _(dve):
            step = Steps(dve, dve_step, 2 * HT)
            dve.wait_ge(rhi_done, 1)
            nc.vector.tensor_tensor(rlo[:, :, 0:RANK], rraw[:], rhi[:, :, 0:RANK], ALU.subtract).then_inc(rlo_done, 1)
            with dve.Fori(0, 2) as half:
                step.turn(half)

                def split_lo(c):
                    dve.wait_ge(whi_done, half * NC_IN + c + 1)
                    dve.wait_ge(mm_done, half * NC_IN * HT + max(c - 1, 0) * HT + 1)
                    nc.vector.tensor_tensor(wlo[:, c % 2], raw[:, c % 2], whi[:, c % 2], ALU.subtract).then_inc(wlo_done, 1)

                def make_h(i):
                    s = i % 2
                    dve.wait_ge(sq_done, half * HT + i + 1)
                    step(nc.vector.reciprocal(rinv[:, s:s + 1], rs[:, s:s + 1]))
                    last = nc.vector.scalar_tensor_tensor(out=x[:, s], in0=x[:, s], scalar=rinv[:, s:s + 1],
                                                          in1=keep["A1"][:], op0=ALU.mult, op1=ALU.mult)
                    step(last)
                    nc.vector.tensor_tensor(x[:, s], x[:, s], keep["sh1"][:], ALU.add).then_inc(h_ready, 1)

                def h_lo(i):
                    for b in range(2):
                        dve.wait_ge(hi_done, (half * HT + i) * 2 + b + 1)
                        nc.vector.tensor_tensor(hlo[:, 4 * b:4 * b + 4, i], tp[:, i % 2, 4 * b:4 * b + 4],
                                                hhi[:, 4 * b:4 * b + 4, i], ALU.subtract).then_inc(lo_done, 1)

                make_h(0)
                split_lo(0)
                make_h(1)
                h_lo(0)
                for i in range(HT):
                    if i + 2 < HT:
                        make_h(i + 2)
                    if i + 1 < HT:
                        h_lo(i + 1)
                    if i == 2:
                        split_lo(1)
                step.check()
                for c in range(2, NC_IN):
                    split_lo(c)

        @block.tensor
        def _(pe):
            pe.sem_inc(mm_done, 1)
            pe.sem_inc(lo_done, 4)
            pe.sem_inc(acc_read, 2)
            pe.sem_inc(r_read, 1)
            with pe.Fori(0, 2) as half:

                def transposes(i):
                    pe.wait_ge(h_ready, half * HT + i + 1)
                    pe.wait_ge(lo_done, (half * HT + i) * 2 + 2)
                    for s in range(KD):
                        mm = nc.tensor.transpose(tp[:, i % 2, s], x[:, i % 2, s * P:(s + 1) * P], keep["const"]("ident"))
                    mm.then_inc(t_done, 1)

                transposes(0)
                for c in range(NC_IN):
                    pe.wait_ge(whi_done, half * NC_IN + c + 1)
                    pe.wait_ge(wlo_done, half * NC_IN + c + 2)
                    for i in range(HT):
                        if c == 0 and i + 1 < HT:
                            transposes(i + 1)
                        if c == 0:
                            pe.wait_ge(lo_done, (half * HT + i) * 2 + 6)
                        pe.wait_ge(acc_read, (half * NC_IN + c) * HT + i + 1)
                        for s in range(KD):
                            mm = split_product(nc, acc[:, i % 2], hhi[:, s, i], hlo[:, s, i], whi[:, c % 2, s],
                                               wlo[:, c % 2, s], s == 0, s == KD - 1)
                        mm.then_inc(mm_done, 1)
                    for b in range(2 if c == 0 else 0):
                        pe.wait_ge(rlo_done, 1)
                        pe.wait_ge(r_read, half * 2 + b + 1)
                        t0 = b * (HT // 2)
                        for s in range(KD):
                            mm = split_product(nc, racc[:], rhi[:, s], rlo[:, s], hhi[:, s, t0:t0 + HT // 2],
                                               hlo[:, s, t0:t0 + HT // 2], s == 0, s == KD - 1)
                        mm.then_inc(r_done, 1)


def phase_mixer(nc, k, A, keep):
    const = keep["const"]
    PAIR = GH // 2
    NSUB = P // SUB
    kcols = [SUB * (i + 1) for i in range(NSUB)]
    kfrom = [sum(kcols[:i]) for i in range(NSUB)]
    KW = sum(kcols)
    CLAMP = 80.0
    proj = k.sb("proj", [P, 2, PROJ])
    rope_x = k.sb("rope_x", [P, 2, 2 * N])
    o_out = k.sb("o_out", [P, 2, D])
    wgk = k.sb("wgk", [RANK + 1, 2 * P])
    normw = k.sb("normw", [P, 2, GDV])
    pos_i, pos_f = k.sb("pos_i", [P, NT], I32), k.sb("pos_f", [P, NT])
    ang, turns, red, wrap = (k.sb(n, [P, NT, RDK // 2]) for n in ("ang", "turns", "red", "wrap"))
    sin, cos = k.sb("sin", [P, NT, RDK // 2]), k.sb("cos", [P, NT, RDK // 2])
    glr = k.sb("glr", [RANK + 1, P])
    az, la, bs = k.sb("neg_abs", [P, 2 * P]), k.sb("log_decay", [P, 2 * P]), k.sb("run", [P, 4 * P])
    az_e, az_l = k.sb("az_exp", [P, 2 * P]), k.sb("az_ln", [P, 2 * P])
    dq, dk = k.sb("dq", [P, 2 * NSUB, SUB]), k.sb("dk", [P, PAIR, KW])
    eq, ek, eb = k.sb("eq", [P, 2, 2 * NSUB, SUB]), k.sb("ek", [P, 2, PAIR, KW]), k.sb("eb", [P, 2, 4 * P])
    qt, qe, kt = k.sb("qt", [P, PAIR, NSUB, 2, SUB]), k.sb("qe", [P, PAIR, P]), k.sb("kt", [P, PAIR, KW])
    kup = k.sb("kup", [P, GH * GDK])
    sg = k.sb("sg", [P, GH, P])
    St = k.sb("gla_state", [P, PAIR, 2 * GDV])
    rm = k.sb("rope_m", [P, 2, 2 * RH, RDK // 2])
    rc = k.sb("rope_c", [P, 2, 2 * RH, RDK // 2])
    rr = k.sb("rope", [P, 2, 2 * RH, RDK])
    rqT, rkT, rqx = (k.sb(n, [P, RH, P]) for n in ("rqT", "rkT", "rqx"))
    kz, sr = k.sb("kz", [P, RH, RDK]), k.sb("sr", [P, RH, P])
    R = k.sb("ret_state", [P, RH, RDK])
    mu = k.sb("mu", [P, RH])
    oc, sq = k.sb("oc", [P, 8, GDV]), k.sb("sq", [P, 8, GDV])
    var, lnv, r8 = (k.sb(n, [P, 8]) for n in ("var", "lnv", "r8"))
    ge, gl, gw, ginv = k.sb("ge", [P, 2, N]), k.sb("gl", [P, 2, N]), k.sb("gw", [P, 2, N]), k.sb("ginv", [P, 2, N])
    b_z, b_run, b_gT, b_gs, b_go, b_gu, b_q, b_k = (k.ps(n, [P, N]) for n in "z run gT gs go gu q k".split())
    names = ("glr z gT gi az az_e ln la run bs exps d qk kup gs sg go gu gS rm rr rt rqT kz rqx rs sr ro ru rR og oc sq var lnv r8 ge "
             "gl ginv gw o out").split()
    ev = {n: k.sem("ev_" + n) for n in names}
    setup_dma, pos_step, pool_set, dve_step, sin_done = k.sems(
        "setup_dma pos_step pool_set dve_step sin_done")
    wait_carrier = k.sem("wait_carrier")
    p_in = [k.sem(f"p_in{s}") for s in range(2)]
    rope_in = [k.sem(f"rope_in{s}") for s in range(2)]
    o_done = [k.sem(f"o_done{s}") for s in range(2)]
    proj_t = keep["proj"].rearrange("(t p) n -> p t n", p=P)
    o_t = keep["o"].rearrange("(t p) n -> p t n", p=P)
    TWO_PI = 2 * np.pi
    c1 = float(np.float32(np.floor(TWO_PI * 2 ** 5) / 2 ** 5))
    c2 = float(np.float32(np.floor((TWO_PI - c1) * 2 ** 14) / 2 ** 14))
    c3 = float(np.float32(TWO_PI - c1 - c2))
    MAGIC = 12582912.0
    HALF = RDK // 2

    def heads(ap, n):
        return ap.rearrange("p (h d) -> p h d", h=n)

    def bc(ap, shape):
        return ap.to_broadcast(shape)

    def tiles(eng, step):
        for u in range(2):
            step(u, u, 0)
        with eng.Fori(1, NT // 2 - 1) as j:
            for u in range(2):
                step(j * 2 + u, u, j)
        for u in range(2):
            step(NT - 2 + u, u, NT // 2 - 1)

    def last_tile(i):
        return isinstance(i, int) and i == NT - 1

    def first_tile(i):
        return isinstance(i, int) and i == 0

    with nc.Block() as block:

        @block.sync
        def _(sp):
            sp.dma_start(wgk[0:RANK, :], A["w_gk2"].rearrange("o r n -> (o r) n")).then_inc(setup_dma, 16)
            sp.dma_start(wgk[RANK:RANK + 1, :], A["b_gk"]).then_inc(setup_dma, 16)
            sp.dma_start(pos_i[:], A["positions"].rearrange("o (t p) -> p (o t)", p=P),
                         allow_slow_non_contiguous=True).then_inc(setup_dma, 16)
            sp.dma_start(normw[:, 0], row(A["gla_onorm"])).then_inc(setup_dma, 16)
            sp.dma_start(normw[:, 1], row(A["ret_onorm"])).then_inc(setup_dma, 16)
            for u in range(2):
                sp.sem_inc(o_done[u], 16)

            def load_rope(i, u):
                sp.wait_ge(ev["rr"], i + 1)
                sp.sem_inc(wait_carrier, 1)
                sp.dma_start(rope_x[:, u], proj_t[:, bass.ds(i, 1), C_RQ:C_RQ + 2 * N]).then_inc(rope_in[u], 16)

            def store(i, u):
                sp.wait_ge(ev["o"], i + 3)
                sp.sem_inc(wait_carrier, 1)
                sp.dma_start(o_t[:, bass.ds(i + 1, 1)], o_out[:, u]).then_inc(o_done[u], 16)

            def load(i, u):
                for n in ("ro", "kup", "gw", "ge"):
                    sp.wait_ge(ev[n], i + 1)
                sp.sem_inc(wait_carrier, 1)
                for c0, c1 in ((0, C_RQ), (C_RV, PROJ)):
                    sp.dma_start(proj[:, u, c0:c1], proj_t[:, bass.ds(i, 1), c0:c1]).then_inc(p_in[u], 16)

            load_rope(0, 0)
            load_rope(1, 1)
            load(0, 0)
            load(1, 1)

            def step(i, u, j):
                if not (isinstance(i, int) and i >= NT - 2):
                    load_rope(i + 2, u)
                    load(i + 2, u)
                store(i, u)

            tiles(sp, step)
            for u in range(2):
                sp.wait_ge(o_done[u], 16 * (NT // 2 + 1))

        @block.gpsimd
        def _(pool):
            nc.gpsimd.memset(St[:], 0.0).then_inc(pool_set, 1)
            nc.gpsimd.memset(R[:], 0.0).then_inc(pool_set, 1)
            nc.gpsimd.memset(sg[:], 0.0).then_inc(pool_set, 1)
            nc.gpsimd.memset(qt[:], 0.0).then_inc(pool_set, 1)
            for n in names:
                pool.sem_inc(ev[n], 2)
            pool.wait_ge(setup_dma, 80)

            def output(t, u):
                pool.wait_ge(ev["gi"], t + 3)
                pool.wait_ge(ev["out"], t + 3)
                nc.gpsimd.tensor_tensor(o_out[:, u], o_out[:, u], gw[:].rearrange("p a n -> p (a n)"),
                                        ALU.mult).then_inc(ev["o"], 1)

            def front_rank(t):
                pool.wait_ge(ev["z"], t + 2)
                nc.gpsimd.tensor_copy(glr[:], keep["glr_t"][:, bass.ds(t * P, P)]).then_inc(ev["glr"], 1)

            def front_rope(t, u, j):
                sin_t = sin[:, bass.ds(t, 1)].to_broadcast([P, 2 * RH, HALF])
                pool.wait_ge(rope_in[u], (j + 1) * 16)
                pool.wait_ge(ev["rr"], t + 2)
                x = heads(rope_x[:, u], 2 * RH)
                nc.gpsimd.tensor_tensor(rm[:, 0], x[:, :, HALF:], sin_t, ALU.mult)
                nc.gpsimd.tensor_tensor(rm[:, 1], x[:, :, 0:HALF], sin_t, ALU.mult).then_inc(ev["rm"], 1)

            def step(i, u, j):
                pj = proj[:, u]
                now, last = i + 3, i + 2
                pool.wait_ge(p_in[u], (j + 1) * 32)
                pool.wait_ge(ev["exps"], now)
                pool.wait_ge(ev["gu"], last)
                nc.gpsimd.tensor_tensor(kup[:], pj[:, C_GK:C_GK + GH * GDK], eb[:, u, 2 * P:4 * P],
                                        ALU.mult).then_inc(ev["kup"], 1)
                pool.wait_ge(ev["rr"], now)
                pool.wait_ge(ev["ru"], last)
                nc.gpsimd.tensor_tensor(kz[:], rr[:, u, RH:2 * RH],
                                        const("zeta").unsqueeze(2).to_broadcast([P, RH, RDK]),
                                        ALU.mult).then_inc(ev["kz"], 1)
                if not first_tile(i):
                    output(i - 1, 1 - u)
                if not last_tile(i):
                    front_rope(i + 1, 1 - u, j + u)
                if not (isinstance(i, int) and i >= NT - 2):
                    front_rank(i + 2)
                pool.wait_ge(ev["o"], last)
                nc.gpsimd.tensor_tensor(heads(gw[:, 0], GH), heads(pj[:, C_GG:C_GG + N], GH),
                                        normw[:, 0:1].to_broadcast([P, GH, GDV]), ALU.mult)
                nc.gpsimd.tensor_tensor(heads(gw[:, 1], RH), heads(pj[:, C_RG:C_RG + N], RH),
                                        normw[:, 1:2].to_broadcast([P, RH, RDK]), ALU.mult).then_inc(ev["gw"], 1)
                pool.wait_ge(ev["ginv"], now)
                pool.wait_ge(ev["gw"], now)
                nc.gpsimd.tensor_tensor(gw[:], gw[:], ginv[:], ALU.mult).then_inc(ev["gi"], 1)

            front_rank(0)
            pool.wait_ge(sin_done, 2)
            front_rope(0, 0, 0)
            front_rank(1)
            tiles(pool, step)
            output(NT - 1, 1)

        @block.scalar
        def _(act):
            act.wait_ge(pos_step, 1)
            nc.scalar.activation(sin[:], red[:], ACT.Sin).then_inc(sin_done, 1)
            nc.scalar.activation(cos[:], wrap[:], ACT.Sin).then_inc(sin_done, 1)
            load_ln_exp(nc)

            def front_log(t):
                act.wait_ge(ev["z"], t + 3)
                act.wait_ge(ev["la"], t + 2)
                nc.scalar.activation(az[:], b_z[:, 0:2 * P], ACT.Abs).then_inc(ev["az"], 1)
                act.wait_ge(ev["az"], t + 3)
                nc.scalar.activation(az_e[:], az[:], ACT.Exp, scale=-1.0).then_inc(ev["az_e"], 1)
                act.wait_ge(ev["az_e"], t + 3)
                nc.scalar.activation(az_l[:], az_e[:], ACT.Ln, bias=const("ones")[:, 0:1]).then_inc(ev["ln"], 1)

            def front_sums(t):
                act.wait_ge(ev["run"], t + 3)
                act.wait_ge(ev["exps"], t + 2)
                nc.scalar.copy(bs[:], b_run[:]).then_inc(ev["bs"], 1)

            def front_exps(t, u):
                act.wait_ge(ev["bs"], t + 3)
                act.wait_ge(ev["d"], t + 3)
                for n in ("qk", "gS", "kup"):
                    act.wait_ge(ev[n], t + 1)
                nc.scalar.activation(eb[:, u], bs[:], ACT.Exp)
                nc.scalar.activation(eq[:, u], dq[:], ACT.Exp)
                nc.scalar.activation(ek[:, u], dk[:], ACT.Exp, scale=-1.0).then_inc(ev["exps"], 1)

            def roots(t):
                act.wait_ge(ev["var"], t + 3)
                nc.scalar.activation(lnv[:], var[:], ACT.Ln, scale=1.0 / GDV, bias=const("eps")).then_inc(ev["lnv"], 1)
                act.wait_ge(ev["lnv"], t + 3)
                act.wait_ge(ev["out"], t + 2)
                nc.scalar.activation(r8[:], lnv[:], ACT.Exp, scale=-0.5).then_inc(ev["r8"], 1)

            def step(i, u, j):
                pj = proj[:, u]
                now, last = i + 3, i + 2
                if not first_tile(i):
                    roots(i - 1)
                if not last_tile(i):
                    front_log(i + 1)
                act.wait_ge(ev["rt"], now)
                act.wait_ge(ev["rs"], last)
                act.wait_ge(ev["rqx"], last)
                nc.scalar.copy(rqT[:], heads(b_q[:], RH))
                nc.scalar.copy(rkT[:], heads(b_k[:], RH)).then_inc(ev["rqT"], 1)
                if not last_tile(i):
                    front_sums(i + 1)
                act.wait_ge(p_in[u], (j + 1) * 32)
                nc.scalar.activation(ge[:, 0], pj[:, C_GG:C_GG + N], ACT.Exp, scale=-1.0)
                nc.scalar.activation(ge[:, 1], pj[:, C_RG:C_RG + N], ACT.Exp, scale=-1.0).then_inc(ev["ge"], 1)
                act.wait_ge(ev["ge"], now)
                nc.scalar.activation(gl[:], ge[:], ACT.Ln, bias=const("ones")[:, 0:1]).then_inc(ev["gl"], 1)
                act.wait_ge(ev["gl"], now)
                act.wait_ge(ev["gi"], last)
                nc.scalar.activation(ginv[:], gl[:], ACT.Exp, scale=-1.0).then_inc(ev["ginv"], 1)
                act.wait_ge(ev["go"], now)
                act.wait_ge(ev["out"], last)
                nc.scalar.copy(oc[:, 0:GH], heads(b_go[:], GH)).then_inc(ev["og"], 1)
                if not last_tile(i):
                    front_exps(i + 1, 1 - u)
                act.wait_ge(ev["og"], now)
                act.wait_ge(ev["oc"], now)
                act.wait_ge(ev["var"], last)
                nc.scalar.activation(sq[:], oc[:], ACT.Square).then_inc(ev["sq"], 1)

            front_log(0)
            front_sums(0)
            front_exps(0, 0)
            tiles(act, step)
            roots(NT - 1)

        @block.vector
        def _(dve):
            own = Steps(dve, dve_step, 0)
            dve.wait_ge(setup_dma, 80)
            own(nc.vector.tensor_copy(pos_f[:], pos_i[:]))
            own(nc.vector.tensor_tensor(ang[:], pos_f[:].unsqueeze(2).to_broadcast([P, NT, HALF]),
                                        const("inv_freq").unsqueeze(1).to_broadcast([P, NT, HALF]), ALU.mult))

            def reduce_turns(out, a):
                own(nc.vector.tensor_scalar(turns[:], a, 1.0 / TWO_PI, MAGIC, ALU.mult, ALU.add))
                own(nc.vector.tensor_scalar(turns[:], turns[:], MAGIC, None, ALU.subtract))
                own(nc.vector.scalar_tensor_tensor(out=out, in0=turns[:], scalar=-c1, in1=a, op0=ALU.mult, op1=ALU.add))
                own(nc.vector.scalar_tensor_tensor(out=out, in0=turns[:], scalar=-c2, in1=out, op0=ALU.mult, op1=ALU.add))
                own(nc.vector.scalar_tensor_tensor(out=out, in0=turns[:], scalar=-c3, in1=out, op0=ALU.mult, op1=ALU.add))

            def clamp(ap):
                own(nc.vector.tensor_scalar(ap, ap, float(np.float32(3.1415925)), -float(np.float32(3.1415925)), ALU.min, ALU.max))

            reduce_turns(red[:], ang[:])
            own(nc.vector.tensor_scalar(wrap[:], red[:], float(np.pi / 2), None, ALU.add))
            own(nc.vector.tensor_scalar(turns[:], wrap[:], float(np.pi), -TWO_PI, ALU.is_gt, ALU.mult))
            own(nc.vector.tensor_tensor(wrap[:], wrap[:], turns[:], ALU.add))
            clamp(red[:])
            clamp(wrap[:])
            dve.sem_inc(pos_step, 1)
            dve.wait_ge(pool_set, 4)
            dve.wait_ge(sin_done, 2)
            SETUP = own.n
            FRONT, PER = 9, 11

            def front_log(t):
                dve.wait_ge(ev["ln"], t + 3)
                dve.wait_ge(ev["run"], t + 2)
                nc.vector.scalar_tensor_tensor(out=la[:], in0=b_z[:, 0:2 * P], scalar=0.0, in1=az_l[:],
                                               op0=ALU.min, op1=ALU.subtract).then_inc(ev["la"], 1)

            def front_differences(t):
                dve.wait_ge(ev["bs"], t + 3)
                dve.wait_ge(ev["exps"], t + 2)
                b2 = bs[:, 0:2 * P]
                sub = b2.rearrange("p (c t) -> p c t", t=SUB)
                own(nc.vector.tensor_tensor(dq[:], sub, sub[:, :, SUB // 2 - 1:SUB // 2].to_broadcast([P, 2 * NSUB, SUB]),
                                            ALU.subtract))
                bp = b2.rearrange("p (a t) -> p a t", a=PAIR)
                for c in range(NSUB):
                    ref = c * SUB + SUB // 2 - 1
                    own(nc.vector.tensor_tensor(dk[:, :, kfrom[c]:kfrom[c] + kcols[c]], bp[:, :, 0:kcols[c]],
                                                bp[:, :, ref:ref + 1].to_broadcast([P, PAIR, kcols[c]]), ALU.subtract))
                own(nc.vector.tensor_scalar(dq[:], dq[:], CLAMP, None, ALU.min))
                nc.vector.tensor_scalar(dk[:], dk[:], -CLAMP, None, ALU.max).then_inc(ev["d"], 1)

            def front_rope(t, u, j):
                cos_t = cos[:, bass.ds(t, 1)].to_broadcast([P, 2 * RH, HALF])
                dve.wait_ge(rope_in[u], (j + 1) * 16)
                dve.wait_ge(ev["rr"], t + 2)
                x = heads(rope_x[:, u], 2 * RH)
                own(nc.vector.tensor_tensor(rc[:, 0], x[:, :, 0:HALF], cos_t, ALU.mult))
                own(nc.vector.tensor_tensor(rc[:, 1], x[:, :, HALF:], cos_t, ALU.mult))
                dve.wait_ge(ev["rm"], t + 3)
                dve.wait_ge(ev["rt"], t + 1)
                dve.wait_ge(ev["kz"], t + 1)
                own(nc.vector.tensor_tensor(rr[:, u, :, 0:HALF], rc[:, 0], rm[:, 0], ALU.subtract))
                nc.vector.tensor_tensor(rr[:, u, :, HALF:], rc[:, 1], rm[:, 1], ALU.add).then_inc(ev["rr"], 1)

            def norms(t, u, j):
                dve.wait_ge(ev["r8"], t + 3)
                dve.wait_ge(o_done[u], (j + 1) * 16)
                nc.vector.tensor_tensor(heads(o_out[:, u], 8), oc[:], r8[:].unsqueeze(2).to_broadcast([P, 8, GDV]),
                                        ALU.mult).then_inc(ev["out"], 1)

            def step(i, u, j):
                now, last = i + 3, i + 2
                own.base, own.n = i * PER + SETUP + FRONT, 0
                dve.wait_ge(ev["exps"], now)
                dve.wait_ge(ev["gT"], now)
                dve.wait_ge(ev["gs"], last)
                dve.wait_ge(ev["go"], last)
                q_t = b_gT[:, 0:2 * P].rearrange("p (a t) -> p a t", a=PAIR)
                k_t = b_gT[:, 2 * P:4 * P].rearrange("p (a t) -> p a t", a=PAIR)
                scale = GDK ** -0.5
                for c in range(NSUB):
                    nc.vector.tensor_tensor(kt[:, :, kfrom[c]:kfrom[c] + kcols[c]], k_t[:, :, 0:kcols[c]],
                                            ek[:, u, :, kfrom[c]:kfrom[c] + kcols[c]], ALU.mult)
                for h in range(2):
                    rows = slice(h * GDK, (h + 1) * GDK)
                    nc.vector.scalar_tensor_tensor(out=qt[rows, :, :, h].rearrange("p a c t -> p (a c) t"),
                                                   in0=b_gT[rows, 0:2 * P].rearrange("p (c t) -> p c t", t=SUB),
                                                   scalar=scale, in1=eq[rows, u], op0=ALU.mult, op1=ALU.mult)
                nc.vector.scalar_tensor_tensor(out=qe[:], in0=q_t, scalar=scale,
                                               in1=eb[:, u, 0:2 * P].rearrange("p (a t) -> p a t", a=PAIR),
                                               op0=ALU.mult, op1=ALU.mult).then_inc(ev["qk"], 1)
                if not last_tile(i):
                    front_log(i + 1)
                if not first_tile(i):
                    norms(i - 1, 1 - u, j - 1 + u)
                dve.wait_ge(ev["rqT"], now)
                dve.wait_ge(ev["ro"], last)
                nc.vector.tensor_tensor(rqx[:], rqT[:], heads(const("xi"), RH), ALU.mult).then_inc(ev["rqx"], 1)
                dve.wait_ge(ev["gs"], now)
                for c in range(NSUB):
                    cols = slice(c * SUB, (c + 1) * SUB)
                    ins = nc.vector.tensor_tensor(
                        sg[0:kcols[c], :, cols], heads(b_gs[:], GH)[0:kcols[c], :, cols],
                        const("causal")[0:kcols[c], cols].unsqueeze(1).to_broadcast([kcols[c], GH, SUB]), ALU.mult)
                ins.then_inc(ev["sg"], 1)
                dve.wait_ge(ev["rs"], now)
                nc.vector.tensor_tensor(sr[:], heads(b_q[:], RH), heads(const("decay"), RH), ALU.mult).then_inc(ev["sr"], 1)
                if not last_tile(i):
                    front_differences(i + 1)
                dve.wait_ge(ev["ro"], now)
                dve.wait_ge(ev["ru"], now)
                for h in range(RH):
                    ins = nc.vector.scalar_tensor_tensor(out=R[:, h], in0=R[:, h], scalar=GAMMA_TILE[h],
                                                         in1=b_run[:, h * RDK:(h + 1) * RDK], op0=ALU.mult, op1=ALU.add)
                ins.then_inc(ev["rR"], 1)
                dve.wait_ge(ev["gu"], now)
                dve.wait_ge(ev["go"], now)
                for h in range(GH):
                    pr, rows = h // 2, slice((h % 2) * GDK, (h % 2 + 1) * GDK)
                    cols = slice((h % 2) * GDV, (h % 2 + 1) * GDV)
                    ins = nc.vector.scalar_tensor_tensor(
                        out=St[rows, pr, cols], in0=St[rows, pr, cols], scalar=eb[rows, u, (pr + 1) * P - 1:(pr + 1) * P],
                        in1=b_gu[rows, pr * 2 * GDV + cols.start:pr * 2 * GDV + cols.stop], op0=ALU.mult, op1=ALU.add)
                ins.then_inc(ev["gS"], 1)
                own(nc.vector.tensor_reduce(mu[:], heads(b_k[:], RH), AX_X, ALU.add))
                own(nc.vector.tensor_scalar(mu[:], mu[:], -1.0 / RDK, None, ALU.mult))
                dve.wait_ge(ev["out"], last)
                nc.vector.tensor_tensor(oc[:, GH:8], heads(b_k[:], RH), mu[:].unsqueeze(2).to_broadcast([P, RH, RDK]),
                                        ALU.add).then_inc(ev["oc"], 1)
                if not last_tile(i):
                    front_rope(i + 1, 1 - u, j + u)
                dve.wait_ge(ev["sq"], now)
                nc.vector.tensor_reduce(var[:], sq[:], AX_X, ALU.add).then_inc(ev["var"], 1)

            front_rope(0, 0, 0)
            front_log(0)
            front_differences(0)
            assert own.n == SETUP + FRONT
            tiles(dve, step)
            norms(NT - 1, 1, NT // 2 - 1)

        @block.tensor
        def _(pe):
            pe.wait_ge(setup_dma, 80)
            pe.wait_ge(pool_set, 4)
            ident = const("ident")

            def front_log(t):
                pe.wait_ge(ev["glr"], t + 3)
                pe.wait_ge(ev["la"], t + 2)
                nc.tensor.matmul(b_z[:, 0:2 * P], glr[:], wgk[:], start=True, stop=True).then_inc(ev["z"], 1)

            def front_sums(t):
                pe.wait_ge(ev["la"], t + 3)
                pe.wait_ge(ev["bs"], t + 2)
                pe.wait_ge(ev["rR"], t + 1)
                for c in range(2):
                    nc.tensor.matmul(b_run[:, c * P:(c + 1) * P], la[:, c * P:(c + 1) * P], const("sum_to"),
                                     start=True, stop=True)
                nc.tensor.matmul(b_run[:, 2 * P:4 * P], const("sum_after"), la[:], start=True,
                                 stop=True).then_inc(ev["run"], 1)

            def step(i, u, j):
                pj = proj[:, u]
                now, last = i + 3, i + 2
                if not last_tile(i):
                    front_log(i + 1)
                pe.wait_ge(p_in[u], (j + 1) * 32)
                pe.wait_ge(ev["qk"], last)
                for c in range(4):
                    mm = nc.tensor.transpose(b_gT[:, c * P:(c + 1) * P], pj[:, C_GQ + c * P:C_GQ + (c + 1) * P], ident)
                mm.then_inc(ev["gT"], 1)
                pe.wait_ge(ev["rr"], now)
                pe.wait_ge(ev["sr"], last)
                pe.wait_ge(ev["oc"], last)
                for h in range(RH):
                    nc.tensor.transpose(b_q[:, h * P:(h + 1) * P], rr[:, u, h], ident)
                for h in range(RH):
                    mm = nc.tensor.transpose(b_k[:, h * P:(h + 1) * P], rr[:, u, RH + h], ident)
                mm.then_inc(ev["rt"], 1)
                pe.wait_ge(ev["kup"], now)
                pe.wait_ge(ev["gS"], last)
                for c in range(PAIR):
                    mm = nc.tensor.matmul(b_gu[:, c * 2 * GDV:(c + 1) * 2 * GDV], kup[:, c * P:(c + 1) * P],
                                          pj[:, C_GV + c * 2 * GDV:C_GV + (c + 1) * 2 * GDV], start=True, stop=True)
                mm.then_inc(ev["gu"], 1)
                pe.wait_ge(ev["qk"], now)
                pe.wait_ge(ev["sg"], last)
                for a in range(PAIR):
                    for c in range(NSUB):
                        mm = nc.tensor.matmul(heads(b_gs[:], GH)[0:kcols[c], 2 * a:2 * a + 2, c * SUB:(c + 1) * SUB],
                                              kt[:, a, kfrom[c]:kfrom[c] + kcols[c]], qt[:, a, c],
                                              start=True, stop=True)
                mm.then_inc(ev["gs"], 1)
                if not last_tile(i):
                    front_sums(i + 1)
                pe.wait_ge(ev["rqT"], now)
                for h in range(RH):
                    mm = nc.tensor.matmul(b_q[:, h * P:(h + 1) * P], rkT[:, h], rqT[:, h], start=True, stop=True)
                mm.then_inc(ev["rs"], 1)
                pe.wait_ge(ev["sg"], now)
                pe.wait_ge(ev["gS"], last)
                pe.wait_ge(ev["og"], last)
                for c in range(PAIR):
                    cols = slice(c * 2 * GDV, (c + 1) * 2 * GDV)
                    nc.tensor.matmul(b_go[:, cols], qe[:, c], St[:, c], start=True, stop=False, skip_group_check=True)
                    for h in (2 * c, 2 * c + 1):
                        mm = nc.tensor.matmul(b_go[:, h * GDV:(h + 1) * GDV], sg[:, h],
                                              pj[:, C_GV + h * GDV:C_GV + (h + 1) * GDV], start=False,
                                              stop=(h % 2 == 1), skip_group_check=True)
                mm.then_inc(ev["go"], 1)
                pe.wait_ge(ev["kz"], now)
                pe.wait_ge(ev["bs"], now if last_tile(i) else now + 1)
                for h in range(RH):
                    mm = nc.tensor.matmul(b_run[:, h * RDK:(h + 1) * RDK], kz[:, h],
                                          pj[:, C_RV + h * RDK:C_RV + (h + 1) * RDK], start=True, stop=True)
                mm.then_inc(ev["ru"], 1)
                pe.wait_ge(ev["sr"], now)
                pe.wait_ge(ev["rqx"], now)
                pe.wait_ge(ev["rR"], last)
                for h in range(RH):
                    nc.tensor.matmul(b_k[:, h * P:(h + 1) * P], sr[:, h], pj[:, C_RV + h * RDK:C_RV + (h + 1) * RDK],
                                     start=True, stop=False)
                    mm = nc.tensor.matmul(b_k[:, h * P:(h + 1) * P], rqx[:, h], R[:, h], start=False, stop=True)
                mm.then_inc(ev["ro"], 1)

            front_log(0)
            front_sums(0)
            tiles(pe, step)



def phase_routing(nc, k, A, keep):
    const = keep["const"]
    raw = k.sb("w_raw", [P, KD, N])
    whi, wlo = (k.sb(n, [P, 2, KD, N], F32R) for n in ("w_hi", "w_lo"))
    wr = k.sb("w_router", [P, KD, E])
    br = k.sb("b_router", [P, E])
    bd = k.sb("b_down", [E, D])
    g1, A2, sh2, g2 = (k.sb(n, [P, D]) for n in ("g1", "A2", "sh2", "g2"))
    empty = k.sb("empty", [P, PLACES, 2], I32)
    o, x = k.sb("o", [P, 2, D]), k.sb("x", [P, 2, D])
    ohi, olo = (k.sb(n, [P, KD, P], F32R) for n in ("o_hi", "o_lo"))
    x2, h2, yi = (k.sb(n, [P, D]) for n in ("x2", "h2", "yi"))
    squares = k.sb("squares", [P, D], mybir.dt.bfloat16)
    h2T = k.sb("h2T", [P, KD, P])
    ssq, lnv, rs = (k.sb(n, [P, 1]) for n in ("ssq", "lnv", "rs"))
    lg, lr, mask, ex, W, key, pick, kf, rkf = (k.sb(n, [P, E]) for n in
                                               "lg lr mask ex W key pick kf rkf".split())
    best, top = k.sb("best", [P, 8]), k.sb("top", [P, 8])
    neg, den = k.sb("neg", [P, 1]), k.sb("den", [P, 1])
    run = k.sb("run", [P, E])
    ri, ra, rb = (k.sb(n, [P, E], I32) for n in ("ri", "ra", "rb"))
    wj, idx, rec = k.sb("wj", [P, TOPK]), k.sb("idx", [P, TOPK], I32), k.sb("rec", [P, TOPK, 2], I32)
    wT = k.sb("wT", [E, P])
    over = k.sb("over", [P, E, NT])
    tiles, groups, cumg, cumt, sel = (k.sb(n, [P, E]) for n in "tiles groups cumg cumt sel".split())
    gT, tT = k.sb("gT", [E, P]), k.sb("tT", [E, P])
    col = k.sb("col", [P, 8])
    table, table_i = k.sb("table", [P, 4]), k.sb("table_i", [P, 4], I32)
    acc, tp, tq = k.ps("acc", [P, 2, N]), k.ps("tp", [P, KD, P]), k.ps("tq", [P, KD, P])
    sm, wt = k.ps("sm", [P, N]), k.ps("wt", [P, N])
    names = ("t1 ohi olo mm xg x2 sq lnv rs h2 t2 h2t lg lgs ex W mask rk wt wtc bd yi rec stored").split()
    ev = {n: k.sem("ev_" + n) for n in names}
    setup_dma, w_in, whi_done, wlo_done, pool_set, dve_step, h2_out, y_out, place_out, empty_set, empty_out = k.sems(
        "setup_dma w_in whi_done wlo_done pool_set dve_step h2_out y_out place_out empty_set empty_out")
    table_step, table_out, wait_carrier, table_ready, table_t = k.sems(
        "table_step table_out wait_carrier table_ready table_t")
    o_in = [k.sem(f"o_in{s}") for s in range(2)]
    x_in = [k.sem(f"x_in{s}") for s in range(2)]
    o_t = keep["o"].rearrange("(t p) n -> p t n", p=P)
    x_t = A["x"].rearrange("o (t p) d -> p (o t) d", p=P)
    h2_t = keep["h2"].rearrange("(t p) n -> p t n", p=P)
    y_t = [y.rearrange("(t p) n -> p t n", p=P) for y in keep["y"]]
    w_t = A["w_out"].rearrange("o (s p) n -> p (o s) n", p=P)
    NOWHERE = 3.0e38
    with nc.Block() as block:

        @block.sync
        def _(sp):
            sp.dma_start(raw[:], w_t[:, :, 0:N]).then_inc(w_in, 16)
            sp.dma_start(wr[:], A["w_router"].rearrange("o (s p) e -> p (o s) e", p=P)).then_inc(setup_dma, 16)
            sp.dma_start(br[:], row(A["b_router"])).then_inc(setup_dma, 16)
            sp.dma_start(bd[:], A["b_down"].rearrange("o e d -> (o e) d")).then_inc(setup_dma, 16)
            for t, n in ((g1, "g1"), (A2, "A2"), (sh2, "sh2"), (g2, "g2")):
                sp.dma_start(t[:], keep[n]).then_inc(setup_dma, 16)
            sp.wait_ge(wlo_done, 1)
            sp.dma_start(raw[:], w_t[:, :, N:2 * N]).then_inc(w_in, 16)
            with sp.Fori(0, NT // 2) as j:
                for u in range(2):
                    i = j * 2 + u
                    sp.wait_ge(ev["t1"], i + 1)
                    sp.dma_start(o[:, u], o_t[:, bass.ds(i + 1, 1)]).then_inc(o_in[u], 16)
                    sp.wait_ge(ev["x2"], i + 1)
                    sp.dma_start(x[:, u], x_t[:, bass.ds(i, 1)]).then_inc(x_in[u], 16)
            sp.wait_ge(table_step, 1)
            sp.dma_start(keep["groups"], table_i[:]).then_inc(table_out, 16)
            sp.wait_ge(table_out, 16)

        @block.gpsimd
        def _(pool):
            nc.gpsimd.memset(run[:], 0.0).then_inc(pool_set, 1)
            for n in names:
                pool.sem_inc(ev[n], 2)
            pool.wait_ge(empty_set, 1)
            pool.dma_start(keep["places"].rearrange("(p q) c -> p (q c)", p=P), empty[:].rearrange("p q c -> p (q c)")
                           ).then_inc(empty_out, 16)
            pool.wait_ge(empty_out, 16)
            with pool.Fori(0, NT) as i:
                pool.wait_ge(ev["yi"], i + 3)
                pool.sem_inc(wait_carrier, 1)
                for half in range(2):
                    pool.dma_start(y_t[half][:, bass.ds(i, 1)], yi[:, half * N:(half + 1) * N]).then_inc(y_out, 16)
                pool.wait_ge(ev["rec"], i + 3)
                pool.sem_inc(wait_carrier, 1)
                for c in range(TOPK):
                    pool.indirect_dma_start(out=keep["places"], out_offset=bass.IndirectOffsetOnAxis(ap=idx[:, c:c + 1], axis=0),
                                            in_=rec[:, c], in_offset=None).then_inc(place_out, 16)
                pool.wait_ge(y_out, (i + 1) * 32)
                pool.wait_ge(place_out, (i + 1) * 16 * TOPK)
                pool.sem_inc(ev["stored"], 1)

        @block.scalar
        def _(act):
            act.sem_inc(h2_out, 16)
            load_ln_exp(nc)
            for c in range(2):
                act.wait_ge(w_in, 16 * (c + 1))
                nc.scalar.copy(whi[:, c], raw[:]).then_inc(whi_done, 1)
            with act.Fori(0, NT) as i:
                now, last = i + 3, i + 2
                act.wait_ge(ev["t1"], now)
                act.wait_ge(ev["mm"], last)
                for b in range(2):
                    nc.scalar.copy(ohi[:, 4 * b:4 * b + 4], tp[:, 4 * b:4 * b + 4]).then_inc(ev["ohi"], 1)
                act.wait_ge(ev["x2"], now)
                nc.scalar.activation(squares[:], x2[:], ACT.Square, accum_out=ssq[:]).then_inc(ev["sq"], 1)
                act.wait_ge(ev["sq"], now)
                nc.scalar.activation(lnv[:], ssq[:], ACT.Ln, scale=1.0 / D, bias=const("eps")).then_inc(ev["lnv"], 1)
                act.wait_ge(ev["lnv"], now)
                act.wait_ge(ev["h2"], last)
                nc.scalar.activation(rs[:], lnv[:], ACT.Exp, scale=-0.5).then_inc(ev["rs"], 1)
                act.wait_ge(ev["h2"], now)
                act.dma_start(h2_t[:, bass.ds(i, 1)], h2[:]).then_inc(h2_out, 16)
                act.wait_ge(ev["t2"], now)
                act.wait_ge(ev["lg"], last)
                for b in range(2):
                    ins = nc.scalar.copy(h2T[:, 4 * b:4 * b + 4], tq[:, 4 * b:4 * b + 4])
                ins.then_inc(ev["h2t"], 1)
                act.wait_ge(ev["lgs"], now)
                act.wait_ge(ev["W"], last)
                nc.scalar.activation(ex[:], lg[:], ACT.Exp, bias=neg[:]).then_inc(ev["ex"], 1)
                act.wait_ge(ev["wt"], now)
                act.wait_ge(ev["bd"], last)
                nc.scalar.copy(wT[:], wt[0:E, 0:P]).then_inc(ev["wtc"], 1)
            act.wait_ge(h2_out, 16 * (NT + 1))

        @block.vector
        def _(dve):
            own = Steps(dve, dve_step)
            own(nc.vector.memset(empty[:], 0))
            own(nc.vector.tensor_scalar(col[:, 0:1], const("number"), float(S), None, ALU.add))
            nc.vector.tensor_copy(empty[:, :, 0], col[:, 0:1].to_broadcast([P, PLACES])).then_inc(empty_set, 1)
            for c in range(2):
                dve.wait_ge(whi_done, c + 1)
                nc.vector.tensor_tensor(wlo[:, c], raw[:], whi[:, c], ALU.subtract).then_inc(wlo_done, 1)
            dve.wait_ge(setup_dma, 7 * 16)
            dve.wait_ge(pool_set, 1)
            SETUP = own.n
            own.per_turn = PER = 2 * 25
            with dve.Fori(0, NT // 2) as j:
                own.base, own.n = j * PER + SETUP, 0
                for u in range(2):
                    i = j * 2 + u
                    now, last = i + 3, i + 2
                    for b in range(2):
                        dve.wait_ge(ev["ohi"], i * 2 + b + 3)
                        nc.vector.tensor_tensor(olo[:, 4 * b:4 * b + 4], tp[:, 4 * b:4 * b + 4], ohi[:, 4 * b:4 * b + 4],
                                                ALU.subtract).then_inc(ev["olo"], 1)
                    dve.wait_ge(ev["mm"], now)
                    own(nc.vector.tensor_tensor(x2[:], acc[:].rearrange("p a n -> p (a n)"), g1[:], ALU.mult))
                    dve.wait_ge(x_in[u], (j + 1) * 16)
                    nc.vector.tensor_tensor(x2[:], x2[:], x[:, u], ALU.add).then_inc(ev["x2"], 1)
                    dve.wait_ge(ev["rs"], now)
                    dve.wait_ge(ev["t2"], last)
                    dve.wait_ge(h2_out, (i + 1) * 16)
                    own(nc.vector.scalar_tensor_tensor(out=h2[:], in0=x2[:], scalar=rs[:], in1=A2[:], op0=ALU.mult,
                                                       op1=ALU.mult))
                    nc.vector.tensor_tensor(h2[:], h2[:], sh2[:], ALU.add).then_inc(ev["h2"], 1)
                    dve.wait_ge(ev["lg"], now)
                    own(nc.vector.tensor_tensor(lg[:], sm[:, 0:E], br[:], ALU.add))
                    dve.sem_inc(wait_carrier, 1)
                    own(nc.vector.max(best[:], lg[:]))
                    nc.vector.tensor_scalar(neg[:], best[:, 0:1], -1.0, None, ALU.mult).then_inc(ev["lgs"], 1)
                    own(nc.vector.memset(best[:, TOPK:8], NOWHERE))
                    dve.sem_inc(wait_carrier, 1)
                    own(nc.vector.match_replace(lr[:], best[:], lg[:], -NOWHERE))
                    dve.wait_ge(ev["rk"], last)
                    nc.vector.tensor_tensor(mask[:], lr[:], lg[:], ALU.not_equal).then_inc(ev["mask"], 1)
                    dve.wait_ge(ev["mask"], now)
                    dve.wait_ge(ev["ex"], now)
                    own(nc.vector.tensor_tensor(W[:], ex[:], mask[:], ALU.mult))
                    own(nc.vector.tensor_reduce(den[:], W[:], AX_X, ALU.add))
                    own(nc.vector.reciprocal(den[:], den[:]))
                    nc.vector.tensor_scalar(W[:], W[:], den[:], None, ALU.mult).then_inc(ev["W"], 1)
                    dve.wait_ge(ev["rk"], now)
                    own(nc.vector.tensor_tensor(rkf[:], sm[:, E:2 * E], run[:], ALU.add))
                    own(nc.vector.tensor_tensor(run[:], sm[:, 2 * E:3 * E], run[:], ALU.add))
                    own(nc.vector.tensor_copy(ri[:], rkf[:]))
                    own(nc.vector.tensor_scalar(ra[:], ri[:], P - 1, 9, ALU.bitwise_and, ALU.logical_shift_left))
                    own(nc.vector.tensor_scalar(rb[:], ri[:], 7, None, ALU.logical_shift_right))
                    own(nc.vector.tensor_tensor(kf[:], ra[:], rb[:], ALU.add))
                    own(nc.vector.scalar_tensor_tensor(out=kf[:], in0=kf[:], scalar=1.0, in1=const("expert_row"),
                                                       op0=ALU.add, op1=ALU.add))
                    own(nc.vector.tensor_tensor(key[:], kf[:], mask[:], ALU.mult))
                    dve.sem_inc(wait_carrier, 1)
                    own(nc.vector.max(top[:], key[:]))
                    dve.wait_ge(ev["stored"], last)
                    own(nc.vector.tensor_scalar(idx[:], top[:, 0:TOPK], 1.0, None, ALU.subtract))
                    dve.wait_ge(ev["W"], now)
                    for c in range(TOPK):
                        own(nc.vector.scalar_tensor_tensor(out=pick[:], in0=key[:], scalar=top[:, c:c + 1], in1=W[:],
                                                           op0=ALU.is_equal, op1=ALU.mult, accum_out=wj[:, c:c + 1]))
                    own(nc.vector.tensor_copy(rec[:, :, 0], const("token")[:, bass.ds(i, 1)].to_broadcast([P, TOPK])))
                    nc.vector.tensor_copy(rec[:].bitcast(F32)[:, :, 1], wj[:]).then_inc(ev["rec"], 1)
                    dve.wait_ge(ev["bd"], now)
                    own(nc.vector.tensor_tensor(yi[:], acc[:].rearrange("p a n -> p (a n)"), g2[:], ALU.mult))
                    nc.vector.tensor_tensor(yi[:], yi[:], x2[:], ALU.add).then_inc(ev["yi"], 1)
                own.check()

            fin = Steps(dve, k.sem("fin"))
            fin(nc.vector.tensor_tensor(over[:], run[:].unsqueeze(2).to_broadcast([P, E, NT]),
                                        const("tile_from").unsqueeze(1).to_broadcast([P, E, NT]), ALU.is_gt))
            fin(nc.vector.tensor_reduce(tiles[:], over[:], AX_X, ALU.add))
            fin(nc.vector.tensor_reduce(groups[:], over[:].rearrange("p e (g t) -> p e g t", t=GT)[:, :, :, 0], AX_X, ALU.add))
            dve.sem_inc(table_ready, 1)
            dve.wait_ge(table_t, 1)
            fin(nc.vector.tensor_copy(gT[:], wt[0:E, 0:P]))
            fin(nc.vector.tensor_copy(tT[:], wt[0:E, P:2 * P]))
            dve.sem_inc(table_ready, 1)
            dve.wait_ge(table_t, 2)
            fin(nc.vector.tensor_copy(cumg[:], sm[:, 0:E]))
            fin(nc.vector.tensor_copy(cumt[:], sm[:, E:2 * E]))
            number, expert = const("number"), col[:, 1:2]
            fin(nc.vector.tensor_scalar(sel[:], cumg[:], number, None, ALU.is_le))
            fin(nc.vector.tensor_reduce(expert, sel[:], AX_X, ALU.add))
            fin(nc.vector.tensor_scalar(sel[:], const("expert"), expert, None, ALU.is_equal))
            fin(nc.vector.tensor_tensor(cumg[:], cumg[:], groups[:], ALU.subtract))
            for c, src in ((2, cumg), (3, tiles), (4, cumt)):
                fin(nc.vector.tensor_tensor(pick[:], sel[:], src[:], ALU.mult))
                fin(nc.vector.tensor_reduce(col[:, c:c + 1], pick[:], AX_X, ALU.add))
            fin(nc.vector.tensor_tensor(col[:, 5:6], number, col[:, 2:3], ALU.subtract))
            fin(nc.vector.tensor_scalar(col[:, 5:6], col[:, 5:6], float(GT), None, ALU.mult))
            fin(nc.vector.tensor_tensor(col[:, 6:7], col[:, 3:4], col[:, 5:6], ALU.subtract))
            fin(nc.vector.tensor_scalar(table[:, 1:2], col[:, 6:7], float(GT), 0.0, ALU.min, ALU.max))
            fin(nc.vector.tensor_scalar(col[:, 7:8], table[:, 1:2], 0.0, None, ALU.is_gt))
            fin(nc.vector.tensor_tensor(table[:, 0:1], expert, col[:, 7:8], ALU.mult))
            fin(nc.vector.tensor_tensor(col[:, 4:5], col[:, 4:5], col[:, 5:6], ALU.add))
            fin(nc.vector.tensor_tensor(table[:, 2:3], col[:, 4:5], col[:, 7:8], ALU.mult))
            fin(nc.vector.scalar_tensor_tensor(out=col[:, 6:7], in0=expert, scalar=float(NT), in1=col[:, 5:6],
                                               op0=ALU.mult, op1=ALU.add))
            fin(nc.vector.tensor_tensor(table[:, 3:4], col[:, 6:7], col[:, 7:8], ALU.mult))
            nc.vector.tensor_copy(table_i[:], table[:]).then_inc(table_step, 1)

        @block.tensor
        def _(pe):
            ident = const("ident")
            pe.wait_ge(wlo_done, 2)
            pe.wait_ge(setup_dma, 7 * 16)
            with pe.Fori(0, NT // 2) as j:
                for u in range(2):
                    i = j * 2 + u
                    now, last = i + 3, i + 2
                    pe.wait_ge(o_in[u], (j + 1) * 16)
                    pe.wait_ge(ev["olo"], i * 2 + 2)
                    for s in range(KD):
                        mm = nc.tensor.transpose(tp[:, s], o[:, u, s * P:(s + 1) * P], ident)
                    mm.then_inc(ev["t1"], 1)
                    pe.wait_ge(ev["olo"], i * 2 + 4)
                    pe.wait_ge(ev["yi"], last)
                    for c in range(2):
                        for s in range(KD):
                            mm = split_product(nc, acc[:, c], ohi[:, s], olo[:, s], whi[:, c, s], wlo[:, c, s],
                                               s == 0, s == KD - 1)
                    mm.then_inc(ev["mm"], 1)
                    pe.wait_ge(ev["h2"], now)
                    pe.wait_ge(ev["h2t"], last)
                    for s in range(KD):
                        mm = nc.tensor.transpose(tq[:, s], h2[:, s * P:(s + 1) * P], ident)
                    mm.then_inc(ev["t2"], 1)
                    pe.wait_ge(ev["h2t"], now)
                    pe.wait_ge(ev["rec"], last)
                    for s in range(KD):
                        mm = nc.tensor.matmul(sm[:, 0:E], h2T[:, s], wr[:, s], start=(s == 0), stop=(s == KD - 1))
                    mm.then_inc(ev["lg"], 1)
                    pe.wait_ge(ev["mask"], now)
                    nc.tensor.matmul(sm[:, E:2 * E], const("before"), mask[:], start=True, stop=True)
                    nc.tensor.matmul(sm[:, 2 * E:3 * E], const("ones"), mask[:], start=True, stop=True).then_inc(ev["rk"], 1)
                    pe.wait_ge(ev["W"], now)
                    pe.wait_ge(ev["wtc"], last)
                    nc.tensor.transpose(wt[0:E, 0:P], W[:], ident).then_inc(ev["wt"], 1)
                    pe.wait_ge(ev["wtc"], now)
                    pe.wait_ge(ev["x2"], now)
                    for c in range(2):
                        mm = nc.tensor.matmul(acc[:, c], wT[:], bd[:, c * N:(c + 1) * N], start=True, stop=True)
                    mm.then_inc(ev["bd"], 1)
            pe.wait_ge(table_ready, 1)
            nc.tensor.transpose(wt[0:E, 0:P], groups[:], ident)
            nc.tensor.transpose(wt[0:E, P:2 * P], tiles[:], ident).then_inc(table_t, 1)
            pe.wait_ge(table_ready, 2)
            nc.tensor.matmul(sm[:, 0:E], gT[:], const("causal")[0:E, 0:E], start=True, stop=True)
            nc.tensor.matmul(sm[:, E:2 * E], tT[:], const("before")[0:E, 0:E], start=True, stop=True).then_inc(table_t, 1)


def phase_experts(nc, k, A, keep):
    const = keep["const"]
    NCH, NGU, H = 6, 4, N // 2
    RAW = 3
    raw = k.sb("w_raw", [P, RAW, KD, H])
    whi, wlo = (k.sb(n, [P, 2, KD, N], F32R) for n in ("w_hi", "w_lo"))
    bias = k.sb("bias", [P, 2, D])
    g2 = k.sb("g2", [P, D])
    xs = k.sb("rows", [P, GT, D])
    xhi, xlo = (k.sb(n, [P, GT, KD, P], F32R) for n in ("x_hi", "x_lo"))
    ahi, alo = (k.sb(n, [P, GT, KD, P], F32R) for n in ("a_hi", "a_lo"))
    gu = k.sb("gate_up", [P, 2, N])
    sg = k.sb("sigmoid", [P, 2, H])
    act_row = k.sb("act_row", [P, GT, H])
    weighted = k.sb("weighted", [P, GT, N])
    rec_next, rec_now = k.sb("rec_next", [P, GT, 2], I32), k.sb("rec_now", [P, GT, 2], I32)
    table = k.sb("table", [1, 4 * P], I32)
    acc = k.ps("acc", [P, 5, N])
    tx = k.ps("tx", [P, 2, 4, P])
    ta = k.ps("ta", [P, 2, P])
    (table_in, g2_in, bias_in, hi_done, lo_done, mm_done, read_done, sg_in, sg_done, act_done, ta_done, ahi_done,
     alo_done, tx_done, xhi_done, xlo_done, weighted_done, rec_next_in, rec_now_in, rec_used, rows_in, y_out, y_added,
     dve_step, wait_carrier, sg_set) = k.sems(
         "table_in g2_in bias_in hi_done lo_done mm_done read_done sg_in sg_done act_done ta_done ahi_done "
         "alo_done tx_done xhi_done xlo_done weighted_done rec_next_in rec_now_in rec_used rows_in y_out y_added "
         "dve_step wait_carrier sg_set")
    raw_in = [k.sem(f"raw_in{s}") for s in range(RAW)]
    gu_w = A["w_gu"].rearrange("o e (s p) n -> p (o e) s n", p=P)
    dn_w = A["w_down"].rearrange("o e (s p) n -> p (o e) s n", p=P)
    gu_b = A["b_gu"].rearrange("o e n -> (o e) n")
    places = keep["places"].rearrange("(p q) c -> p q c", p=P)

    def bank(c, t):
        return c % 2 if t == 0 else t + 1

    def field(eng, g, f, most):
        return eng.value_load(table[0:1, bass.ds(g * 4 + f, 1)], min_val=0, max_val=most)

    EXPERT, TILES, BEFORE, PLACE = range(4)

    class Group:

        def __init__(self, eng, g):
            self.T = field(eng, g, TILES, GT)
            self.before = field(eng, g, BEFORE, NG * GT)
            self.g = g

        def chunk_tile(self, c, t):
            return self.before * NCH + self.T * c + (t + 2)

        def chunks_before(self, c):
            return self.before * NCH + self.T * c + 1

        def gu_tile(self, c, t):
            return self.before * NGU + self.T * c + (t + 2)

        def down_tile(self, c, t):
            return self.before * 2 + self.T * (c - NGU) + (t + 2)

        def halves(self, n):
            return self.g * (2 * NCH) + (n + RAW)

    with nc.Block() as block:

        @block.sync
        def _(sp):
            sp.dma_start(table[:], keep["groups"].rearrange("g f -> (g f)").unsqueeze(0)).then_inc(table_in, 16)
            sp.dma_start(g2[:], keep["g2"]).then_inc(g2_in, 16)
            sp.sem_inc(lo_done, RAW)
            sp.sem_inc(read_done, 1)
            sp.sem_inc(mm_done, 1)
            sp.wait_ge(table_in, 16)
            with sp.Fori(0, NG) as g:
                G = Group(sp, g)
                expert = field(sp, g, EXPERT, E - 1)
                with sp.If(G.T > 0):
                    for n in range(2 * NCH):
                        c, half = n // 2, n % 2
                        if n == 0:
                            sp.wait_ge(act_done, G.before * NGU + 1)
                            sp.dma_start(bias[:].rearrange("p a n -> p (a n)"),
                                         gu_b[bass.ds(expert, 1), :].rearrange("o n -> (o n)").partition_broadcast(P)
                                         ).then_inc(bias_in, 16)
                        sp.wait_ge(lo_done, G.halves(n - RAW + 1))
                        w, col = (gu_w, half * D + c * H) if c < NGU else (dn_w, (c - NGU) * N + half * H)
                        sp.dma_start(raw[:, n % RAW], w[:, bass.ds(expert, 1), :, col:col + H]
                                     ).then_inc(raw_in[n % RAW], 16)
                    sp.nop()

        @block.gpsimd
        def _(pool):
            pool.wait_ge(table_in, 16)
            for s in (ta_done, alo_done, weighted_done, y_added, act_done, rec_used):
                pool.sem_inc(s, 1)
            pool.sem_inc(tx_done, 1)

            def fetch_rows(g, T, place, before):
                pool.dma_start(rec_next[:], places[:, bass.ds(place, GT), :]).then_inc(rec_next_in, 16)
                pool.wait_ge(rec_next_in, (g + 1) * 16)
                pool.sem_inc(wait_carrier, 1)
                for t in range(GT):
                    with pool.If(T > t):
                        pool.indirect_dma_start(out=xs[:, t], out_offset=None, in_=keep["h2"],
                                                in_offset=bass.IndirectOffsetOnAxis(ap=rec_next[:, t, 0:1], axis=0)
                                                ).then_inc(rows_in, 16)
                pool.wait_ge(rows_in, (before + T) * 16)
                pool.sem_inc(wait_carrier, 1)

            T0 = field(pool, 0, TILES, GT)
            fetch_rows(0, T0, 0, 0)
            with pool.Fori(0, NG) as g:
                G = Group(pool, g)
                place = field(pool, g, PLACE, PLACES - GT)
                nT, nbefore, nplace = field(pool, g + 1, TILES, GT), field(pool, g + 1, BEFORE, NG * GT), field(pool, g + 1, PLACE, PLACES - GT)
                with pool.If(G.T > 0):
                    pool.wait_ge(rec_used, g + 1)
                    pool.sem_inc(wait_carrier, 1)
                    pool.dma_start(rec_now[:], places[:, bass.ds(place, GT), :]).then_inc(rec_now_in, 16)
                    pool.wait_ge(rec_now_in, (g + 1) * 16)
                    pool.sem_inc(wait_carrier, 1)
                    with pool.If(nT > 0):
                        pool.wait_ge(tx_done, G.before + G.T + 1)
                        pool.sem_inc(wait_carrier, 1)
                        fetch_rows(g + 1, nT, nplace, nbefore)
                    for c in (NGU, NGU + 1):
                        for t in range(GT):
                            with pool.If(G.T > t):
                                pool.wait_ge(weighted_done, G.down_tile(c, t))
                                pool.sem_inc(wait_carrier, 1)
                                pool.indirect_dma_start(
                                    out=keep["y"][c - NGU],
                                    out_offset=bass.IndirectOffsetOnAxis(ap=rec_now[:, t, 0:1], axis=0),
                                    in_=weighted[:, t], in_offset=None, compute_op=ALU.add).then_inc(y_out, 16)
                                pool.wait_ge(y_out, (G.down_tile(c, t) - 1) * 16)
                                pool.sem_inc(y_added, 1)
                    pool.sem_inc(wait_carrier, 1)

        @block.scalar
        def _(act):
            act.wait_ge(table_in, 16)

            def weights_hi(g, n, freed):
                act.wait_ge(raw_in[n % RAW], (g * (2 * NCH // RAW) + n // RAW + 1) * 16)
                act.wait_ge(mm_done, freed)
                c, half = n // 2, n % 2
                nc.scalar.copy(whi[:, c % 2, :, half * H:(half + 1) * H], raw[:, n % RAW]).then_inc(hi_done, 1)

            def rows_hi(base, t):
                act.wait_ge(tx_done, base + (t + 2))
                for b in range(2):
                    nc.scalar.copy(xhi[:, t, 4 * b:4 * b + 4], tx[:, b]).then_inc(xhi_done, 1)

            nc.scalar.activation(sg[:, 0, 0:1], const("eps"), ACT.Sigmoid).then_inc(sg_set, 1)
            act.wait_ge(sg_set, 1)
            for half in range(2):
                weights_hi(0, half, 1)
            T0 = field(act, 0, TILES, GT)
            for t in range(GT):
                with act.If(T0 > t):
                    rows_hi(0, t)
            with act.Fori(0, NG) as g:
                G = Group(act, g)
                nT = field(act, g + 1, TILES, GT)
                with act.If(G.T > 0):

                    def activations_hi(c, t):
                        act.wait_ge(ta_done, G.gu_tile(c, t))
                        nc.scalar.copy(ahi[:, t, 2 * c:2 * c + 2], ta[:]).then_inc(ahi_done, 1)

                    def next_rows_hi(t):
                        with act.If(nT > t):
                            rows_hi(G.before + G.T, t)

                    for c in range(NGU):
                        for half in range(2):
                            weights_hi(g, 2 * (c + 1) + half, G.chunks_before(c))
                        for t in range(GT):
                            with act.If(G.T > t):
                                if c >= 1:
                                    activations_hi(c - 1, t)
                                act.wait_ge(sg_in, G.gu_tile(c, t) - 1)
                                nc.scalar.activation(sg[:, t % 2], gu[:, t % 2, 0:H], ACT.Sigmoid,
                                                     scale=SIG).then_inc(sg_done, 1)
                    weights_hi(g, 2 * NCH - 2, G.chunks_before(NGU))
                    activations_hi(NGU - 1, 0)
                    next_rows_hi(0)
                    weights_hi(g, 2 * NCH - 1, G.chunks_before(NGU))
                    for t in range(1, GT):
                        with act.If(G.T > t):
                            activations_hi(NGU - 1, t)
                    for half in range(2):
                        next_rows_hi(1 + half)
                        with act.If(nT > 0):
                            weights_hi(g + 1, half, G.chunks_before(NGU + 1))
                    next_rows_hi(3)
                    act.nop()

        @block.vector
        def _(dve):
            dve.wait_ge(table_in, 16)
            dve.wait_ge(g2_in, 16)

            def weights_lo(g, n, freed):
                dve.wait_ge(hi_done, g * (2 * NCH) + n + 1)
                dve.wait_ge(mm_done, freed)
                c, half = n // 2, n % 2
                cols = slice(half * H, (half + 1) * H)
                nc.vector.tensor_tensor(wlo[:, c % 2, :, cols], raw[:, n % RAW], whi[:, c % 2, :, cols],
                                        ALU.subtract).then_inc(lo_done, 1)

            def rows_lo(base, t):
                for b in range(2):
                    dve.wait_ge(xhi_done, base * 2 + (2 * t + b + 1))
                    nc.vector.tensor_tensor(xlo[:, t, 4 * b:4 * b + 4], tx[:, b], xhi[:, t, 4 * b:4 * b + 4],
                                            ALU.subtract).then_inc(xlo_done, 1)

            def swiglu(G, g, c, t):
                if t == 0 and c == 0:
                    dve.wait_ge(bias_in, (g + 1) * 16)
                u = t % 2
                dve.wait_ge(act_done, G.gu_tile(c, t) - 1)
                dve.wait_ge(mm_done, G.chunk_tile(c, t))
                nc.vector.tensor_tensor(gu[:, u].rearrange("p (a n) -> p a n", a=2),
                                        acc[:, bank(c, t)].rearrange("p (a n) -> p a n", a=2),
                                        bias[:, :, c * H:(c + 1) * H], ALU.add).then_inc(read_done, 1)
                dve.wait_ge(read_done, G.chunk_tile(c, t))
                nc.vector.tensor_scalar(gu[:, u, 0:H], gu[:, u, 0:H], LIMIT, None, ALU.min).then_inc(sg_in, 1)
                nc.vector.tensor_scalar(gu[:, u, H:N], gu[:, u, H:N], LIMIT, -LIMIT, ALU.min, ALU.max).then_inc(dve_step, 1)
                dve.wait_ge(sg_done, G.gu_tile(c, t) - 1)
                nc.vector.tensor_tensor(gu[:, u, 0:H], gu[:, u, 0:H], sg[:, u], ALU.mult).then_inc(dve_step, 1)
                dve.wait_ge(dve_step, (G.gu_tile(c, t) - 1) * 2)
                nc.vector.scalar_tensor_tensor(out=act_row[:, t], in0=gu[:, u, H:N], scalar=1.0, in1=gu[:, u, 0:H],
                                               op0=ALU.add, op1=ALU.mult).then_inc(act_done, 1)

            for half in range(2):
                weights_lo(0, half, 1)
            T0 = field(dve, 0, TILES, GT)
            for t in range(GT):
                with dve.If(T0 > t):
                    rows_lo(0, t)
            with dve.Fori(0, NG) as g:
                G = Group(dve, g)
                nT = field(dve, g + 1, TILES, GT)
                with dve.If(G.T > 0):

                    def activations_lo(c, t):
                        dve.wait_ge(ahi_done, G.gu_tile(c, t) - 1)
                        nc.vector.tensor_tensor(alo[:, t, 2 * c:2 * c + 2], ta[:], ahi[:, t, 2 * c:2 * c + 2],
                                                ALU.subtract).then_inc(alo_done, 1)

                    def weigh(c, t):
                        dve.wait_ge(mm_done, G.chunk_tile(c, t))
                        dve.wait_ge(y_added, G.before * 2 + (t + 2 if c > NGU else 1))
                        cols = slice((c - NGU) * N, (c - NGU + 1) * N)
                        nc.vector.scalar_tensor_tensor(
                            out=weighted[:, t], in0=acc[:, bank(c, t)], scalar=rec_now[:].bitcast(F32)[:, t, 1:2],
                            in1=g2[:, cols], op0=ALU.mult, op1=ALU.mult).then_inc(weighted_done, 1)
                        dve.wait_ge(weighted_done, G.down_tile(c, t))
                        dve.sem_inc(read_done, 1)

                    def next_rows_lo(t):
                        with dve.If(nT > t):
                            rows_lo(G.before + G.T, t)

                    for c in range(NGU):
                        for half in range(2):
                            weights_lo(g, 2 * (c + 1) + half, G.chunks_before(c))
                        for t in range(GT):
                            with dve.If(G.T > t):
                                if c >= 1:
                                    activations_lo(c - 1, t)
                                swiglu(G, g, c, t)
                    weights_lo(g, 2 * NCH - 2, G.chunks_before(NGU))
                    activations_lo(NGU - 1, 0)
                    next_rows_lo(0)
                    weights_lo(g, 2 * NCH - 1, G.chunks_before(NGU))
                    dve.wait_ge(rec_now_in, (g + 1) * 16)
                    dve.sem_inc(wait_carrier, 1)
                    weigh(NGU, 0)
                    for t in range(1, GT):
                        with dve.If(G.T > t):
                            activations_lo(NGU - 1, t)
                            weigh(NGU, t)
                    for half in range(2):
                        next_rows_lo(1 + half)
                        with dve.If(nT > 0):
                            weights_lo(g + 1, half, G.chunks_before(NGU + 1))
                    for t in range(GT):
                        with dve.If(G.T > t):
                            weigh(NGU + 1, t)
                    next_rows_lo(3)
                    dve.sem_inc(rec_used, 1)

        @block.tensor
        def _(pe):
            ident = const("ident")
            pe.wait_ge(table_in, 16)

            def rows(t):
                for s in range(KD):
                    mm = nc.tensor.transpose(tx[:, s // 4, s % 4], xs[:, t, s * P:(s + 1) * P], ident)
                mm.then_inc(tx_done, 1)

            def activations(G, c, t):
                pe.wait_ge(act_done, G.gu_tile(c, t))
                pe.wait_ge(alo_done, G.gu_tile(c, t) - 1)
                for s in range(2):
                    mm = nc.tensor.transpose(ta[:, s], act_row[:, t, s * P:(s + 1) * P], ident)
                mm.then_inc(ta_done, 1)

            T0 = field(pe, 0, TILES, GT)
            pe.sem_inc(xlo_done, 2)
            for t in range(GT):
                with pe.If(T0 > t):
                    if t == 0:
                        pe.wait_ge(rows_in, T0 * 16)
                    pe.wait_ge(xlo_done, 2 * t + 2)
                    rows(t)
            with pe.Fori(0, NG) as g:
                G = Group(pe, g)
                nT = field(pe, g + 1, TILES, GT)
                with pe.If(G.T > 0):

                    def next_rows(t):
                        with pe.If(nT > t):
                            if t == 0:
                                pe.wait_ge(rows_in, (G.before + G.T + nT) * 16)
                            pe.wait_ge(xlo_done, (G.before + G.T) * 2 + (2 * t + 2))
                            rows(t)

                    for c in range(NCH):
                        pe.wait_ge(lo_done, G.halves(2 * c + 2))
                        for t in range(GT):
                            with pe.If(G.T > t):
                                if c == 0:
                                    pe.wait_ge(xlo_done, G.before * 2 + (2 * t + 4))
                                    pe.wait_ge(read_done, G.chunks_before(0))
                                elif t == 0:
                                    if c >= 2:
                                        pe.wait_ge(read_done, G.chunk_tile(c - 2, 0))
                                else:
                                    pe.wait_ge(read_done, G.chunk_tile(c - 1, t))
                                a_hi, a_lo = (xhi, xlo) if c < NGU else (ahi, alo)
                                for s in range(KD):
                                    if c == NGU and s == 0:
                                        if t > 0:
                                            activations(G, NGU - 1, t)
                                        else:
                                            with pe.If(G.T > 1):
                                                activations(G, NGU - 1, t)
                                    if c == NGU and t == 0 and s == 2 * (NGU - 2):
                                        pe.wait_ge(alo_done, G.gu_tile(NGU - 1, 0) - 1)
                                    if c == NGU and s == 2 * (NGU - 1):
                                        if t == 0:
                                            with pe.If(G.T < 2):
                                                activations(G, NGU - 1, t)
                                            next_rows(0)
                                        pe.wait_ge(alo_done, G.gu_tile(NGU - 1, t))
                                    if c == NGU + 1 and t == 0 and s in (2, 6):
                                        next_rows(s // 4 + 1)
                                    mm = split_product(nc, acc[:, bank(c, t)], a_hi[:, t, s], a_lo[:, t, s],
                                                       whi[:, c % 2, s], wlo[:, c % 2, s], s == 0, s == KD - 1)
                                mm.then_inc(mm_done, 1)
                                if 1 <= c < NGU:
                                    activations(G, c - 1, t)
                    next_rows(3)
                    pe.nop()


def phase_finish(nc, k, A, keep):
    const = keep["const"]
    SLOTS = 4
    y, z = k.sb("y", [P, SLOTS, D]), k.sb("z", [P, SLOTS, D])
    squares = k.sb("squares", [P, D], mybir.dt.bfloat16)
    nf = k.sb("norm_f", [P, D])
    ssq, rms, rinv = (k.sb(n, [P, NT]) for n in ("ssq", "rms", "rinv"))
    nf_in, sq_done, rms_done, inv_done, done = k.sems("nf_in sq_done rms_done inv_done done")
    y_in = [k.sem(f"y_in{s}") for s in range(SLOTS)]
    out_done = [k.sem(f"out_done{s}") for s in range(SLOTS)]
    y_t = [a.rearrange("(t p) n -> p t n", p=P) for a in keep["y"]]
    out_t = keep["out"].rearrange("o (t p) d -> p (o t) d", p=P)
    with nc.Block() as block:

        @block.sync
        def _(sp):
            sp.dma_start(nf[:], A["norm_f"].partition_broadcast(P)).then_inc(nf_in, 16)
            for i in range(NT):
                if i >= SLOTS:
                    sp.wait_ge(done, i - SLOTS + 1)
                for half in range(2):
                    sp.dma_start(y[:, i % SLOTS, half * N:(half + 1) * N], y_t[half][:, i]).then_inc(y_in[i % SLOTS], 16)

        @block.scalar
        def _(act):
            for i in range(NT):
                act.wait_ge(y_in[i % SLOTS], 32 * (i // SLOTS + 1))
                nc.scalar.activation(squares[:], y[:, i % SLOTS], ACT.Square, accum_out=ssq[:, i:i + 1]).then_inc(sq_done, 1)
                act.wait_ge(sq_done, i + 1)
                nc.scalar.activation(rms[:, i:i + 1], ssq[:, i:i + 1], ACT.Sqrt, scale=1.0 / D,
                                     bias=const("eps")).then_inc(rms_done, 1)

        @block.vector
        def _(dve):
            dve.wait_ge(nf_in, 16)
            for i in range(NT):
                s = i % SLOTS
                dve.wait_ge(rms_done, i + 1)
                nc.vector.reciprocal(rinv[:, i:i + 1], rms[:, i:i + 1]).then_inc(inv_done, 1)
                dve.wait_ge(inv_done, i + 1)
                if i >= SLOTS:
                    dve.wait_ge(out_done[s], 16 * (i // SLOTS))
                nc.vector.scalar_tensor_tensor(out=z[:, s], in0=y[:, s], scalar=rinv[:, i:i + 1], in1=nf[:],
                                               op0=ALU.mult, op1=ALU.mult).then_inc(done, 1)

        @block.gpsimd
        def _(pool):
            for i in range(NT):
                pool.wait_ge(done, i + 1)
                pool.dma_start(out_t[:, i], z[:, i % SLOTS]).then_inc(out_done[i % SLOTS], 16)
            for s in range(SLOTS):
                pool.wait_ge(out_done[s], 16 * (NT // SLOTS))


def program(nc, A, out):
    def dram(name, shape, dt=F32):
        return nc.dram_tensor(name, shape, dt, kind="Internal").ap()

    with ExitStack() as ctx:
        k = Kit(nc, ctx, "keep")
        keep = {n: dram(n + "_rep", (P, D)) for n in ("g1", "sh2", "A2", "g2")}
        keep["proj"] = dram("proj", (S, PROJ))
        keep["o"] = dram("mixed", (S + P, D))
        keep["h2"] = dram("h2_rows", (ROWS, D))
        keep["y"] = [dram(f"y_rows{half}", (ROWS, N)) for half in range(2)]
        keep["places"] = dram("places", (P * PLACES, 2), I32)
        keep["groups"] = dram("groups", (P, 4), I32)
        keep["const_all"] = k.sb("const", [P, sum(w for _, w in CONST_AT.values())])
        keep["const"] = lambda name: keep["const_all"][:, CONST_AT[name][0]:sum(CONST_AT[name])]
        keep["out"] = out

        def run(phase):
            with ExitStack() as c:
                k = Kit(nc, c, phase.__name__[6:9])
                phase(nc, k, A, keep)
                k.clear_sems()

        with ExitStack() as mixing:
            keep["glr_t"] = Kit(nc, mixing, "mixing").sb("glr_t", [RANK + 1, S])
            with ExitStack() as early:
                ke = Kit(nc, early, "early")
                keep["A1"], keep["sh1"] = ke.sb("A1", [P, D]), ke.sb("sh1", [P, D])
                run(phase_modulation)
                run(phase_projection)
            run(phase_mixer)
        run(phase_routing)
        run(phase_experts)
        run(phase_finish)


_INS = ['x', 'c', 'positions', 'w_ada', 'b_ada', 'norm1', 'w_in', 'w_gk2', 'b_gk', 'gla_onorm', 'ret_onorm', 'w_out',
        'norm2', 'w_router', 'b_router', 'w_gu', 'b_gu', 'w_down', 'b_down', 'norm_f']


def kernel(**inputs):
    import concourse.bacc as bacc
    from concourse.bass_utils import run_bass_kernel_spmd

    nc = bacc.Bacc("TRN2", target_bir_lowering=False, num_devices=1)
    arrays = {n: np.ascontiguousarray(inputs[n]) for n in _INS}
    arrays["const"] = constants()[0]
    A = {n: nc.dram_tensor("in_" + n, a.shape, mybir.dt.from_np(a.dtype), kind="ExternalInput").ap()
         for n, a in arrays.items()}
    out = nc.dram_tensor("out", (1, S, D), F32, kind="ExternalOutput").ap()
    program(nc, A, out)
    r = run_bass_kernel_spmd(nc, [{"in_" + n: a for n, a in arrays.items()}], core_ids=[0])
    return r.results[0]["out"]
```

```python
from contextlib import ExitStack

import numpy as np
import concourse.bass as bass
from concourse import mybir

P = 128
F32 = mybir.dt.float32
F32R = mybir.dt.float32r
I32 = mybir.dt.int32
ALU = mybir.AluOpType
ACT = mybir.ActivationFunctionType
AX_X = mybir.AxisListType.X

D = 1024
S = 2048
NT = S // P
KD = D // P
N = 512
EPS = 1e-6

GH, GDK, GDV, RANK = 4, 64, 128, 16
RH, RDK = 4, 128
GATE_NORM = 16.0
SUB = 32
ROPE_BASE = 10000.0
PROJ = 3584
NC_IN = PROJ // N
GLR = 1536
C_GQ, C_GK, C_GV, C_GG = 0, 256, 512, 1024
C_RQ, C_RK, C_RV, C_RG = 1536, 2048, 2560, 3072

E = 32
TOPK = 4
GT = 4
ROWS = S + P
PLACES = E * NT
NG = (S * TOPK - E) // (GT * P) + E
LIMIT = 7.0
SIG = 1.702



def w_in_column(chunk):
    return chunk * N + (RANK if chunk * N >= GLR else 0)


class Kit:

    def __init__(self, nc, ctx, phase):
        self.nc, self.ctx, self.phase, self.signals = nc, ctx, phase, []

    def sb(self, name, shape, dt=F32):
        return self.ctx.enter_context(self.nc.sbuf_tensor(f"{self.phase}_{name}", shape, dt))

    def ps(self, name, shape):
        return self.ctx.enter_context(self.nc.psum_tensor(f"{self.phase}_bank_{name}", shape, F32))

    def sem(self, name):
        self.signals.append(self.nc.alloc_semaphore(f"{self.phase}_{name}"))
        return self.signals[-1]

    def sems(self, names):
        return [self.sem(n) for n in names.split()]

    def clear_sems(self):
        self.nc.clear_and_free_semaphores(self.signals)
        self.nc.all_engine_barrier()


class Steps:

    def __init__(self, eng, sem, per_turn=0):
        self.eng, self.sem, self.per_turn, self.base, self.n = eng, sem, per_turn, 0, 0

    def turn(self, i):
        self.base, self.n = i * self.per_turn, 0

    def __call__(self, ins):
        ins.then_inc(self.sem, 1)
        self.n += 1
        self.eng.wait_ge(self.sem, self.base + self.n)

    def check(self):
        assert self.n == self.per_turn, (self.n, self.per_turn)


def split_product(nc, out, act_hi, act_lo, w_hi, w_lo, first, last):
    nc.tensor.matmul(out, act_hi, w_hi, start=first, stop=False)
    nc.tensor.matmul(out, act_hi, w_lo, start=False, stop=False)
    return nc.tensor.matmul(out, act_lo, w_hi, start=False, stop=last)


def for_tiles(eng, step):
    for u in range(2):
        step(u, u, 0)
    with eng.Fori(1, NT // 2 - 1) as j:
        for u in range(2):
            step(j * 2 + u, u, j)
    for u in range(2):
        step(NT - 2 + u, u, NT // 2 - 1)


def is_tile(i, n):
    return isinstance(i, int) and i == n


def load_ln_exp(nc):
    nc.scalar.add_instruction(mybir.InstLoadActFuncSet(act_func_set_id=6, name=nc.get_next_instruction_name(),
                                                       engine=mybir.EngineType.Activation))


def tiles_of(ap):
    return ap.rearrange("o (t p) d -> p (o t) d", p=P)


def rows_of(ap):
    return ap.rearrange("o (s p) n -> p (o s) n", p=P)


def row(ap, n=P):
    return ap.rearrange("o n -> (o n)").partition_broadcast(n)


def constants():
    p = np.arange(P, dtype=np.float64)
    s, t = p[:, None], p[None, :]
    parts = {}
    parts["ident"] = (s == t).astype(np.float64)
    parts["ones"] = np.ones((P, P))
    parts["before"] = (s < t).astype(np.float64)
    parts["causal"] = (s <= t).astype(np.float64)
    parts["expert"] = np.broadcast_to(np.arange(E), (P, E))
    parts["expert_row"] = np.broadcast_to(np.arange(E) * NT, (P, E))
    parts["tile_from"] = np.broadcast_to(np.arange(NT) * P, (P, NT))
    parts["number"] = p[:, None]
    parts["eps"] = np.full((P, 1), EPS)
    parts["token"] = p[:, None] + P * np.arange(NT)[None, :]
    parts["sum_to"] = (s <= t) / GATE_NORM
    parts["sum_after"] = (s > t) / GATE_NORM
    log_gamma = np.log(1.0 - 2.0 ** (-5.0 - np.arange(RH)))
    rel = (t - s)[:, None, :] * log_gamma[None, :, None]
    parts["decay"] = (np.where((t >= s)[:, None, :], np.exp(np.minimum(rel, 0.0)), 0.0) * RDK ** -0.5).reshape(P, -1)
    parts["xi"] = np.broadcast_to(np.exp((p + 1)[None, None, :] * log_gamma[None, :, None]), (P, RH, P)).reshape(P, -1)
    parts["zeta"] = np.exp((P - 1 - p)[:, None] * log_gamma[None, :]) * RDK ** -0.5
    half = RDK // 2
    inv = (np.float32(ROPE_BASE) ** (-np.arange(half, dtype=np.float32) / np.float32(half))).astype(np.float32)
    parts["inv_freq"] = np.broadcast_to(inv, (P, half))
    at, n = {}, 0
    for name, a in parts.items():
        at[name] = (n, a.shape[1])
        n += a.shape[1]
    return np.concatenate([np.asarray(a, np.float32) for a in parts.values()], axis=1), at


CONST_AT = constants()[1]
CONST_SHARED = CONST_AT["sum_to"][0]
GAMMA_TILE = [float(np.exp(P * np.log(1.0 - 2.0 ** (-5.0 - h)))) for h in range(RH)]


def phase_modulation(nc, k, A, keep):
    W_SLOTS = 3
    n_chunk = 6 * D // N
    c_col, neg, den, silu = (k.sb(n, [P, KD]) for n in ("c_col", "exp_neg_c", "den", "silu"))
    silu_rep = k.sb("silu_rep", [P, KD, P])
    w = k.sb("w_ada", [P, W_SLOTS, KD, N])
    b = k.sb("b_ada", [P, 6 * D])
    mod = k.sb("mod", [P, 6 * D])
    norms = k.sb("norms", [P, 2, D])
    zero = k.sb("zero", [P, D])
    acc = k.ps("acc", [P, 2, N])
    c_in, b_in, mod_out, const_in, exp_done, dve_step = k.sems("c_in b_in mod_out const_in exp_done dve_step")
    silu_ready, acc_full, acc_read, mod_ready = k.sems("silu_ready acc_full acc_read mod_ready")
    zero_set, zero_out = k.sems("zero_set zero_out")
    w_in = [k.sem(f"w_in{s}") for s in range(W_SLOTS)]
    w_dram = A["w_ada"].rearrange("o (s p) n -> p (o s) n", p=P)
    ones = keep["const"]("ones")

    def first_loads(pool):
        for i in range(2):
            pool.dma_start(keep["x"][:, i], tiles_of(A["x"])[:, i:i + 1]).then_inc(keep["x_in"][i], 16)
        for c in range(2):
            col = w_in_column(c)
            pool.dma_start(keep["w_raw"][:, c], rows_of(A["w_in"])[:, :, col:col + N]).then_inc(keep["raw_in"][c], 16)

    with nc.Block() as block:

        @block.sync
        def _(sp):
            sp.dma_start(c_col[:], A["c"].rearrange("o (s p) -> p (o s)", p=P),
                         allow_slow_non_contiguous=True).then_inc(c_in, 16)
            sp.dma_start(keep["const_all"][:], A["const"][:, 0:CONST_SHARED]).then_inc(const_in, 16)
            for n in range(n_chunk):
                if n >= W_SLOTS:
                    sp.wait_ge(acc_full, n - W_SLOTS + 1)
                sp.dma_start(w[:, n % W_SLOTS], w_dram[:, :, n * N:(n + 1) * N]).then_inc(w_in[n % W_SLOTS], 16)
            for j, name, ready, n in ((2, "g1", acc_read, 6), (3, "sh2", acc_read, 8), (4, "A2", mod_ready, 1),
                                      (5, "g2", acc_read, n_chunk)):
                sp.wait_ge(ready, n)
                sp.dma_start(keep[name], mod[:, j * D:(j + 1) * D]).then_inc(mod_out, 16)
            sp.wait_ge(mod_out, 64)

        @block.scalar
        def _(act):
            act.dma_start(b[:], row(A["b_ada"])).then_inc(b_in, 16)
            act.dma_start(norms[:, 0], row(A["norm1"])).then_inc(b_in, 16)
            act.dma_start(norms[:, 1], row(A["norm2"])).then_inc(b_in, 16)
            act.wait_ge(c_in, 16)
            nc.scalar.activation(neg[:], c_col[:], ACT.Exp, scale=-1.0).then_inc(exp_done, 1)

        @block.gpsimd
        def _(pool):
            nc.gpsimd.memset(keep["glr_t"][:], 1.0).then_inc(zero_set, 1)
            nc.gpsimd.memset(zero[:], 0.0).then_inc(zero_set, 1)
            pool.wait_ge(zero_set, 2)
            pool.dma_start(keep["h2"][S:ROWS, :], zero[:]).then_inc(zero_out, 16)
            for half in range(2):
                pool.dma_start(keep["y"][half][S:ROWS, :], zero[:, 0:N]).then_inc(zero_out, 16)
            pool.wait_ge(acc_full, n_chunk - W_SLOTS)
            first_loads(pool)
            pool.wait_ge(zero_out, 48)

        @block.vector
        def _(dve):
            step = Steps(dve, dve_step)
            dve.wait_ge(exp_done, 1)
            step(nc.vector.tensor_scalar(den[:], neg[:], 1.0, None, ALU.add))
            step(nc.vector.reciprocal(neg[:], den[:]))
            step(nc.vector.tensor_tensor(silu[:], c_col[:], neg[:], ALU.mult))
            dve.wait_ge(const_in, 16)
            for s in range(KD):
                nc.vector.tensor_scalar(silu_rep[:, s], ones, silu[:, s:s + 1], None, ALU.mult).then_inc(silu_ready, 1)
            dve.wait_ge(b_in, 48)
            for n in range(n_chunk):
                dve.wait_ge(acc_full, n + 1)
                nc.vector.tensor_tensor(mod[:, n * N:(n + 1) * N], acc[:, n % 2], b[:, n * N:(n + 1) * N],
                                        ALU.add).then_inc(acc_read, 1)
                dve.wait_ge(acc_read, n + 1)
                if n == 3:
                    step(nc.vector.tensor_copy(keep["sh1"][:], mod[:, 0:D]))
                    step(nc.vector.scalar_tensor_tensor(out=keep["A1"][:], in0=mod[:, D:2 * D], scalar=1.0,
                                                        in1=norms[:, 0], op0=ALU.add, op1=ALU.mult))
                if n == 9:
                    nc.vector.scalar_tensor_tensor(out=mod[:, 4 * D:5 * D], in0=mod[:, 4 * D:5 * D], scalar=1.0,
                                                   in1=norms[:, 1], op0=ALU.add, op1=ALU.mult).then_inc(mod_ready, 1)

        @block.tensor
        def _(pe):
            pe.wait_ge(silu_ready, KD)
            for n in range(n_chunk):
                pe.wait_ge(w_in[n % W_SLOTS], 16 * (n // W_SLOTS + 1))
                if n >= 2:
                    pe.wait_ge(acc_read, n - 1)
                for s in range(KD):
                    mm = nc.tensor.matmul(acc[:, n % 2], silu_rep[:, s], w[:, n % W_SLOTS, s],
                                          start=(s == 0), stop=(s == KD - 1))
                mm.then_inc(acc_full, 1)


def phase_projection(nc, k, A, keep):
    HT = NT // 2
    raw = keep["w_raw"]
    whi, wlo = (k.sb(n, [P, 2, KD, N], F32R) for n in ("w_hi", "w_lo"))
    rraw = k.sb("rank_raw", [P, KD, RANK])
    rhi, rlo = (k.sb(n, [P, KD, P], F32R) for n in ("rank_hi", "rank_lo"))
    hhi, hlo = (k.sb(n, [P, KD, HT, P], F32R) for n in ("h_hi", "h_lo"))
    x = keep["x"]
    squares = k.sb("squares", [P, D], mybir.dt.bfloat16)
    ssq, rs, rinv = (k.sb(n, [P, 2]) for n in ("ssq", "rms", "rinv"))
    sum_done = k.sem("sum_done")
    stage = k.sb("stage", [P, 2, N])
    tp = k.ps("tp", [P, 2, KD, P])
    acc = k.ps("acc", [P, 2, N])
    racc = k.ps("racc", [P, N])
    sq_done, dve_step, h_ready, t_done, hi_done, lo_done = k.sems(
        "sq_done dve_step h_ready t_done hi_done lo_done")
    whi_done, wlo_done, mm_done, acc_read, r_done, r_read, rank_in, rank_set, rhi_done, rlo_done = k.sems(
        "whi_done wlo_done mm_done acc_read r_done r_read rank_in rank_set rhi_done rlo_done")
    x_in, raw_in = keep["x_in"], keep["raw_in"]
    out_done = [k.sem(f"out_done{s}") for s in range(2)]
    USES = [(NC_IN + 1) // 2, NC_IN // 2]
    x_t, w_t = tiles_of(A["x"]), rows_of(A["w_in"])
    proj_t = keep["proj"].rearrange("(t p) n -> p t n", p=P)

    with nc.Block() as block:

        @block.gpsimd
        def _(pool):
            nc.gpsimd.memset(rhi[:].bitcast(F32), 0.0).then_inc(rank_set, 1)
            nc.gpsimd.memset(rlo[:].bitcast(F32), 0.0).then_inc(rank_set, 1)

            pool.sem_inc(wlo_done, 1)
            pool.sem_inc(t_done, 2)

            def load_w(half, c):
                pool.wait_ge(wlo_done, half * NC_IN + max(c, 1))
                col = w_in_column(c)
                pool.dma_start(raw[:, c % 2], w_t[:, :, col:col + N]).then_inc(raw_in[c % 2], 16)

            def load_x(half, i):
                pool.wait_ge(t_done, half * HT + i + 1)
                pool.dma_start(x[:, i % 2], x_t[:, half * HT + i:half * HT + i + 1]).then_inc(x_in[i % 2], 16)

            for i in range(2, HT):
                load_x(0, i)
                if i == 3:
                    pool.dma_start(rraw[:], w_t[:, :, GLR:GLR + RANK]).then_inc(rank_in, 16)
            for c in range(2, NC_IN):
                load_w(0, c)
                if c == 3:
                    for i in range(2):
                        load_x(1, i)
            for i in range(2):
                load_w(1, i)
            for i in range(2, HT):
                load_x(1, i)
            for c in range(2, NC_IN):
                load_w(1, c)

        @block.scalar
        def _(act):
            act.sem_inc(out_done[0], 16)
            act.sem_inc(out_done[1], 16)
            with act.Fori(0, 2) as half:

                def split_hi(c):
                    act.wait_ge(raw_in[c % 2], (half * USES[c % 2] + c // 2 + 1) * 16)
                    act.wait_ge(mm_done, half * NC_IN * HT + max(c - 1, 0) * HT + 1)
                    nc.scalar.copy(whi[:, c % 2], raw[:, c % 2]).then_inc(whi_done, 1)

                def square(i):
                    act.wait_ge(x_in[i % 2], (half * (HT // 2) + i // 2 + 1) * 16)
                    nc.scalar.activation(squares[:], x[:, i % 2], ACT.Square,
                                         accum_out=ssq[:, i % 2:i % 2 + 1]).then_inc(sum_done, 1)
                    act.wait_ge(sum_done, half * HT + i + 1)
                    nc.scalar.activation(rs[:, i % 2:i % 2 + 1], ssq[:, i % 2:i % 2 + 1], ACT.Sqrt, scale=1.0 / D,
                                         bias=keep["const"]("eps")).then_inc(sq_done, 1)

                def h_hi(i):
                    act.wait_ge(t_done, half * HT + i + 3)
                    for b in range(2):
                        nc.scalar.copy(hhi[:, 4 * b:4 * b + 4, i], tp[:, i % 2, 4 * b:4 * b + 4]).then_inc(hi_done, 1)

                def evacuate(c, i):
                    act.wait_ge(mm_done, (half * NC_IN + c) * HT + i + 2)
                    act.wait_ge(out_done[i % 2], ((half * NC_IN + c) * (HT // 2) + i // 2 + 1) * 16)
                    nc.scalar.copy(stage[:, i % 2], acc[:, i % 2]).then_inc(acc_read, 1)

                square(0)
                square(1)
                split_hi(0)
                h_hi(0)
                for c in range(NC_IN):
                    if 1 <= c < NC_IN - 1:
                        split_hi(c + 1)
                    for i in range(HT):
                        if c == 0 and i + 2 < HT:
                            square(i + 2)
                        if c == 0 and i + 1 < HT:
                            h_hi(i + 1)
                        evacuate(c, i)
                        if c == 0 and i == 2:
                            split_hi(1)
                        if c == 0 and i == 5:
                            act.wait_ge(rank_in, 16)
                            act.wait_ge(rank_set, 2)
                            nc.scalar.copy(rhi[:, :, 0:RANK], rraw[:]).then_inc(rhi_done, 1)
                    for b in range(2 if c == 0 else 0):
                        act.wait_ge(r_done, half * 2 + b + 1)
                        nc.scalar.copy(keep["glr_t"][0:RANK, bass.ds((half * 2 + b) * N, N)],
                                       racc[0:RANK, :]).then_inc(r_read, 1)

        @block.sync
        def _(sp):
            with sp.Fori(0, 2) as half:
                for c in range(NC_IN):
                    for i in range(HT):
                        sp.wait_ge(acc_read, (half * NC_IN + c) * HT + i + 3)
                        sp.dma_start(proj_t[:, bass.ds(half * HT + i, 1), c * N:(c + 1) * N],
                                       stage[:, i % 2]).then_inc(out_done[i % 2], 16)
            for s in range(2):
                sp.wait_ge(out_done[s], (NC_IN * HT + 1) * 16)

        @block.vector
        def _(dve):
            step = Steps(dve, dve_step, 2 * HT)
            with dve.Fori(0, 2) as half:
                step.turn(half)

                def split_lo(c):
                    dve.wait_ge(whi_done, half * NC_IN + c + 1)
                    dve.wait_ge(mm_done, half * NC_IN * HT + max(c - 1, 0) * HT + 1)
                    nc.vector.tensor_tensor(wlo[:, c % 2], raw[:, c % 2], whi[:, c % 2], ALU.subtract).then_inc(wlo_done, 1)

                def make_h(i):
                    s = i % 2
                    dve.wait_ge(sq_done, half * HT + i + 1)
                    step(nc.vector.reciprocal(rinv[:, s:s + 1], rs[:, s:s + 1]))
                    last = nc.vector.scalar_tensor_tensor(out=x[:, s], in0=x[:, s], scalar=rinv[:, s:s + 1],
                                                          in1=keep["A1"][:], op0=ALU.mult, op1=ALU.mult)
                    step(last)
                    nc.vector.tensor_tensor(x[:, s], x[:, s], keep["sh1"][:], ALU.add).then_inc(h_ready, 1)

                def h_lo(i):
                    for b in range(2):
                        dve.wait_ge(hi_done, (half * HT + i) * 2 + b + 1)
                        nc.vector.tensor_tensor(hlo[:, 4 * b:4 * b + 4, i], tp[:, i % 2, 4 * b:4 * b + 4],
                                                hhi[:, 4 * b:4 * b + 4, i], ALU.subtract).then_inc(lo_done, 1)

                make_h(0)
                make_h(1)
                split_lo(0)
                h_lo(0)
                for i in range(HT):
                    if i + 2 < HT:
                        make_h(i + 2)
                    if i + 1 < HT:
                        h_lo(i + 1)
                    if i == 2:
                        split_lo(1)
                    if i == 5:
                        dve.wait_ge(rhi_done, half + 1)
                        nc.vector.tensor_tensor(rlo[:, :, 0:RANK], rraw[:], rhi[:, :, 0:RANK],
                                                ALU.subtract).then_inc(rlo_done, 1)
                step.check()
                for c in range(2, NC_IN):
                    split_lo(c)

        @block.tensor
        def _(pe):
            pe.sem_inc(mm_done, 1)
            pe.sem_inc(lo_done, 4)
            pe.sem_inc(acc_read, 2)
            pe.sem_inc(r_read, 1)
            with pe.Fori(0, 2) as half:

                def transposes(i):
                    pe.wait_ge(h_ready, half * HT + i + 1)
                    pe.wait_ge(lo_done, (half * HT + i) * 2 + 2)
                    for s in range(KD):
                        mm = nc.tensor.transpose(tp[:, i % 2, s], x[:, i % 2, s * P:(s + 1) * P], keep["const"]("ident"))
                    mm.then_inc(t_done, 1)

                transposes(0)
                for c in range(NC_IN):
                    pe.wait_ge(whi_done, half * NC_IN + c + 1)
                    pe.wait_ge(wlo_done, half * NC_IN + c + 2)
                    for i in range(HT):
                        if c == 0 and i + 1 < HT:
                            transposes(i + 1)
                        if c == 0:
                            pe.wait_ge(lo_done, (half * HT + i) * 2 + 6)
                        pe.wait_ge(acc_read, (half * NC_IN + c) * HT + i + 1)
                        for s in range(KD):
                            mm = split_product(nc, acc[:, i % 2], hhi[:, s, i], hlo[:, s, i], whi[:, c % 2, s],
                                               wlo[:, c % 2, s], s == 0, s == KD - 1)
                        mm.then_inc(mm_done, 1)
                    for b in range(2 if c == 0 else 0):
                        pe.wait_ge(rlo_done, half + 1)
                        pe.wait_ge(r_read, half * 2 + b + 1)
                        t0 = b * (HT // 2)
                        for s in range(KD):
                            mm = split_product(nc, racc[:], rhi[:, s], rlo[:, s], hhi[:, s, t0:t0 + HT // 2],
                                               hlo[:, s, t0:t0 + HT // 2], s == 0, s == KD - 1)
                        mm.then_inc(r_done, 1)


def phase_mixer(nc, k, A, keep):
    own_const = k.sb("const", [P, sum(w for _, w in CONST_AT.values()) - CONST_SHARED])
    PAIR = GH // 2
    NSUB = P // SUB
    kcols = [SUB * (i + 1) for i in range(NSUB)]
    kfrom = [sum(kcols[:i]) for i in range(NSUB)]
    KW = sum(kcols)
    CLAMP = 80.0
    proj = k.sb("proj", [P, 2, PROJ])
    rope_x = k.sb("rope_x", [P, 2, 2 * N])
    o_out = k.sb("o_out", [P, 2, D])
    wgk = k.sb("wgk", [RANK + 1, 2 * P])
    normw = k.sb("normw", [P, 2, GDV])
    pos_i, pos_f = k.sb("pos_i", [P, NT], I32), k.sb("pos_f", [P, NT])
    ang, turns, red, wrap = (k.sb(n, [P, NT, RDK // 2]) for n in ("ang", "turns", "red", "wrap"))
    sin, cos = k.sb("sin", [P, NT, RDK // 2]), k.sb("cos", [P, NT, RDK // 2])
    glr = k.sb("glr", [RANK + 1, P])
    az, la, bs = k.sb("neg_abs", [P, 2 * P]), k.sb("log_decay", [P, 2 * P]), k.sb("run", [P, 4 * P])
    az_e, az_l = k.sb("az_exp", [P, 2 * P]), k.sb("az_ln", [P, 2 * P])
    dq, dk = k.sb("dq", [P, 2 * NSUB, SUB]), k.sb("dk", [P, PAIR, KW])
    eq, ek, eb = k.sb("eq", [P, 2, 2 * NSUB, SUB]), k.sb("ek", [P, 2, PAIR, KW]), k.sb("eb", [P, 2, 4 * P])
    qt, qe, kt = k.sb("qt", [P, PAIR, NSUB, 2, SUB]), k.sb("qe", [P, PAIR, P]), k.sb("kt", [P, PAIR, KW])
    kup = k.sb("kup", [P, GH * GDK])
    sg = k.sb("sg", [P, GH, P])
    St = k.sb("gla_state", [P, PAIR, 2 * GDV])
    rm = k.sb("rope_m", [P, 2, 2 * RH, RDK // 2])
    rc = k.sb("rope_c", [P, 2, 2 * RH, RDK // 2])
    rr = k.sb("rope", [P, 2, 2 * RH, RDK])
    rqT, rkT, rqx = (k.sb(n, [P, RH, P]) for n in ("rqT", "rkT", "rqx"))
    kz, sr = k.sb("kz", [P, RH, RDK]), k.sb("sr", [P, RH, P])
    R = k.sb("ret_state", [P, RH, RDK])
    mu = k.sb("mu", [P, RH])
    oc, sq = k.sb("oc", [P, 8, GDV]), k.sb("sq", [P, 8, GDV])
    var, lnv, r8 = (k.sb(n, [P, 8]) for n in ("var", "lnv", "r8"))
    ge, gl, gw, ginv = k.sb("ge", [P, 2, N]), k.sb("gl", [P, 2, N]), k.sb("gw", [P, 2, N]), k.sb("ginv", [P, 2, N])
    b_z, b_run, b_gT, b_gs, b_go, b_gu, b_q, b_k = (k.ps(n, [P, N]) for n in "z run gT gs go gu q k".split())
    names = ("glr z gT gi az az_e ln la run bs exps d qk kup gs sg go gu gS rm rr rt rqT kz rqx rs sr ro ru rR og oc mu var lnv r8 ge "
             "gl ginv gw o out").split()
    ev = {n: k.sem("ev_" + n) for n in names}
    setup_dma, pos_step, pool_set, dve_step, sin_done = k.sems(
        "setup_dma pos_step pool_set dve_step sin_done")
    wait_carrier = k.sem("wait_carrier")
    p_in = [k.sem(f"p_in{s}") for s in range(2)]
    rope_in = [k.sem(f"rope_in{s}") for s in range(2)]
    o_done = [k.sem(f"o_done{s}") for s in range(2)]
    proj_t = keep["proj"].rearrange("(t p) n -> p t n", p=P)
    o_t = keep["o"].rearrange("(t p) n -> p t n", p=P)
    TWO_PI = 2 * np.pi
    c1 = float(np.float32(np.floor(TWO_PI * 2 ** 5) / 2 ** 5))
    c2 = float(np.float32(np.floor((TWO_PI - c1) * 2 ** 14) / 2 ** 14))
    c3 = float(np.float32(TWO_PI - c1 - c2))
    MAGIC = 12582912.0
    HALF = RDK // 2

    def const(name):
        at, width = CONST_AT[name]
        return keep["const"](name) if at < CONST_SHARED else own_const[:, at - CONST_SHARED:at - CONST_SHARED + width]

    def heads(ap, n):
        return ap.rearrange("p (h d) -> p h d", h=n)

    def bc(ap, shape):
        return ap.to_broadcast(shape)

    with nc.Block() as block:

        @block.sync
        def _(sp):
            sp.dma_start(wgk[0:RANK, :], A["w_gk2"].rearrange("o r n -> (o r) n")).then_inc(setup_dma, 16)
            sp.dma_start(wgk[RANK:RANK + 1, :], A["b_gk"]).then_inc(setup_dma, 16)
            sp.dma_start(pos_i[:], A["positions"].rearrange("o (t p) -> p (o t)", p=P),
                         allow_slow_non_contiguous=True).then_inc(setup_dma, 16)
            sp.dma_start(own_const[:], A["const"][:, CONST_SHARED:]).then_inc(setup_dma, 16)
            sp.dma_start(normw[:, 0], row(A["gla_onorm"])).then_inc(setup_dma, 16)
            sp.dma_start(normw[:, 1], row(A["ret_onorm"])).then_inc(setup_dma, 16)
            for u in range(2):
                sp.sem_inc(o_done[u], 16)

            def load_rope(i, u):
                sp.wait_ge(ev["rr"], i + 1)
                sp.sem_inc(wait_carrier, 1)
                sp.dma_start(rope_x[:, u], proj_t[:, bass.ds(i, 1), C_RQ:C_RQ + 2 * N]).then_inc(rope_in[u], 16)

            def store(i, u):
                sp.wait_ge(ev["o"], i + 3)
                sp.sem_inc(wait_carrier, 1)
                sp.dma_start(o_t[:, bass.ds(i + 1, 1)], o_out[:, u]).then_inc(o_done[u], 16)

            def load(i, u):
                for n in ("ro", "kup", "gw", "ge"):
                    sp.wait_ge(ev[n], i + 1)
                sp.sem_inc(wait_carrier, 1)
                for c0, c1 in ((0, C_RQ), (C_RV, PROJ)):
                    sp.dma_start(proj[:, u, c0:c1], proj_t[:, bass.ds(i, 1), c0:c1]).then_inc(p_in[u], 16)

            load_rope(0, 0)
            load_rope(1, 1)
            load(0, 0)
            load(1, 1)
            for c in range(2):
                sp.dma_start(keep["w_out"][:, c], rows_of(A["w_out"])[:, :, c * N:(c + 1) * N]).then_inc(keep["w_out_in"], 16)

            def step(i, u, j):
                if not (isinstance(i, int) and i >= NT - 2):
                    load_rope(i + 2, u)
                    load(i + 2, u)
                store(i, u)

            for_tiles(sp, step)
            for u in range(2):
                sp.wait_ge(o_done[u], 16 * (NT // 2 + 1))

        @block.gpsimd
        def _(pool):
            nc.gpsimd.memset(St[:], 0.0).then_inc(pool_set, 1)
            nc.gpsimd.memset(R[:], 0.0).then_inc(pool_set, 1)
            nc.gpsimd.memset(sg[:], 0.0).then_inc(pool_set, 1)
            nc.gpsimd.memset(qt[:], 0.0).then_inc(pool_set, 1)
            for n in names:
                pool.sem_inc(ev[n], 2)
            pool.wait_ge(setup_dma, 96)

            def output(t, u):
                pool.wait_ge(ev["gi"], t + 3)
                pool.wait_ge(ev["out"], t + 3)
                nc.gpsimd.tensor_tensor(o_out[:, u], o_out[:, u], gw[:].rearrange("p a n -> p (a n)"),
                                        ALU.mult).then_inc(ev["o"], 1)

            def front_rank(t):
                pool.wait_ge(ev["z"], t + 2)
                nc.gpsimd.tensor_copy(glr[:], keep["glr_t"][:, bass.ds(t * P, P)]).then_inc(ev["glr"], 1)

            def front_rope(t, u, j):
                sin_t = sin[:, bass.ds(t, 1)].to_broadcast([P, 2 * RH, HALF])
                pool.wait_ge(rope_in[u], (j + 1) * 16)
                pool.wait_ge(ev["rr"], t + 2)
                x = heads(rope_x[:, u], 2 * RH)
                nc.gpsimd.tensor_tensor(rm[:, 0], x[:, :, HALF:], sin_t, ALU.mult)
                nc.gpsimd.tensor_tensor(rm[:, 1], x[:, :, 0:HALF], sin_t, ALU.mult).then_inc(ev["rm"], 1)

            def step(i, u, j):
                pj = proj[:, u]
                now, last = i + 3, i + 2
                if not is_tile(i, NT - 1):
                    front_rope(i + 1, 1 - u, j + u)
                pool.wait_ge(p_in[u], (j + 1) * 32)
                pool.wait_ge(ev["exps"], now)
                pool.wait_ge(ev["gu"], last)
                nc.gpsimd.tensor_tensor(kup[:], pj[:, C_GK:C_GK + GH * GDK], eb[:, u, 2 * P:4 * P],
                                        ALU.mult).then_inc(ev["kup"], 1)
                pool.wait_ge(ev["rr"], now)
                pool.wait_ge(ev["ru"], last)
                nc.gpsimd.tensor_tensor(kz[:], rr[:, u, RH:2 * RH],
                                        const("zeta").unsqueeze(2).to_broadcast([P, RH, RDK]),
                                        ALU.mult).then_inc(ev["kz"], 1)
                if not is_tile(i, 0):
                    output(i - 1, 1 - u)
                if not (isinstance(i, int) and i >= NT - 2):
                    front_rank(i + 2)
                pool.wait_ge(ev["o"], last)
                nc.gpsimd.tensor_tensor(heads(gw[:, 0], GH), heads(pj[:, C_GG:C_GG + N], GH),
                                        normw[:, 0:1].to_broadcast([P, GH, GDV]), ALU.mult)
                nc.gpsimd.tensor_tensor(heads(gw[:, 1], RH), heads(pj[:, C_RG:C_RG + N], RH),
                                        normw[:, 1:2].to_broadcast([P, RH, RDK]), ALU.mult).then_inc(ev["gw"], 1)
                pool.wait_ge(ev["ginv"], now)
                pool.wait_ge(ev["gw"], now)
                nc.gpsimd.tensor_tensor(gw[:], gw[:], ginv[:], ALU.mult).then_inc(ev["gi"], 1)

            front_rank(0)
            pool.wait_ge(sin_done, 2)
            front_rope(0, 0, 0)
            front_rank(1)
            for_tiles(pool, step)
            output(NT - 1, 1)

        @block.scalar
        def _(act):
            act.wait_ge(pos_step, 1)
            nc.scalar.activation(sin[:], red[:], ACT.Sin).then_inc(sin_done, 1)
            nc.scalar.activation(cos[:], wrap[:], ACT.Sin).then_inc(sin_done, 1)
            load_ln_exp(nc)

            def front_log(t):
                act.wait_ge(ev["z"], t + 3)
                act.wait_ge(ev["la"], t + 2)
                nc.scalar.activation(az[:], b_z[:, 0:2 * P], ACT.Abs).then_inc(ev["az"], 1)
                act.wait_ge(ev["az"], t + 3)
                nc.scalar.activation(az_e[:], az[:], ACT.Exp, scale=-1.0).then_inc(ev["az_e"], 1)
                act.wait_ge(ev["az_e"], t + 3)
                nc.scalar.activation(az_l[:], az_e[:], ACT.Ln, bias=const("ones")[:, 0:1]).then_inc(ev["ln"], 1)

            def front_sums(t):
                act.wait_ge(ev["run"], t + 3)
                act.wait_ge(ev["exps"], t + 2)
                nc.scalar.copy(bs[:], b_run[:]).then_inc(ev["bs"], 1)

            def front_exps(t, u):
                act.wait_ge(ev["bs"], t + 3)
                act.wait_ge(ev["d"], t + 3)
                for n in ("qk", "gS", "kup"):
                    act.wait_ge(ev[n], t + 1)
                nc.scalar.activation(eb[:, u], bs[:], ACT.Exp)
                nc.scalar.activation(eq[:, u], dq[:], ACT.Exp)
                nc.scalar.activation(ek[:, u], dk[:], ACT.Exp, scale=-1.0).then_inc(ev["exps"], 1)

            def roots(t):
                act.wait_ge(ev["var"], t + 3)
                nc.scalar.activation(lnv[:], var[:], ACT.Ln, scale=1.0 / GDV, bias=const("eps")).then_inc(ev["lnv"], 1)
                act.wait_ge(ev["lnv"], t + 3)
                act.wait_ge(ev["out"], t + 2)
                nc.scalar.activation(r8[:], lnv[:], ACT.Exp, scale=-0.5).then_inc(ev["r8"], 1)

            def step(i, u, j):
                pj = proj[:, u]
                now, last = i + 3, i + 2
                if not is_tile(i, 0):
                    roots(i - 1)
                if not is_tile(i, NT - 1):
                    front_log(i + 1)
                act.wait_ge(ev["rt"], now)
                act.wait_ge(ev["rs"], last)
                act.wait_ge(ev["rqx"], last)
                nc.scalar.copy(rqT[:], heads(b_q[:], RH))
                nc.scalar.copy(rkT[:], heads(b_k[:], RH)).then_inc(ev["rqT"], 1)
                if not is_tile(i, NT - 1):
                    front_sums(i + 1)
                act.wait_ge(p_in[u], (j + 1) * 32)
                nc.scalar.activation(ge[:, 0], pj[:, C_GG:C_GG + N], ACT.Exp, scale=-1.0)
                nc.scalar.activation(ge[:, 1], pj[:, C_RG:C_RG + N], ACT.Exp, scale=-1.0).then_inc(ev["ge"], 1)
                act.wait_ge(ev["ge"], now)
                nc.scalar.activation(gl[:], ge[:], ACT.Ln, bias=const("ones")[:, 0:1]).then_inc(ev["gl"], 1)
                act.wait_ge(ev["gl"], now)
                act.wait_ge(ev["gi"], last)
                nc.scalar.activation(ginv[:], gl[:], ACT.Exp, scale=-1.0).then_inc(ev["ginv"], 1)
                act.wait_ge(ev["go"], now)
                act.wait_ge(ev["out"], last)
                nc.scalar.copy(oc[:, 0:GH], heads(b_go[:], GH)).then_inc(ev["og"], 1)
                if not is_tile(i, NT - 1):
                    front_exps(i + 1, 1 - u)
                act.wait_ge(ev["mu"], now)
                for h in range(RH):
                    nc.scalar.activation(oc[:, GH + h], heads(b_k[:], RH)[:, h], ACT.Identity, bias=mu[:, h:h + 1])
                act.wait_ge(ev["var"], last)
                act.wait_ge(ev["lnv"], last)
                for h in range(RH):
                    ins = nc.scalar.activation(sq[:, GH + h], heads(b_k[:], RH)[:, h], ACT.Square, bias=mu[:, h:h + 1],
                                               accum_out=var[:, GH + h:GH + h + 1])
                ins.then_inc(ev["oc"], 1)
                act.wait_ge(ev["og"], now)
                for h in range(GH):
                    ins = nc.scalar.activation(sq[:, h], oc[:, h], ACT.Square, accum_out=var[:, h:h + 1])
                ins.then_inc(ev["var"], 1)

            front_log(0)
            front_sums(0)
            front_exps(0, 0)
            for_tiles(act, step)
            roots(NT - 1)

        @block.vector
        def _(dve):
            own = Steps(dve, dve_step, 0)
            dve.wait_ge(setup_dma, 96)
            own(nc.vector.tensor_copy(pos_f[:], pos_i[:]))
            own(nc.vector.tensor_tensor(ang[:], pos_f[:].unsqueeze(2).to_broadcast([P, NT, HALF]),
                                        const("inv_freq").unsqueeze(1).to_broadcast([P, NT, HALF]), ALU.mult))

            def reduce_turns(out, a):
                own(nc.vector.tensor_scalar(turns[:], a, 1.0 / TWO_PI, MAGIC, ALU.mult, ALU.add))
                own(nc.vector.tensor_scalar(turns[:], turns[:], MAGIC, None, ALU.subtract))
                own(nc.vector.scalar_tensor_tensor(out=out, in0=turns[:], scalar=-c1, in1=a, op0=ALU.mult, op1=ALU.add))
                own(nc.vector.scalar_tensor_tensor(out=out, in0=turns[:], scalar=-c2, in1=out, op0=ALU.mult, op1=ALU.add))
                own(nc.vector.scalar_tensor_tensor(out=out, in0=turns[:], scalar=-c3, in1=out, op0=ALU.mult, op1=ALU.add))

            def clamp(ap):
                own(nc.vector.tensor_scalar(ap, ap, float(np.float32(3.1415925)), -float(np.float32(3.1415925)), ALU.min, ALU.max))

            reduce_turns(red[:], ang[:])
            own(nc.vector.tensor_scalar(wrap[:], red[:], float(np.pi / 2), None, ALU.add))
            own(nc.vector.tensor_scalar(turns[:], wrap[:], float(np.pi), -TWO_PI, ALU.is_gt, ALU.mult))
            own(nc.vector.tensor_tensor(wrap[:], wrap[:], turns[:], ALU.add))
            clamp(red[:])
            clamp(wrap[:])
            dve.sem_inc(pos_step, 1)
            dve.wait_ge(pool_set, 4)
            dve.wait_ge(sin_done, 2)
            SETUP = own.n
            FRONT, PER = 9, 10

            def front_log(t):
                dve.wait_ge(ev["ln"], t + 3)
                dve.wait_ge(ev["run"], t + 2)
                nc.vector.scalar_tensor_tensor(out=la[:], in0=b_z[:, 0:2 * P], scalar=0.0, in1=az_l[:],
                                               op0=ALU.min, op1=ALU.subtract).then_inc(ev["la"], 1)

            def front_differences(t):
                dve.wait_ge(ev["bs"], t + 3)
                dve.wait_ge(ev["exps"], t + 2)
                b2 = bs[:, 0:2 * P]
                sub = b2.rearrange("p (c t) -> p c t", t=SUB)
                own(nc.vector.tensor_tensor(dq[:], sub, sub[:, :, SUB // 2 - 1:SUB // 2].to_broadcast([P, 2 * NSUB, SUB]),
                                            ALU.subtract))
                bp = b2.rearrange("p (a t) -> p a t", a=PAIR)
                for c in range(NSUB):
                    ref = c * SUB + SUB // 2 - 1
                    own(nc.vector.tensor_tensor(dk[:, :, kfrom[c]:kfrom[c] + kcols[c]], bp[:, :, 0:kcols[c]],
                                                bp[:, :, ref:ref + 1].to_broadcast([P, PAIR, kcols[c]]), ALU.subtract))
                own(nc.vector.tensor_scalar(dq[:], dq[:], CLAMP, None, ALU.min))
                nc.vector.tensor_scalar(dk[:], dk[:], -CLAMP, None, ALU.max).then_inc(ev["d"], 1)

            def front_rope(t, u, j):
                cos_t = cos[:, bass.ds(t, 1)].to_broadcast([P, 2 * RH, HALF])
                dve.wait_ge(rope_in[u], (j + 1) * 16)
                dve.wait_ge(ev["rr"], t + 2)
                x = heads(rope_x[:, u], 2 * RH)
                own(nc.vector.tensor_tensor(rc[:, 0], x[:, :, 0:HALF], cos_t, ALU.mult))
                own(nc.vector.tensor_tensor(rc[:, 1], x[:, :, HALF:], cos_t, ALU.mult))
                dve.wait_ge(ev["rm"], t + 3)
                dve.wait_ge(ev["rt"], t + 1)
                dve.wait_ge(ev["kz"], t + 1)
                own(nc.vector.tensor_tensor(rr[:, u, :, 0:HALF], rc[:, 0], rm[:, 0], ALU.subtract))
                nc.vector.tensor_tensor(rr[:, u, :, HALF:], rc[:, 1], rm[:, 1], ALU.add).then_inc(ev["rr"], 1)

            def norms(t, u, j):
                dve.wait_ge(ev["r8"], t + 3)
                dve.wait_ge(o_done[u], (j + 1) * 16)
                nc.vector.tensor_tensor(heads(o_out[:, u], 8), oc[:], r8[:].unsqueeze(2).to_broadcast([P, 8, GDV]),
                                        ALU.mult).then_inc(ev["out"], 1)

            def step(i, u, j):
                now, last = i + 3, i + 2
                own.base, own.n = i * PER + SETUP + FRONT, 0
                dve.wait_ge(ev["exps"], now)
                dve.wait_ge(ev["gT"], now)
                dve.wait_ge(ev["gs"], last)
                dve.wait_ge(ev["go"], last)
                q_t = b_gT[:, 0:2 * P].rearrange("p (a t) -> p a t", a=PAIR)
                k_t = b_gT[:, 2 * P:4 * P].rearrange("p (a t) -> p a t", a=PAIR)
                scale = GDK ** -0.5
                for c in range(NSUB):
                    nc.vector.tensor_tensor(kt[:, :, kfrom[c]:kfrom[c] + kcols[c]], k_t[:, :, 0:kcols[c]],
                                            ek[:, u, :, kfrom[c]:kfrom[c] + kcols[c]], ALU.mult)
                for h in range(2):
                    rows = slice(h * GDK, (h + 1) * GDK)
                    nc.vector.scalar_tensor_tensor(out=qt[rows, :, :, h].rearrange("p a c t -> p (a c) t"),
                                                   in0=b_gT[rows, 0:2 * P].rearrange("p (c t) -> p c t", t=SUB),
                                                   scalar=scale, in1=eq[rows, u], op0=ALU.mult, op1=ALU.mult)
                nc.vector.scalar_tensor_tensor(out=qe[:], in0=q_t, scalar=scale,
                                               in1=eb[:, u, 0:2 * P].rearrange("p (a t) -> p a t", a=PAIR),
                                               op0=ALU.mult, op1=ALU.mult).then_inc(ev["qk"], 1)
                if not is_tile(i, 0):
                    norms(i - 1, 1 - u, j - 1 + u)
                if not is_tile(i, NT - 1):
                    front_log(i + 1)
                dve.wait_ge(ev["rqT"], now)
                dve.wait_ge(ev["ro"], last)
                nc.vector.tensor_tensor(rqx[:], rqT[:], heads(const("xi"), RH), ALU.mult).then_inc(ev["rqx"], 1)
                dve.wait_ge(ev["gs"], now)
                for c in range(NSUB):
                    cols = slice(c * SUB, (c + 1) * SUB)
                    ins = nc.vector.tensor_tensor(
                        sg[0:kcols[c], :, cols], heads(b_gs[:], GH)[0:kcols[c], :, cols],
                        const("causal")[0:kcols[c], cols].unsqueeze(1).to_broadcast([kcols[c], GH, SUB]), ALU.mult)
                ins.then_inc(ev["sg"], 1)
                if not is_tile(i, NT - 1):
                    front_rope(i + 1, 1 - u, j + u)
                dve.wait_ge(ev["rs"], now)
                nc.vector.tensor_tensor(sr[:], heads(b_q[:], RH), heads(const("decay"), RH), ALU.mult).then_inc(ev["sr"], 1)
                if not is_tile(i, NT - 1):
                    front_differences(i + 1)
                dve.wait_ge(ev["ro"], now)
                dve.wait_ge(ev["oc"], last)
                own(nc.vector.tensor_reduce(mu[:], heads(b_k[:], RH), AX_X, ALU.add))
                nc.vector.tensor_scalar(mu[:], mu[:], -1.0 / RDK, None, ALU.mult).then_inc(ev["mu"], 1)
                dve.wait_ge(ev["ru"], now)
                for h in range(RH):
                    ins = nc.vector.scalar_tensor_tensor(out=R[:, h], in0=R[:, h], scalar=GAMMA_TILE[h],
                                                         in1=b_run[:, h * RDK:(h + 1) * RDK], op0=ALU.mult, op1=ALU.add)
                ins.then_inc(ev["rR"], 1)
                dve.wait_ge(ev["gu"], now)
                dve.wait_ge(ev["go"], now)
                for h in range(GH):
                    pr, rows = h // 2, slice((h % 2) * GDK, (h % 2 + 1) * GDK)
                    cols = slice((h % 2) * GDV, (h % 2 + 1) * GDV)
                    ins = nc.vector.scalar_tensor_tensor(
                        out=St[rows, pr, cols], in0=St[rows, pr, cols], scalar=eb[rows, u, (pr + 1) * P - 1:(pr + 1) * P],
                        in1=b_gu[rows, pr * 2 * GDV + cols.start:pr * 2 * GDV + cols.stop], op0=ALU.mult, op1=ALU.add)
                ins.then_inc(ev["gS"], 1)

            front_rope(0, 0, 0)
            front_log(0)
            front_differences(0)
            assert own.n == SETUP + FRONT
            for_tiles(dve, step)
            norms(NT - 1, 1, NT // 2 - 1)

        @block.tensor
        def _(pe):
            pe.wait_ge(setup_dma, 96)
            pe.wait_ge(pool_set, 4)
            ident = const("ident")

            def front_log(t):
                pe.wait_ge(ev["glr"], t + 3)
                pe.wait_ge(ev["la"], t + 2)
                nc.tensor.matmul(b_z[:, 0:2 * P], glr[:], wgk[:], start=True, stop=True).then_inc(ev["z"], 1)

            def front_sums(t):
                pe.wait_ge(ev["la"], t + 3)
                pe.wait_ge(ev["bs"], t + 2)
                pe.wait_ge(ev["rR"], t + 1)
                for c in range(2):
                    nc.tensor.matmul(b_run[:, c * P:(c + 1) * P], la[:, c * P:(c + 1) * P], const("sum_to"),
                                     start=True, stop=True)
                nc.tensor.matmul(b_run[:, 2 * P:4 * P], const("sum_after"), la[:], start=True,
                                 stop=True).then_inc(ev["run"], 1)

            def step(i, u, j):
                pj = proj[:, u]
                now, last = i + 3, i + 2
                if not is_tile(i, NT - 1):
                    front_log(i + 1)
                pe.wait_ge(p_in[u], (j + 1) * 32)
                pe.wait_ge(ev["qk"], last)
                for c in range(4):
                    mm = nc.tensor.transpose(b_gT[:, c * P:(c + 1) * P], pj[:, C_GQ + c * P:C_GQ + (c + 1) * P], ident)
                mm.then_inc(ev["gT"], 1)
                pe.wait_ge(ev["rr"], now)
                pe.wait_ge(ev["sr"], last)
                pe.wait_ge(ev["oc"], last)
                for h in range(RH):
                    nc.tensor.transpose(b_q[:, h * P:(h + 1) * P], rr[:, u, h], ident)
                for h in range(RH):
                    mm = nc.tensor.transpose(b_k[:, h * P:(h + 1) * P], rr[:, u, RH + h], ident)
                mm.then_inc(ev["rt"], 1)
                pe.wait_ge(ev["kup"], now)
                pe.wait_ge(ev["gS"], last)
                for c in range(PAIR):
                    mm = nc.tensor.matmul(b_gu[:, c * 2 * GDV:(c + 1) * 2 * GDV], kup[:, c * P:(c + 1) * P],
                                          pj[:, C_GV + c * 2 * GDV:C_GV + (c + 1) * 2 * GDV], start=True, stop=True)
                mm.then_inc(ev["gu"], 1)
                pe.wait_ge(ev["qk"], now)
                pe.wait_ge(ev["sg"], last)
                for a in range(PAIR):
                    for c in range(NSUB):
                        mm = nc.tensor.matmul(heads(b_gs[:], GH)[0:kcols[c], 2 * a:2 * a + 2, c * SUB:(c + 1) * SUB],
                                              kt[:, a, kfrom[c]:kfrom[c] + kcols[c]], qt[:, a, c],
                                              start=True, stop=True)
                mm.then_inc(ev["gs"], 1)
                if not is_tile(i, NT - 1):
                    front_sums(i + 1)
                pe.wait_ge(ev["rqT"], now)
                for h in range(RH):
                    mm = nc.tensor.matmul(b_q[:, h * P:(h + 1) * P], rkT[:, h], rqT[:, h], start=True, stop=True)
                mm.then_inc(ev["rs"], 1)
                pe.wait_ge(ev["sg"], now)
                pe.wait_ge(ev["gS"], last)
                pe.wait_ge(ev["og"], last)
                for c in range(PAIR):
                    cols = slice(c * 2 * GDV, (c + 1) * 2 * GDV)
                    nc.tensor.matmul(b_go[:, cols], qe[:, c], St[:, c], start=True, stop=False, skip_group_check=True)
                    for h in (2 * c, 2 * c + 1):
                        mm = nc.tensor.matmul(b_go[:, h * GDV:(h + 1) * GDV], sg[:, h],
                                              pj[:, C_GV + h * GDV:C_GV + (h + 1) * GDV], start=False,
                                              stop=(h % 2 == 1), skip_group_check=True)
                mm.then_inc(ev["go"], 1)
                pe.wait_ge(ev["kz"], now)
                pe.wait_ge(ev["bs"], now if is_tile(i, NT - 1) else now + 1)
                for h in range(RH):
                    mm = nc.tensor.matmul(b_run[:, h * RDK:(h + 1) * RDK], kz[:, h],
                                          pj[:, C_RV + h * RDK:C_RV + (h + 1) * RDK], start=True, stop=True)
                mm.then_inc(ev["ru"], 1)
                pe.wait_ge(ev["sr"], now)
                pe.wait_ge(ev["rqx"], now)
                pe.wait_ge(ev["rR"], last)
                for h in range(RH):
                    nc.tensor.matmul(b_k[:, h * P:(h + 1) * P], sr[:, h], pj[:, C_RV + h * RDK:C_RV + (h + 1) * RDK],
                                     start=True, stop=False)
                    mm = nc.tensor.matmul(b_k[:, h * P:(h + 1) * P], rqx[:, h], R[:, h], start=False, stop=True)
                mm.then_inc(ev["ro"], 1)

            front_log(0)
            front_sums(0)
            for_tiles(pe, step)



def phase_routing(nc, k, A, keep):
    const = keep["const"]
    raw, w_in = keep["w_out"], keep["w_out_in"]
    whi, wlo = (k.sb(n, [P, 2, KD, N], F32R) for n in ("w_hi", "w_lo"))
    wr = k.sb("w_router", [P, KD, E])
    br = k.sb("b_router", [P, E])
    bd = k.sb("b_down", [E, D])
    g1, A2, sh2, g2 = (k.sb(n, [P, D]) for n in ("g1", "A2", "sh2", "g2"))
    empty = k.sb("empty", [P, PLACES, 2], I32)
    o, x = k.sb("o", [P, 2, D]), k.sb("x", [P, 2, D])
    ohi, olo = (k.sb(n, [P, KD, P], F32R) for n in ("o_hi", "o_lo"))
    x2 = k.sb("x2", [P, 2, D])
    h2, yi = k.sb("h2", [P, D]), k.sb("yi", [P, D])
    squares = k.sb("squares", [P, D], mybir.dt.bfloat16)
    h2T = k.sb("h2T", [P, KD, P])
    ssq, lnv, rs = (k.sb(n, [P, 1]) for n in ("ssq", "lnv", "rs"))
    lg, lr, mask, ex, W, key, pick, kf, rkf = (k.sb(n, [P, E]) for n in
                                               "lg lr mask ex W key pick kf rkf".split())
    best, top = k.sb("best", [P, 8]), k.sb("top", [P, 8])
    neg, den = k.sb("neg", [P, 1]), k.sb("den", [P, 1])
    run = k.sb("run", [P, E])
    ri, ra, rb = (k.sb(n, [P, E], I32) for n in ("ri", "ra", "rb"))
    wj, idx, rec = k.sb("wj", [P, TOPK]), k.sb("idx", [P, TOPK], I32), k.sb("rec", [P, TOPK, 2], I32)
    wT = k.sb("wT", [E, P])
    over = k.sb("over", [P, E, NT])
    tiles, groups, cumg, cumt, sel = (k.sb(n, [P, E]) for n in "tiles groups cumg cumt sel".split())
    gT, tT = k.sb("gT", [E, P]), k.sb("tT", [E, P])
    col = k.sb("col", [P, 8])
    table, table_i = k.sb("table", [P, 4]), k.sb("table_i", [P, 4], I32)
    acc, tp, tq = k.ps("acc", [P, 2, N]), k.ps("tp", [P, KD, P]), k.ps("tq", [P, KD, P])
    sm, wt = k.ps("sm", [P, N]), k.ps("wt", [P, N])
    names = ("accr rkr t1 ohi olo mm xg x2 sq lnv rs h2 t2 h2t lg lgs ex W mask rk wt wtc bd yi rec stored").split()
    ev = {n: k.sem("ev_" + n) for n in names}
    setup_dma, whi_done, wlo_done, pool_set, dve_step, h2_out, y_out, place_out, empty_set, empty_out = k.sems(
        "setup_dma whi_done wlo_done pool_set dve_step h2_out y_out place_out empty_set empty_out")
    table_step, table_out, wait_carrier, table_ready, table_t = k.sems(
        "table_step table_out wait_carrier table_ready table_t")
    o_in = [k.sem(f"o_in{s}") for s in range(2)]
    x_in = [k.sem(f"x_in{s}") for s in range(2)]
    o_t = keep["o"].rearrange("(t p) n -> p t n", p=P)
    x_t = A["x"].rearrange("o (t p) d -> p (o t) d", p=P)
    h2_t = keep["h2"].rearrange("(t p) n -> p t n", p=P)
    y_t = [y.rearrange("(t p) n -> p t n", p=P) for y in keep["y"]]
    NOWHERE = 3.0e38
    with nc.Block() as block:

        @block.sync
        def _(sp):

            def load_o(i, u):
                sp.wait_ge(ev["t1"], i + 1)
                sp.dma_start(o[:, u], o_t[:, bass.ds(i + 1, 1)]).then_inc(o_in[u], 16)

            def load_x(i, u):
                sp.wait_ge(ev["x2"], i + 1)
                sp.dma_start(x[:, u], x_t[:, bass.ds(i, 1)]).then_inc(x_in[u], 16)

            for u in range(2):
                load_o(u, u)
            sp.dma_start(wr[:], A["w_router"].rearrange("o (s p) e -> p (o s) e", p=P)).then_inc(setup_dma, 16)
            sp.dma_start(br[:], row(A["b_router"])).then_inc(setup_dma, 16)
            sp.dma_start(bd[:], A["b_down"].rearrange("o e d -> (o e) d")).then_inc(setup_dma, 16)
            for t, n in ((g1, "g1"), (A2, "A2"), (sh2, "sh2"), (g2, "g2")):
                sp.dma_start(t[:], keep[n]).then_inc(setup_dma, 16)
            for u in range(2):
                load_x(u, u)
            with sp.Fori(1, NT // 2) as j:
                for u in range(2):
                    load_o(j * 2 + u, u)
                    load_x(j * 2 + u, u)
            sp.wait_ge(table_step, 1)
            sp.dma_start(keep["groups"], table_i[:]).then_inc(table_out, 16)
            sp.wait_ge(table_out, 16)

        @block.gpsimd
        def _(pool):
            nc.gpsimd.memset(run[:], 0.0).then_inc(pool_set, 1)
            for n in names:
                pool.sem_inc(ev[n], 2)
            pool.wait_ge(empty_set, 1)
            pool.dma_start(keep["places"].rearrange("(p q) c -> p (q c)", p=P), empty[:].rearrange("p q c -> p (q c)")
                           ).then_inc(empty_out, 16)
            pool.wait_ge(empty_out, 16)
            with pool.Fori(0, NT) as i:
                pool.wait_ge(ev["yi"], i + 3)
                pool.sem_inc(wait_carrier, 1)
                for half in range(2):
                    pool.dma_start(y_t[half][:, bass.ds(i, 1)], yi[:, half * N:(half + 1) * N]).then_inc(y_out, 16)
                pool.wait_ge(ev["rec"], i + 3)
                pool.sem_inc(wait_carrier, 1)
                for c in range(TOPK):
                    pool.indirect_dma_start(out=keep["places"], out_offset=bass.IndirectOffsetOnAxis(ap=idx[:, c:c + 1], axis=0),
                                            in_=rec[:, c], in_offset=None).then_inc(place_out, 16)
                pool.wait_ge(y_out, (i + 1) * 32)
                pool.wait_ge(place_out, (i + 1) * 16 * TOPK)
                pool.sem_inc(ev["stored"], 1)

        @block.scalar
        def _(act):
            act.sem_inc(h2_out, 16)
            load_ln_exp(nc)
            for c in range(2):
                act.wait_ge(w_in, 32)
                nc.scalar.copy(whi[:, c], raw[:, c]).then_inc(whi_done, 1)

            def split_hi(t):
                act.wait_ge(ev["t1"], t + 3)
                act.wait_ge(ev["mm"], t + 2)
                for b in range(2):
                    nc.scalar.copy(ohi[:, 4 * b:4 * b + 4], tp[:, 4 * b:4 * b + 4]).then_inc(ev["ohi"], 1)

            def weights_t(t):
                act.wait_ge(ev["wt"], t + 3)
                act.wait_ge(ev["bd"], t + 2)
                nc.scalar.copy(wT[:], wt[0:E, 0:P]).then_inc(ev["wtc"], 1)

            def step(i, u, j):
                now, last = i + 3, i + 2
                if not is_tile(i, NT - 1):
                    split_hi(i + 1)
                if not is_tile(i, 0):
                    weights_t(i - 1)
                act.wait_ge(ev["x2"], now)
                nc.scalar.activation(squares[:], x2[:, u], ACT.Square, accum_out=ssq[:]).then_inc(ev["sq"], 1)
                act.wait_ge(ev["sq"], now)
                nc.scalar.activation(lnv[:], ssq[:], ACT.Ln, scale=1.0 / D, bias=const("eps")).then_inc(ev["lnv"], 1)
                act.wait_ge(ev["lnv"], now)
                act.wait_ge(ev["h2"], last)
                nc.scalar.activation(rs[:], lnv[:], ACT.Exp, scale=-0.5).then_inc(ev["rs"], 1)
                act.wait_ge(ev["h2"], now)
                act.dma_start(h2_t[:, bass.ds(i, 1)], h2[:]).then_inc(h2_out, 16)
                act.wait_ge(ev["t2"], now)
                act.wait_ge(ev["lg"], last)
                for b in range(2):
                    ins = nc.scalar.copy(h2T[:, 4 * b:4 * b + 4], tq[:, 4 * b:4 * b + 4])
                ins.then_inc(ev["h2t"], 1)
                act.wait_ge(ev["lgs"], now)
                act.wait_ge(ev["W"], last)
                nc.scalar.activation(ex[:], lg[:], ACT.Exp, bias=neg[:]).then_inc(ev["ex"], 1)

            split_hi(0)
            for_tiles(act, step)
            weights_t(NT - 1)
            act.wait_ge(h2_out, 16 * (NT + 1))

        @block.vector
        def _(dve):
            own = Steps(dve, dve_step)
            for c in range(2):
                dve.wait_ge(whi_done, c + 1)
                nc.vector.tensor_tensor(wlo[:, c], raw[:, c], whi[:, c], ALU.subtract).then_inc(wlo_done, 1)
            own(nc.vector.memset(empty[:], 0))
            own(nc.vector.tensor_scalar(col[:, 0:1], const("number"), float(S), None, ALU.add))
            nc.vector.tensor_copy(empty[:, :, 0], col[:, 0:1].to_broadcast([P, PLACES])).then_inc(empty_set, 1)
            dve.wait_ge(setup_dma, 7 * 16)
            dve.wait_ge(pool_set, 1)
            SETUP = own.n
            BEFORE, PER = 16, 25

            def split_lo(t):
                for b in range(2):
                    dve.wait_ge(ev["ohi"], t * 2 + b + 3)
                    nc.vector.tensor_tensor(olo[:, 4 * b:4 * b + 4], tp[:, 4 * b:4 * b + 4], ohi[:, 4 * b:4 * b + 4],
                                            ALU.subtract).then_inc(ev["olo"], 1)

            def first_rows(t, u):
                dve.wait_ge(ev["bd"], t + 3)
                dve.wait_ge(ev["stored"], t + 2)
                own(nc.vector.tensor_tensor(yi[:], tq[:].rearrange("p s n -> p (s n)"), g2[:], ALU.mult))
                nc.vector.tensor_tensor(yi[:], yi[:], x2[:, u], ALU.add).then_inc(ev["yi"], 1)

            def list_places(t):
                dve.wait_ge(ev["rk"], t + 3)
                own(nc.vector.tensor_tensor(rkf[:], sm[:, E:2 * E], run[:], ALU.add))
                own(nc.vector.tensor_tensor(run[:], sm[:, 2 * E:3 * E], run[:], ALU.add))
                dve.sem_inc(ev["rkr"], 1)
                own(nc.vector.tensor_copy(ri[:], rkf[:]))
                own(nc.vector.tensor_scalar(ra[:], ri[:], P - 1, 9, ALU.bitwise_and, ALU.logical_shift_left))
                own(nc.vector.tensor_scalar(rb[:], ri[:], 7, None, ALU.logical_shift_right))
                own(nc.vector.tensor_tensor(kf[:], ra[:], rb[:], ALU.add))
                own(nc.vector.scalar_tensor_tensor(out=kf[:], in0=kf[:], scalar=1.0, in1=const("expert_row"),
                                                   op0=ALU.add, op1=ALU.add))
                own(nc.vector.tensor_tensor(key[:], kf[:], mask[:], ALU.mult))
                dve.sem_inc(wait_carrier, 1)
                own(nc.vector.max(top[:], key[:]))
                dve.wait_ge(ev["stored"], t + 2)
                own(nc.vector.tensor_scalar(idx[:], top[:, 0:TOPK], 1.0, None, ALU.subtract))
                for c in range(TOPK):
                    own(nc.vector.scalar_tensor_tensor(out=pick[:], in0=key[:], scalar=top[:, c:c + 1], in1=W[:],
                                                       op0=ALU.is_equal, op1=ALU.mult, accum_out=wj[:, c:c + 1]))
                own(nc.vector.tensor_copy(rec[:, :, 0], const("token")[:, bass.ds(t, 1)].to_broadcast([P, TOPK])))
                nc.vector.tensor_copy(rec[:].bitcast(F32)[:, :, 1], wj[:]).then_inc(ev["rec"], 1)

            def step(i, u, j):
                now, last = i + 3, i + 2
                own.base, own.n = SETUP + (0 if is_tile(i, 0) else i * PER - BEFORE), 0
                dve.wait_ge(ev["mm"], now)
                own(nc.vector.tensor_tensor(x2[:, u], acc[:].rearrange("p a n -> p (a n)"), g1[:], ALU.mult))
                dve.sem_inc(ev["accr"], 1)
                if not is_tile(i, NT - 1):
                    split_lo(i + 1)
                dve.wait_ge(x_in[u], (j + 1) * 16)
                nc.vector.tensor_tensor(x2[:, u], x2[:, u], x[:, u], ALU.add).then_inc(ev["x2"], 1)
                if not is_tile(i, 0):
                    first_rows(i - 1, 1 - u)
                dve.wait_ge(ev["rs"], now)
                dve.wait_ge(ev["t2"], last)
                dve.wait_ge(h2_out, (i + 1) * 16)
                own(nc.vector.scalar_tensor_tensor(out=h2[:], in0=x2[:, u], scalar=rs[:], in1=A2[:], op0=ALU.mult,
                                                   op1=ALU.mult))
                nc.vector.tensor_tensor(h2[:], h2[:], sh2[:], ALU.add).then_inc(ev["h2"], 1)
                if not is_tile(i, 0):
                    list_places(i - 1)
                dve.wait_ge(ev["lg"], now)
                own(nc.vector.tensor_tensor(lg[:], sm[:, 0:E], br[:], ALU.add))
                dve.sem_inc(wait_carrier, 1)
                own(nc.vector.max(best[:], lg[:]))
                nc.vector.tensor_scalar(neg[:], best[:, 0:1], -1.0, None, ALU.mult).then_inc(ev["lgs"], 1)
                own(nc.vector.memset(best[:, TOPK:8], NOWHERE))
                dve.sem_inc(wait_carrier, 1)
                own(nc.vector.match_replace(lr[:], best[:], lg[:], -NOWHERE))
                nc.vector.tensor_tensor(mask[:], lr[:], lg[:], ALU.not_equal).then_inc(ev["mask"], 1)
                dve.wait_ge(ev["mask"], now)
                dve.wait_ge(ev["ex"], now)
                dve.wait_ge(ev["wt"], last)
                own(nc.vector.tensor_tensor(W[:], ex[:], mask[:], ALU.mult))
                own(nc.vector.tensor_reduce(den[:], W[:], AX_X, ALU.add))
                own(nc.vector.reciprocal(den[:], den[:]))
                nc.vector.tensor_scalar(W[:], W[:], den[:], None, ALU.mult).then_inc(ev["W"], 1)

            split_lo(0)
            for_tiles(dve, step)
            own.base, own.n = SETUP + NT * PER - BEFORE, 0
            first_rows(NT - 1, 1)
            list_places(NT - 1)

            fin = Steps(dve, k.sem("fin"))
            fin(nc.vector.tensor_tensor(over[:], run[:].unsqueeze(2).to_broadcast([P, E, NT]),
                                        const("tile_from").unsqueeze(1).to_broadcast([P, E, NT]), ALU.is_gt))
            fin(nc.vector.tensor_reduce(tiles[:], over[:], AX_X, ALU.add))
            fin(nc.vector.tensor_reduce(groups[:], over[:].rearrange("p e (g t) -> p e g t", t=GT)[:, :, :, 0], AX_X, ALU.add))
            dve.sem_inc(table_ready, 1)
            dve.wait_ge(table_t, 1)
            fin(nc.vector.tensor_copy(gT[:], wt[0:E, 0:P]))
            fin(nc.vector.tensor_copy(tT[:], wt[0:E, P:2 * P]))
            dve.sem_inc(table_ready, 1)
            dve.wait_ge(table_t, 2)
            fin(nc.vector.tensor_copy(cumg[:], sm[:, 0:E]))
            fin(nc.vector.tensor_copy(cumt[:], sm[:, E:2 * E]))
            number, expert = const("number"), col[:, 1:2]
            fin(nc.vector.tensor_scalar(sel[:], cumg[:], number, None, ALU.is_le))
            fin(nc.vector.tensor_reduce(expert, sel[:], AX_X, ALU.add))
            fin(nc.vector.tensor_scalar(sel[:], const("expert"), expert, None, ALU.is_equal))
            fin(nc.vector.tensor_tensor(cumg[:], cumg[:], groups[:], ALU.subtract))
            for c, src in ((2, cumg), (3, tiles), (4, cumt)):
                fin(nc.vector.tensor_tensor(pick[:], sel[:], src[:], ALU.mult))
                fin(nc.vector.tensor_reduce(col[:, c:c + 1], pick[:], AX_X, ALU.add))
            fin(nc.vector.tensor_tensor(col[:, 5:6], number, col[:, 2:3], ALU.subtract))
            fin(nc.vector.tensor_scalar(col[:, 5:6], col[:, 5:6], float(GT), None, ALU.mult))
            fin(nc.vector.tensor_tensor(col[:, 6:7], col[:, 3:4], col[:, 5:6], ALU.subtract))
            fin(nc.vector.tensor_scalar(table[:, 1:2], col[:, 6:7], float(GT), 0.0, ALU.min, ALU.max))
            fin(nc.vector.tensor_scalar(col[:, 7:8], table[:, 1:2], 0.0, None, ALU.is_gt))
            fin(nc.vector.tensor_tensor(table[:, 0:1], expert, col[:, 7:8], ALU.mult))
            fin(nc.vector.tensor_tensor(col[:, 4:5], col[:, 4:5], col[:, 5:6], ALU.add))
            fin(nc.vector.tensor_tensor(table[:, 2:3], col[:, 4:5], col[:, 7:8], ALU.mult))
            fin(nc.vector.scalar_tensor_tensor(out=col[:, 6:7], in0=expert, scalar=float(NT), in1=col[:, 5:6],
                                               op0=ALU.mult, op1=ALU.add))
            fin(nc.vector.tensor_tensor(table[:, 3:4], col[:, 6:7], col[:, 7:8], ALU.mult))
            nc.vector.tensor_copy(table_i[:], table[:]).then_inc(table_step, 1)

        @block.tensor
        def _(pe):
            ident = const("ident")

            def transposed(t, u, j):
                pe.wait_ge(o_in[u], (j + 1) * 16)
                pe.wait_ge(ev["olo"], t * 2 + 2)
                for s in range(KD):
                    mm = nc.tensor.transpose(tp[:, s], o[:, u, s * P:(s + 1) * P], ident)
                mm.then_inc(ev["t1"], 1)

            def product(t, c, s0=0, s1=KD):
                if s0 == 0:
                    pe.wait_ge(ev["olo"], t * 2 + 4)
                    pe.wait_ge(ev["accr"], t + 2)
                for s in range(s0, s1):
                    mm = split_product(nc, acc[:, c], ohi[:, s], olo[:, s], whi[:, c, s], wlo[:, c, s],
                                       s == 0, s == KD - 1)
                if c == 1 and s1 == KD:
                    mm.then_inc(ev["mm"], 1)

            def step(i, u, j):
                now, last = i + 3, i + 2
                if not is_tile(i, NT - 1):
                    product(i + 1, 0, 0, KD - 2)
                pe.wait_ge(ev["h2"], now)
                pe.wait_ge(ev["h2t"], last)
                pe.wait_ge(ev["yi"], last)
                for s in range(KD):
                    mm = nc.tensor.transpose(tq[:, s], h2[:, s * P:(s + 1) * P], ident)
                mm.then_inc(ev["t2"], 1)
                if not is_tile(i, NT - 1):
                    product(i + 1, 0, KD - 2, KD)
                pe.wait_ge(ev["h2t"], now)
                pe.wait_ge(ev["lgs"], last)
                pe.wait_ge(ev["rkr"], last)
                for s in range(KD):
                    mm = nc.tensor.matmul(sm[:, 0:E], h2T[:, s], wr[:, s], start=(s == 0), stop=(s == KD - 1))
                mm.then_inc(ev["lg"], 1)
                if not is_tile(i, NT - 1):
                    product(i + 1, 1, 0, KD - 1)
                pe.wait_ge(ev["mask"], now)
                nc.tensor.matmul(sm[:, E:2 * E], const("before"), mask[:], start=True, stop=True)
                nc.tensor.matmul(sm[:, 2 * E:3 * E], const("ones"), mask[:], start=True, stop=True).then_inc(ev["rk"], 1)
                pe.wait_ge(ev["W"], now)
                pe.wait_ge(ev["wtc"], last)
                nc.tensor.transpose(wt[0:E, 0:P], W[:], ident).then_inc(ev["wt"], 1)
                if not is_tile(i, NT - 1):
                    product(i + 1, 1, KD - 1, KD)
                if not (isinstance(i, int) and i >= NT - 2):
                    transposed(i + 2, u, j + 1)
                pe.wait_ge(ev["wtc"], now)
                for c in range(2):
                    mm = nc.tensor.matmul(tq[:, 4 * c:4 * c + 4].rearrange("p s n -> p (s n)"), wT[:],
                                          bd[:, c * N:(c + 1) * N], start=True, stop=True)
                mm.then_inc(ev["bd"], 1)

            transposed(0, 0, 0)
            for c in range(2):
                pe.wait_ge(wlo_done, c + 1)
                product(0, c)
            pe.wait_ge(setup_dma, 7 * 16)
            transposed(1, 1, 0)
            for_tiles(pe, step)
            pe.wait_ge(table_ready, 1)
            nc.tensor.transpose(wt[0:E, 0:P], groups[:], ident)
            nc.tensor.transpose(wt[0:E, P:2 * P], tiles[:], ident).then_inc(table_t, 1)
            pe.wait_ge(table_ready, 2)
            nc.tensor.matmul(sm[:, 0:E], gT[:], const("causal")[0:E, 0:E], start=True, stop=True)
            nc.tensor.matmul(sm[:, E:2 * E], tT[:], const("before")[0:E, 0:E], start=True, stop=True).then_inc(table_t, 1)


def phase_experts(nc, k, A, keep):
    const = keep["const"]
    NCH, NGU, H = 6, 4, N // 2
    HK = KD // 2
    RAW = 4
    raw = k.sb("w_raw", [P, RAW, HK, N])
    whi, wlo = (k.sb(n, [P, 2, KD, N], F32R) for n in ("w_hi", "w_lo"))
    bias = k.sb("bias", [P, 2, D])
    g2 = k.sb("g2", [P, D])
    xs = k.sb("rows", [P, GT, D])
    xhi, xlo = (k.sb(n, [P, GT, KD, P], F32R) for n in ("x_hi", "x_lo"))
    ahi, alo = (k.sb(n, [P, GT, KD, P], F32R) for n in ("a_hi", "a_lo"))
    gu = k.sb("gate_up", [P, 2, N])
    act_row = k.sb("act_row", [P, GT, H])
    weighted = k.sb("weighted", [P, GT, N])
    rec_next, rec_now = k.sb("rec_next", [P, GT, 2], I32), k.sb("rec_now", [P, GT, 2], I32)
    table = k.sb("table", [1, 4 * (NG + 1)], I32)
    acc = k.ps("acc", [P, 5, N])
    tx = k.ps("tx", [P, 2, 4, P])
    ta = k.ps("ta", [P, 2, P])
    (table_in, g2_in, bias_in, hi_done, lo_done, mm_half, mm_done, read_done, sg_in, sg_done, act_done, ta_done, ahi_done,
     alo_done, tx_done, xhi_done, xlo_done, weighted_done, rec_next_in, rec_now_in, rec_used, rows_in, y_out, y_added,
     dve_step, wait_carrier, sg_set) = k.sems(
         "table_in g2_in bias_in hi_done lo_done mm_half mm_done read_done sg_in sg_done act_done ta_done ahi_done "
         "alo_done tx_done xhi_done xlo_done weighted_done rec_next_in rec_now_in rec_used rows_in y_out y_added "
         "dve_step wait_carrier sg_set")
    raw_in = [k.sem(f"raw_in{s}") for s in range(RAW)]
    gu_w = A["w_gu"].rearrange("o e (s p) n -> p (o e) s n", p=P)
    dn_w = A["w_down"].rearrange("o e (s p) n -> p (o e) s n", p=P)
    gu_b = A["b_gu"].rearrange("o e n -> (o e) n")
    places = keep["places"].rearrange("(p q) c -> p q c", p=P)

    def weighted_at(c, t):
        if c == NGU + 1 and t < 2:
            return act_row[:, 2 * t:2 * t + 2].rearrange("p a n -> p (a n)")
        return weighted[:, t]

    def bank(c, t):
        return c % 2 if t == 0 else t + 1

    def field(eng, g, f, most):
        return eng.value_load(table[0:1, bass.ds(g * 4 + f, 1)], min_val=0, max_val=most)

    EXPERT, TILES, BEFORE, PLACE = range(4)

    class Group:

        def __init__(self, eng, g, T):
            self.T = T
            self.before = field(eng, g, BEFORE, NG * GT)
            self.g = g

        def chunk_tile(self, c, t):
            return self.before * NCH + self.T * c + (t + 2)

        def chunks_before(self, c):
            return self.before * NCH + self.T * c + 1

        def gu_tile(self, c, t):
            return self.before * NGU + self.T * c + (t + 2)

        def down_tile(self, c, t):
            return self.before * 2 + self.T * (c - NGU) + (t + 2)

        def halves(self, n):
            return self.g * (2 * NCH) + (n + RAW)

    with nc.Block() as block:

        @block.sync
        def _(sp):
            sp.dma_start(table[:], keep["groups"][0:NG + 1, :].rearrange("g f -> (g f)").unsqueeze(0)).then_inc(table_in, 16)
            sp.dma_start(g2[:], keep["g2"]).then_inc(g2_in, 16)
            sp.sem_inc(lo_done, RAW)
            sp.sem_inc(read_done, 1)
            sp.sem_inc(mm_half, 1)
            sp.sem_inc(mm_done, 1)
            sp.wait_ge(table_in, 16)
            with sp.Fori(0, NG) as g:
                T = field(sp, g, TILES, GT)
                with sp.If(T > 0):
                    G = Group(sp, g, T)
                    expert = field(sp, g, EXPERT, E - 1)
                    for n in range(2 * NCH):
                        c, half = n // 2, n % 2
                        if n == RAW:
                            sp.wait_ge(act_done, G.before * NGU + 1)
                            sp.dma_start(bias[:].rearrange("p a n -> p (a n)"),
                                         gu_b[bass.ds(expert, 1), :].rearrange("o n -> (o n)").partition_broadcast(P)
                                         ).then_inc(bias_in, 16)
                        sp.wait_ge(lo_done, G.halves(n - RAW + 1))
                        rows = slice(half * HK, (half + 1) * HK)
                        for part in range(2):
                            w, col = (gu_w, part * D + c * H) if c < NGU else (dn_w, (c - NGU) * N + part * H)
                            sp.dma_start(raw[:, n % RAW, :, part * H:(part + 1) * H],
                                         w[:, bass.ds(expert, 1), rows, col:col + H]).then_inc(raw_in[n % RAW], 16)
                    sp.nop()

        @block.gpsimd
        def _(pool):
            pool.wait_ge(table_in, 16)
            for s in (ta_done, alo_done, weighted_done, y_added, act_done, rec_used):
                pool.sem_inc(s, 1)
            pool.sem_inc(tx_done, 1)

            def fetch_rows(g, T, place, before):
                pool.dma_start(rec_next[:], places[:, bass.ds(place, GT), :]).then_inc(rec_next_in, 16)
                pool.wait_ge(rec_next_in, (g + 1) * 16)
                pool.sem_inc(wait_carrier, 1)
                for t in range(GT):
                    with pool.If(T > t):
                        pool.indirect_dma_start(out=xs[:, t], out_offset=None, in_=keep["h2"],
                                                in_offset=bass.IndirectOffsetOnAxis(ap=rec_next[:, t, 0:1], axis=0)
                                                ).then_inc(rows_in, 16)
                pool.wait_ge(rows_in, (before + T) * 16)
                pool.sem_inc(wait_carrier, 1)

            T0 = field(pool, 0, TILES, GT)
            fetch_rows(0, T0, 0, 0)
            with pool.Fori(0, NG) as g:
                T = field(pool, g, TILES, GT)
                with pool.If(T > 0):
                    G = Group(pool, g, T)
                    place = field(pool, g, PLACE, PLACES - GT)
                    nT, nbefore, nplace = (field(pool, g + 1, f, most) for f, most in
                                           ((TILES, GT), (BEFORE, NG * GT), (PLACE, PLACES - GT)))
                    pool.wait_ge(rec_used, g + 1)
                    pool.sem_inc(wait_carrier, 1)
                    pool.dma_start(rec_now[:], places[:, bass.ds(place, GT), :]).then_inc(rec_now_in, 16)
                    pool.wait_ge(rec_now_in, (g + 1) * 16)
                    pool.sem_inc(wait_carrier, 1)
                    with pool.If(nT > 0):
                        pool.wait_ge(tx_done, G.before + G.T + 1)
                        pool.sem_inc(wait_carrier, 1)
                        fetch_rows(g + 1, nT, nplace, nbefore)
                    for c in (NGU, NGU + 1):
                        for t in range(GT):
                            with pool.If(G.T > t):
                                pool.wait_ge(weighted_done, G.down_tile(c, t))
                                pool.sem_inc(wait_carrier, 1)
                                pool.indirect_dma_start(
                                    out=keep["y"][c - NGU],
                                    out_offset=bass.IndirectOffsetOnAxis(ap=rec_now[:, t, 0:1], axis=0),
                                    in_=weighted_at(c, t), in_offset=None, compute_op=ALU.add).then_inc(y_out, 16)
                        pool.wait_ge(y_out, (G.before * 2 + G.T * (c - NGU + 1)) * 16)
                        pool.sem_inc(y_added, 1)

        @block.scalar
        def _(act):
            act.wait_ge(table_in, 16)

            def weights_hi(g, n, freed):
                act.wait_ge(raw_in[n % RAW], (g * (2 * NCH // RAW) + n // RAW + 1) * 32)
                c, half = n // 2, n % 2
                act.wait_ge(mm_done if half else mm_half, freed)
                nc.scalar.copy(whi[:, c % 2, half * HK:(half + 1) * HK], raw[:, n % RAW]).then_inc(hi_done, 1)

            def rows_hi(base, t):
                act.wait_ge(tx_done, base + (t + 2))
                for b in range(2):
                    nc.scalar.copy(xhi[:, t, 4 * b:4 * b + 4], tx[:, b]).then_inc(xhi_done, 1)

            nc.scalar.activation(act_row[:, 0, 0:1], const("eps"), ACT.Sigmoid).then_inc(sg_set, 1)
            act.wait_ge(sg_set, 1)
            for half in range(2):
                weights_hi(0, half, 1)
            T0 = field(act, 0, TILES, GT)
            for t in range(GT):
                with act.If(T0 > t):
                    rows_hi(0, t)
            with act.Fori(0, NG) as g:
                T = field(act, g, TILES, GT)
                with act.If(T > 0):
                    G = Group(act, g, T)
                    nT = field(act, g + 1, TILES, GT)

                    def activations_hi(c, t):
                        act.wait_ge(ta_done, G.gu_tile(c, t))
                        nc.scalar.copy(ahi[:, t, 2 * c:2 * c + 2], ta[:]).then_inc(ahi_done, 1)

                    def next_rows_hi(t):
                        with act.If(nT > t):
                            rows_hi(G.before + G.T, t)

                    for c in range(NGU):
                        for half in range(2):
                            weights_hi(g, 2 * (c + 1) + half, G.chunks_before(c))
                        for t in range(GT):
                            with act.If(G.T > t):
                                if c >= 1:
                                    activations_hi(c - 1, t)
                                if c == 0 and t == 0:
                                    act.wait_ge(y_added, g * 2 + 1)
                                act.wait_ge(sg_in, G.gu_tile(c, t) - 1)
                                nc.scalar.activation(act_row[:, t], gu[:, t % 2, 0:H], ACT.Sigmoid,
                                                     scale=SIG).then_inc(sg_done, 1)
                    weights_hi(g, 2 * NCH - 2, G.chunks_before(NGU))
                    activations_hi(NGU - 1, 0)
                    next_rows_hi(0)
                    weights_hi(g, 2 * NCH - 1, G.chunks_before(NGU))
                    for t in range(1, GT):
                        with act.If(G.T > t):
                            activations_hi(NGU - 1, t)
                    for half in range(2):
                        with act.If(nT > 0):
                            weights_hi(g + 1, half, G.chunks_before(NGU + 1))
                        next_rows_hi(1 + half)
                    next_rows_hi(3)
                    act.nop()

        @block.vector
        def _(dve):
            dve.wait_ge(table_in, 16)
            dve.wait_ge(g2_in, 16)

            def weights_lo(g, n):
                dve.wait_ge(hi_done, g * (2 * NCH) + n + 1)
                c, half = n // 2, n % 2
                rows = slice(half * HK, (half + 1) * HK)
                nc.vector.tensor_tensor(wlo[:, c % 2, rows], raw[:, n % RAW], whi[:, c % 2, rows],
                                        ALU.subtract).then_inc(lo_done, 1)

            def rows_lo(base, t):
                for b in range(2):
                    dve.wait_ge(xhi_done, base * 2 + (2 * t + b + 1))
                    nc.vector.tensor_tensor(xlo[:, t, 4 * b:4 * b + 4], tx[:, b], xhi[:, t, 4 * b:4 * b + 4],
                                            ALU.subtract).then_inc(xlo_done, 1)

            def clip(G, g, c, t):
                if t == 0 and c == 0:
                    dve.wait_ge(bias_in, (g + 1) * 16)
                u = t % 2
                dve.wait_ge(act_done, G.gu_tile(c, t) - 1)
                dve.wait_ge(mm_done, G.chunk_tile(c, t))
                nc.vector.tensor_tensor(gu[:, u].rearrange("p (a n) -> p a n", a=2),
                                        acc[:, bank(c, t)].rearrange("p (a n) -> p a n", a=2),
                                        bias[:, :, c * H:(c + 1) * H], ALU.add).then_inc(read_done, 1)
                dve.wait_ge(read_done, G.chunk_tile(c, t))
                nc.vector.tensor_scalar(gu[:, u, 0:H], gu[:, u, 0:H], LIMIT, None, ALU.min).then_inc(sg_in, 1)
                nc.vector.tensor_scalar(gu[:, u, H:N], gu[:, u, H:N], LIMIT, -LIMIT, ALU.min, ALU.max).then_inc(dve_step, 1)

            def swiglu(G, c, t):
                u = t % 2
                dve.wait_ge(sg_done, G.gu_tile(c, t) - 1)
                nc.vector.tensor_tensor(gu[:, u, 0:H], gu[:, u, 0:H], act_row[:, t], ALU.mult).then_inc(dve_step, 1)
                dve.wait_ge(dve_step, (G.gu_tile(c, t) - 1) * 2)
                nc.vector.scalar_tensor_tensor(out=act_row[:, t], in0=gu[:, u, H:N], scalar=1.0, in1=gu[:, u, 0:H],
                                               op0=ALU.add, op1=ALU.mult).then_inc(act_done, 1)

            for half in range(2):
                weights_lo(0, half)
            T0 = field(dve, 0, TILES, GT)
            for t in range(GT):
                with dve.If(T0 > t):
                    rows_lo(0, t)
            with dve.Fori(0, NG) as g:
                T = field(dve, g, TILES, GT)
                with dve.If(T > 0):
                    G = Group(dve, g, T)
                    nT = field(dve, g + 1, TILES, GT)

                    def activations_lo(c, t):
                        dve.wait_ge(ahi_done, G.gu_tile(c, t) - 1)
                        nc.vector.tensor_tensor(alo[:, t, 2 * c:2 * c + 2], ta[:], ahi[:, t, 2 * c:2 * c + 2],
                                                ALU.subtract).then_inc(alo_done, 1)

                    def weigh(c, t):
                        dve.wait_ge(mm_done, G.chunk_tile(c, t))
                        if c == NGU or t >= 2:
                            dve.wait_ge(y_added, G.g * 2 + (c - NGU + 1))
                        cols = slice((c - NGU) * N, (c - NGU + 1) * N)
                        nc.vector.scalar_tensor_tensor(
                            out=weighted_at(c, t), in0=acc[:, bank(c, t)], scalar=rec_now[:].bitcast(F32)[:, t, 1:2],
                            in1=g2[:, cols], op0=ALU.mult, op1=ALU.mult).then_inc(weighted_done, 1)
                        dve.wait_ge(weighted_done, G.down_tile(c, t))
                        dve.sem_inc(read_done, 1)

                    def next_rows_lo(t):
                        with dve.If(nT > t):
                            rows_lo(G.before + G.T, t)

                    for c in range(NGU):
                        weights_lo(g, 2 * (c + 1))
                        for t in range(GT):
                            with dve.If(G.T > t):
                                if c >= 1:
                                    activations_lo(c - 1, t)
                                clip(G, g, c, t)
                                if t == 0:
                                    weights_lo(g, 2 * (c + 1) + 1)
                                swiglu(G, c, t)
                    weights_lo(g, 2 * NCH - 2)
                    activations_lo(NGU - 1, 0)
                    next_rows_lo(0)
                    weights_lo(g, 2 * NCH - 1)
                    dve.wait_ge(rec_now_in, (g + 1) * 16)
                    dve.sem_inc(wait_carrier, 1)
                    weigh(NGU, 0)
                    for t in range(1, GT):
                        with dve.If(G.T > t):
                            activations_lo(NGU - 1, t)
                            weigh(NGU, t)
                    for half in range(2):
                        next_rows_lo(1 + half)
                        with dve.If(nT > 0):
                            weights_lo(g + 1, half)
                    for t in range(GT):
                        with dve.If(G.T > t):
                            weigh(NGU + 1, t)
                    next_rows_lo(3)
                    dve.sem_inc(rec_used, 1)

        @block.tensor
        def _(pe):
            ident = const("ident")
            pe.wait_ge(table_in, 16)

            def rows(t):
                for s in range(KD):
                    mm = nc.tensor.transpose(tx[:, s // 4, s % 4], xs[:, t, s * P:(s + 1) * P], ident)
                mm.then_inc(tx_done, 1)

            def activations(G, c, t):
                pe.wait_ge(act_done, G.gu_tile(c, t))
                pe.wait_ge(alo_done, G.gu_tile(c, t) - 1)
                for s in range(2):
                    mm = nc.tensor.transpose(ta[:, s], act_row[:, t, s * P:(s + 1) * P], ident)
                mm.then_inc(ta_done, 1)

            T0 = field(pe, 0, TILES, GT)
            pe.sem_inc(xlo_done, 2)
            for t in range(GT):
                with pe.If(T0 > t):
                    if t == 0:
                        pe.wait_ge(rows_in, T0 * 16)
                    pe.wait_ge(xlo_done, 2 * t + 2)
                    rows(t)
            with pe.Fori(0, NG) as g:
                T = field(pe, g, TILES, GT)
                with pe.If(T > 0):
                    G = Group(pe, g, T)
                    nT = field(pe, g + 1, TILES, GT)

                    def next_rows(t):
                        with pe.If(nT > t):
                            if t == 0:
                                pe.wait_ge(rows_in, (G.before + G.T + nT) * 16)
                            pe.wait_ge(xlo_done, (G.before + G.T) * 2 + (2 * t + 2))
                            rows(t)

                    for c in range(NCH):
                        pe.wait_ge(lo_done, G.halves(2 * c + 1))
                        for t in range(GT):
                            with pe.If(G.T > t):
                                if c == 0:
                                    pe.wait_ge(xlo_done, G.before * 2 + (2 * t + 4))
                                if t > 0:
                                    pe.wait_ge(read_done, G.chunk_tile(c - 1, t) if c else G.chunks_before(0))
                                elif c >= 2:
                                    pe.wait_ge(read_done, G.chunk_tile(c - 2, 0))
                                a_hi, a_lo = (xhi, xlo) if c < NGU else (ahi, alo)
                                for s in range(KD):
                                    if s == HK:
                                        mm.then_inc(mm_half, 1)
                                        if t == 0:
                                            pe.wait_ge(lo_done, G.halves(2 * c + 2))
                                    if c == NGU and t > 0 and s == 0:
                                        activations(G, NGU - 1, t)
                                    if c == NGU and t == 0 and s == 2:
                                        with pe.If(G.T > 1):
                                            activations(G, NGU - 1, t)
                                    if c == NGU and t == 0 and s == 2 * (NGU - 2):
                                        pe.wait_ge(alo_done, G.gu_tile(NGU - 1, 0) - 1)
                                    if c == NGU and s == 2 * (NGU - 1):
                                        if t == 0:
                                            with pe.If(G.T < 2):
                                                activations(G, NGU - 1, t)
                                            next_rows(0)
                                        pe.wait_ge(alo_done, G.gu_tile(NGU - 1, t))
                                    if c == NGU + 1 and t == 0 and s in (1, 6):
                                        next_rows(s // 4 + 1)
                                    mm = split_product(nc, acc[:, bank(c, t)], a_hi[:, t, s], a_lo[:, t, s],
                                                       whi[:, c % 2, s], wlo[:, c % 2, s], s == 0, s == KD - 1)
                                mm.then_inc(mm_done, 1)
                                if 1 <= c < NGU:
                                    activations(G, c - 1, t)
                    next_rows(3)
                    pe.wait_ge(read_done, G.chunk_tile(NGU, 0))
                    pe.nop()


def phase_finish(nc, k, A, keep):
    const = keep["const"]
    SLOTS = 4
    y, z = k.sb("y", [P, SLOTS, D]), k.sb("z", [P, SLOTS, D])
    squares = k.sb("squares", [P, D], mybir.dt.bfloat16)
    nf = k.sb("norm_f", [P, D])
    ssq, rms, rinv = (k.sb(n, [P, NT]) for n in ("ssq", "rms", "rinv"))
    nf_in, sq_done, rms_done, inv_done, done = k.sems("nf_in sq_done rms_done inv_done done")
    y_in = [k.sem(f"y_in{s}") for s in range(SLOTS)]
    out_done = [k.sem(f"out_done{s}") for s in range(SLOTS)]
    y_t = [a.rearrange("(t p) n -> p t n", p=P) for a in keep["y"]]
    out_t = keep["out"].rearrange("o (t p) d -> p (o t) d", p=P)
    with nc.Block() as block:

        @block.sync
        def _(sp):
            sp.dma_start(nf[:], A["norm_f"].partition_broadcast(P)).then_inc(nf_in, 16)
            for i in range(NT):
                if i >= SLOTS:
                    sp.wait_ge(done, i - SLOTS + 1)
                for half in range(2):
                    sp.dma_start(y[:, i % SLOTS, half * N:(half + 1) * N], y_t[half][:, i]).then_inc(y_in[i % SLOTS], 16)

        @block.scalar
        def _(act):
            for i in range(NT):
                act.wait_ge(y_in[i % SLOTS], 32 * (i // SLOTS + 1))
                nc.scalar.activation(squares[:], y[:, i % SLOTS], ACT.Square, accum_out=ssq[:, i:i + 1]).then_inc(sq_done, 1)
                act.wait_ge(sq_done, i + 1)
                nc.scalar.activation(rms[:, i:i + 1], ssq[:, i:i + 1], ACT.Sqrt, scale=1.0 / D,
                                     bias=const("eps")).then_inc(rms_done, 1)

        @block.vector
        def _(dve):
            dve.wait_ge(nf_in, 16)
            for i in range(NT):
                s = i % SLOTS
                dve.wait_ge(rms_done, i + 1)
                nc.vector.reciprocal(rinv[:, i:i + 1], rms[:, i:i + 1]).then_inc(inv_done, 1)
                dve.wait_ge(inv_done, i + 1)
                if i >= SLOTS:
                    dve.wait_ge(out_done[s], 16 * (i // SLOTS))
                nc.vector.scalar_tensor_tensor(out=z[:, s], in0=y[:, s], scalar=rinv[:, i:i + 1], in1=nf[:],
                                               op0=ALU.mult, op1=ALU.mult).then_inc(done, 1)

        @block.gpsimd
        def _(pool):
            for i in range(NT):
                pool.wait_ge(done, i + 1)
                pool.dma_start(out_t[:, i], z[:, i % SLOTS]).then_inc(out_done[i % SLOTS], 16)
            for s in range(SLOTS):
                pool.wait_ge(out_done[s], 16 * (NT // SLOTS))


def program(nc, A, out):
    def dram(name, shape, dt=F32):
        return nc.dram_tensor(name, shape, dt, kind="Internal").ap()

    with ExitStack() as ctx:
        k = Kit(nc, ctx, "keep")
        keep = {n: dram(n + "_rep", (P, D)) for n in ("g1", "sh2", "A2", "g2")}
        keep["proj"] = dram("proj", (S, PROJ))
        keep["o"] = dram("mixed", (S + P, D))
        keep["h2"] = dram("h2_rows", (ROWS, D))
        keep["y"] = [dram(f"y_rows{half}", (ROWS, N)) for half in range(2)]
        keep["places"] = dram("places", (P * PLACES, 2), I32)
        keep["groups"] = dram("groups", (P, 4), I32)
        keep["const_all"] = k.sb("const", [P, CONST_SHARED])
        keep["const"] = lambda name: keep["const_all"][:, CONST_AT[name][0]:sum(CONST_AT[name])]
        keep["out"] = out

        def run(phase):
            with ExitStack() as c:
                k = Kit(nc, c, phase.__name__[6:9])
                phase(nc, k, A, keep)
                k.clear_sems()

        with ExitStack() as mixing:
            keep["glr_t"] = Kit(nc, mixing, "mixing").sb("glr_t", [RANK + 1, S])
            with ExitStack() as early:
                ke = Kit(nc, early, "early")
                keep["A1"], keep["sh1"] = ke.sb("A1", [P, D]), ke.sb("sh1", [P, D])
                keep["x"], keep["w_raw"] = ke.sb("x", [P, 2, D]), ke.sb("w_raw", [P, 2, KD, N])
                keep["x_in"] = [ke.sem(f"x_in{s}") for s in range(2)]
                keep["raw_in"] = [ke.sem(f"raw_in{s}") for s in range(2)]
                run(phase_modulation)
                run(phase_projection)
                ke.clear_sems()
            kw = Kit(nc, mixing, "w_out")
            keep["w_out"], keep["w_out_in"] = kw.sb("raw", [P, 2, KD, N]), kw.sem("in")
            run(phase_mixer)
            run(phase_routing)
            kw.clear_sems()
        run(phase_experts)
        run(phase_finish)


_INS = ['x', 'c', 'positions', 'w_ada', 'b_ada', 'norm1', 'w_in', 'w_gk2', 'b_gk', 'gla_onorm', 'ret_onorm', 'w_out',
        'norm2', 'w_router', 'b_router', 'w_gu', 'b_gu', 'w_down', 'b_down', 'norm_f']


def kernel(**inputs):
    import concourse.bacc as bacc
    from concourse.bass_utils import run_bass_kernel_spmd

    nc = bacc.Bacc("TRN2", target_bir_lowering=False, num_devices=1)
    arrays = {n: np.ascontiguousarray(inputs[n]) for n in _INS}
    arrays["const"] = constants()[0]
    A = {n: nc.dram_tensor("in_" + n, a.shape, mybir.dt.from_np(a.dtype), kind="ExternalInput").ap()
         for n, a in arrays.items()}
    out = nc.dram_tensor("out", (1, S, D), F32, kind="ExternalOutput").ap()
    program(nc, A, out)
    r = run_bass_kernel_spmd(nc, [{"in_" + n: a for n, a in arrays.items()}], core_ids=[0])
    return r.results[0]["out"]
```
